# Optimizing a Trainium2 kernel written in Bass

```python
import math
import jax, jax.numpy as jnp
from jax import lax
import numpy as np

D_MODEL = 1024
BATCH = 1
SEQ = 512
DEPTH = 1

HEAD_DIM = 128
N_HEADS = D_MODEL // HEAD_DIM
GDN_HEADS = N_HEADS // 2
NSA_HEADS = N_HEADS - GDN_HEADS
GDN_WIDTH = GDN_HEADS * HEAD_DIM
NSA_WIDTH = NSA_HEADS * HEAD_DIM
GDN_CONV = 4
GDN_CHUNK = 64
CMP_BLOCK = 32
CMP_STRIDE = 16
SEL_BLOCK = 64
N_SELECT = 16
WINDOW = 512
Q_BLOCK = 128
D_FF = 2816
FFN_CONV = 3
N_GATES = 3
IN_SPLITS = (GDN_WIDTH, GDN_WIDTH, GDN_WIDTH, GDN_WIDTH, GDN_HEADS, GDN_HEADS,
             NSA_WIDTH, HEAD_DIM, HEAD_DIM, HEAD_DIM, HEAD_DIM, HEAD_DIM, HEAD_DIM,
             N_GATES * NSA_HEADS)
N_IN = 4 * GDN_WIDTH + 2 * GDN_HEADS + NSA_WIDTH + 6 * HEAD_DIM + N_GATES * NSA_HEADS
EPS = 1e-6
NEG_INF = -1e30
FORCE_BONUS = 1e4


def rmsnorm(x, w):
    xf = x.astype(jnp.float32)
    y = xf * lax.rsqrt(jnp.mean(xf * xf, axis=-1, keepdims=True) + EPS)
    return (y * w.astype(jnp.float32)).astype(x.dtype)

def l2norm(x):
    xf = x.astype(jnp.float32)
    return xf * lax.rsqrt(jnp.sum(xf * xf, axis=-1, keepdims=True) + EPS)

def causal_dwconv(x, w, b=None):
    k = w.shape[0]
    y = lax.conv_general_dilated(x, w[:, None, :].astype(x.dtype), window_strides=(1,),
                                 padding=[(k - 1, 0)], dimension_numbers=('NWC', 'WIO', 'NWC'),
                                 feature_group_count=x.shape[-1])
    if b is not None:
        y = y + b
    return y

def masked_softmax(s, mask):
    p = jax.nn.softmax(jnp.where(mask, s, NEG_INF), axis=-1)
    return jnp.where(mask, p, 0.0)

def gated_delta_chunked(q, k, v, g, beta):
    B, S, H, dk = q.shape
    dv = v.shape[-1]
    n = S // GDN_CHUNK
    f32 = jnp.float32

    def to_chunks(t):
        t = t.astype(f32).reshape((B, n, GDN_CHUNK) + t.shape[2:])
        return jnp.moveaxis(t, 3, 1)

    q, k, v, g, beta = (to_chunks(t) for t in (q, k, v, g, beta))
    q = q * (dk ** -0.5)
    gc = jnp.cumsum(g, axis=-1)
    idx = jnp.arange(GDN_CHUNK)
    incl = idx[:, None] >= idx[None, :]
    strict = idx[:, None] > idx[None, :]
    decay = jnp.exp(jnp.where(incl, gc[..., :, None] - gc[..., None, :], NEG_INF))
    k_beta = k * beta[..., None]
    a_mat = jnp.where(strict, jnp.einsum('bhncd,bhnsd->bhncs', k_beta, k) * decay, 0.0)
    eye = jnp.eye(GDN_CHUNK, dtype=f32)
    t_mat = lax.linalg.triangular_solve(eye + a_mat, jnp.broadcast_to(eye, a_mat.shape),
                                        left_side=True, lower=True, unit_diagonal=True)
    u = t_mat @ (v * beta[..., None])
    w = t_mat @ (k_beta * jnp.exp(gc)[..., None])
    attn_intra = jnp.where(incl, jnp.einsum('bhncd,bhnsd->bhncs', q, k) * decay, 0.0)
    q_dec = q * jnp.exp(gc)[..., None]
    k_dec = k * jnp.exp(gc[..., -1:] - gc)[..., None]
    g_last = jnp.exp(gc[..., -1])

    def step(state, inp):
        u_i, w_i, qd_i, kd_i, a_i, gl_i = inp
        v_new = u_i - w_i @ state
        o_i = qd_i @ state + a_i @ v_new
        state = state * gl_i[..., None, None] + jnp.swapaxes(kd_i, -1, -2) @ v_new
        return state, o_i

    xs = tuple(jnp.moveaxis(t, 2, 0) for t in (u, w, q_dec, k_dec, attn_intra, g_last))
    state0 = jnp.zeros((B, H, dk, dv), f32)
    _, o = lax.scan(step, state0, xs)
    return jnp.transpose(o, (1, 0, 3, 2, 4)).reshape(B, S, H, dv)

def nsa_compress(kv, pos, w1, w2):
    B, S, D = kv.shape
    n_cmp = (S - CMP_BLOCK) // CMP_STRIDE + 1
    idx = jnp.arange(n_cmp)[:, None] * CMP_STRIDE + jnp.arange(CMP_BLOCK)[None, :]
    blocks = kv[:, idx] + pos
    hid = jax.nn.silu(blocks.reshape(B, n_cmp, CMP_BLOCK * D) @ w1)
    return hid @ w2

def nsa_attention(q, k_cmp, v_cmp, k_slc, v_slc, k_win, v_win, gates):
    f32 = jnp.float32
    q, k_cmp, v_cmp, k_slc, v_slc, k_win, v_win, gates = (
        t.astype(f32) for t in (q, k_cmp, v_cmp, k_slc, v_slc, k_win, v_win, gates))
    B, S, H, D = q.shape
    scale = D ** -0.5
    n_cmp = k_cmp.shape[1]
    n_sel = S // SEL_BLOCK
    n_pick = min(N_SELECT, n_sel)
    cs = jnp.arange(n_cmp) * CMP_STRIDE
    ss = jnp.arange(n_sel) * SEL_BLOCK
    ov = jnp.minimum(cs[:, None] + CMP_BLOCK, ss[None, :] + SEL_BLOCK) - jnp.maximum(cs[:, None], ss[None, :])
    overlap = jnp.clip(ov, 0, None).astype(f32) / CMP_BLOCK
    cmp_end = cs + CMP_BLOCK - 1
    k_blocks = k_slc.reshape(B, n_sel, SEL_BLOCK, D)
    v_blocks = v_slc.reshape(B, n_sel, SEL_BLOCK, D)
    k_win_pad = jnp.pad(k_win, ((0, 0), (WINDOW, 0), (0, 0)))
    v_win_pad = jnp.pad(v_win, ((0, 0), (WINDOW, 0), (0, 0)))
    blk = jnp.arange(n_sel)
    gather = jax.vmap(lambda kb, ib: kb[ib])

    def block(qi):
        t0 = qi * Q_BLOCK
        qb = lax.dynamic_slice_in_dim(q, t0, Q_BLOCK, axis=1)
        gb = lax.dynamic_slice_in_dim(gates, t0, Q_BLOCK, axis=1)
        t = t0 + jnp.arange(Q_BLOCK)
        mask_c = cmp_end[None, :] <= t[:, None]
        s_c = jnp.einsum('bqhd,bkd->bqhk', qb, k_cmp) * scale
        p_c = masked_softmax(s_c, mask_c[None, :, None, :])
        o_c = jnp.einsum('bqhk,bkd->bqhd', p_c, v_cmp)
        imp = jnp.einsum('bqhk,kj->bqj', p_c, overlap)
        cur = t // SEL_BLOCK
        valid = blk[None, :] <= cur[:, None]
        forced = (blk[None, :] == 0) | (blk[None, :] == cur[:, None]) | (blk[None, :] == cur[:, None] - 1)
        imp = jnp.where(valid[None], imp + jnp.where(forced, FORCE_BONUS, 0.0)[None], NEG_INF)
        _, sel = lax.top_k(imp, n_pick)
        ks = gather(k_blocks, sel).reshape(B, Q_BLOCK, n_pick * SEL_BLOCK, D)
        vs = gather(v_blocks, sel).reshape(B, Q_BLOCK, n_pick * SEL_BLOCK, D)
        pos_s = (sel[..., None] * SEL_BLOCK + jnp.arange(SEL_BLOCK)).reshape(B, Q_BLOCK, n_pick * SEL_BLOCK)
        mask_s = pos_s <= t[None, :, None]
        s_s = jnp.einsum('bqhd,bqkd->bqhk', qb, ks) * scale
        p_s = masked_softmax(s_s, mask_s[:, :, None, :])
        o_s = jnp.einsum('bqhk,bqkd->bqhd', p_s, vs)
        kw = lax.dynamic_slice_in_dim(k_win_pad, t0, Q_BLOCK + WINDOW, axis=1)
        vw = lax.dynamic_slice_in_dim(v_win_pad, t0, Q_BLOCK + WINDOW, axis=1)
        pos_w = t0 - WINDOW + jnp.arange(Q_BLOCK + WINDOW)
        mask_w = (pos_w[None, :] <= t[:, None]) & (pos_w[None, :] > t[:, None] - WINDOW) & (pos_w[None, :] >= 0)
        s_w = jnp.einsum('bqhd,bkd->bqhk', qb, kw) * scale
        p_w = masked_softmax(s_w, mask_w[None, :, None, :])
        o_w = jnp.einsum('bqhk,bkd->bqhd', p_w, vw)
        return gb[..., 0:1] * o_c + gb[..., 1:2] * o_s + gb[..., 2:3] * o_w

    out = lax.map(block, jnp.arange(S // Q_BLOCK))
    return jnp.moveaxis(out, 0, 1).reshape(B, S, H, D)

def hybrid_layer(x, c, ada_w, ada_b, norm1_w, w_in, gdn_conv_w, gdn_A_log, gdn_dt_bias,
                 gdn_out_norm_w, nsa_q_norm_w, nsa_k_norm_cmp, nsa_k_norm_slc, nsa_k_norm_win,
                 cmp_k_pos, cmp_k_w1, cmp_k_w2, cmp_v_pos, cmp_v_w1, cmp_v_w2, w_out,
                 norm2_w, ffn_w_up, ffn_conv_w, ffn_conv_b, ffn_w_down):
    f32 = jnp.float32
    B, S, _ = x.shape
    mod = jax.nn.silu(c) @ ada_w + ada_b
    shift1, scale1, gate1, shift2, scale2, gate2 = jnp.split(mod[:, None, :], 6, axis=-1)

    h = rmsnorm(x, norm1_w) * (1 + scale1) + shift1
    proj = h @ w_in
    offsets = np.cumsum(IN_SPLITS)[:-1].tolist()
    (gq, gk, gv, gz, ga, gbeta, nq, kc, vc, ksl, vsl, kwn, vwn, ng) = jnp.split(proj, offsets, axis=-1)

    qkv = jax.nn.silu(causal_dwconv(jnp.concatenate([gq, gk, gv], axis=-1), gdn_conv_w))
    gq, gk, gv = jnp.split(qkv, 3, axis=-1)
    hd = (B, S, GDN_HEADS, HEAD_DIM)
    q_g = l2norm(gq.reshape(hd))
    k_g = l2norm(gk.reshape(hd))
    v_g = gv.reshape(hd)
    beta = jax.nn.sigmoid(gbeta.astype(f32))
    log_decay = -jnp.exp(gdn_A_log.astype(f32)) * jax.nn.softplus(ga.astype(f32) + gdn_dt_bias.astype(f32))
    o_g = gated_delta_chunked(q_g, k_g, v_g, log_decay, beta)
    o_g = rmsnorm(o_g, gdn_out_norm_w) * jax.nn.silu(gz.reshape(hd).astype(f32))

    q_n = rmsnorm(nq.reshape(B, S, NSA_HEADS, HEAD_DIM), nsa_q_norm_w)
    k_cmp = rmsnorm(nsa_compress(kc, cmp_k_pos, cmp_k_w1, cmp_k_w2), nsa_k_norm_cmp)
    v_cmp = nsa_compress(vc, cmp_v_pos, cmp_v_w1, cmp_v_w2)
    k_slc = rmsnorm(ksl, nsa_k_norm_slc)
    k_win = rmsnorm(kwn, nsa_k_norm_win)
    gates = jax.nn.sigmoid(ng.reshape(B, S, NSA_HEADS, N_GATES))
    o_n = nsa_attention(q_n, k_cmp, v_cmp, k_slc, vsl, k_win, vwn, gates)

    mixed = jnp.concatenate([o_g.reshape(B, S, GDN_WIDTH), o_n.reshape(B, S, NSA_WIDTH)], axis=-1)
    x = x + gate1 * (mixed.astype(x.dtype) @ w_out)

    h2 = rmsnorm(x, norm2_w) * (1 + scale2) + shift2
    up = causal_dwconv(h2 @ ffn_w_up, ffn_conv_w, ffn_conv_b)
    a, b = jnp.split(up, 2, axis=-1)
    x = x + gate2 * ((jax.nn.silu(a) * b) @ ffn_w_down)
    return x

def first_inputs(seed: int = 0) -> dict:
    key = jax.random.key(seed)
    ks = jax.random.split(key, 32)
    f32 = jnp.float32
    L = DEPTH

    def nrm(k, shape, s):
        return jax.random.normal(k, shape, f32) * s

    def gain(k, n):
        return 1.0 + 0.02 * jax.random.normal(k, (L, n), f32)

    dt = jnp.exp(jax.random.uniform(ks[8], (L, GDN_HEADS), f32, math.log(1e-3), math.log(1e-1)))
    return {
        'x': nrm(ks[0], (BATCH, SEQ, D_MODEL), 1.0),
        'c': nrm(ks[1], (BATCH, D_MODEL), 1.0),
        'ada_w': nrm(ks[2], (L, D_MODEL, 6 * D_MODEL), 0.5 * D_MODEL ** -0.5),
        'ada_b': nrm(ks[3], (L, 6 * D_MODEL), 0.02),
        'norm1_w': gain(ks[4], D_MODEL),
        'w_in': nrm(ks[5], (L, D_MODEL, N_IN), D_MODEL ** -0.5),
        'gdn_conv_w': nrm(ks[6], (L, GDN_CONV, 3 * GDN_WIDTH), GDN_CONV ** -0.5),
        'gdn_A_log': jnp.log(jax.random.uniform(ks[7], (L, GDN_HEADS), f32, 1.0, 16.0)),
        'gdn_dt_bias': dt + jnp.log(-jnp.expm1(-dt)),
        'gdn_out_norm_w': gain(ks[9], HEAD_DIM),
        'nsa_q_norm_w': gain(ks[10], HEAD_DIM),
        'nsa_k_norm_cmp': gain(ks[11], HEAD_DIM),
        'nsa_k_norm_slc': gain(ks[12], HEAD_DIM),
        'nsa_k_norm_win': gain(ks[13], HEAD_DIM),
        'cmp_k_pos': nrm(ks[14], (L, CMP_BLOCK, HEAD_DIM), 0.02),
        'cmp_k_w1': nrm(ks[15], (L, CMP_BLOCK * HEAD_DIM, HEAD_DIM), (CMP_BLOCK * HEAD_DIM) ** -0.5),
        'cmp_k_w2': nrm(ks[16], (L, HEAD_DIM, HEAD_DIM), HEAD_DIM ** -0.5),
        'cmp_v_pos': nrm(ks[17], (L, CMP_BLOCK, HEAD_DIM), 0.02),
        'cmp_v_w1': nrm(ks[18], (L, CMP_BLOCK * HEAD_DIM, HEAD_DIM), (CMP_BLOCK * HEAD_DIM) ** -0.5),
        'cmp_v_w2': nrm(ks[19], (L, HEAD_DIM, HEAD_DIM), HEAD_DIM ** -0.5),
        'w_out': nrm(ks[20], (L, D_MODEL, D_MODEL), D_MODEL ** -0.5),
        'norm2_w': gain(ks[21], D_MODEL),
        'ffn_w_up': nrm(ks[22], (L, D_MODEL, 2 * D_FF), D_MODEL ** -0.5),
        'ffn_conv_w': nrm(ks[23], (L, FFN_CONV, 2 * D_FF), FFN_CONV ** -0.5),
        'ffn_conv_b': nrm(ks[24], (L, 2 * D_FF), 0.02),
        'ffn_w_down': nrm(ks[25], (L, D_FF, D_MODEL), D_FF ** -0.5),
    }

def first_block(x, c, ada_w, ada_b, norm1_w, w_in, gdn_conv_w, gdn_A_log, gdn_dt_bias,
              gdn_out_norm_w, nsa_q_norm_w, nsa_k_norm_cmp, nsa_k_norm_slc, nsa_k_norm_win,
              cmp_k_pos, cmp_k_w1, cmp_k_w2, cmp_v_pos, cmp_v_w1, cmp_v_w2, w_out,
              norm2_w, ffn_w_up, ffn_conv_w, ffn_conv_b, ffn_w_down):
    for l in range(DEPTH):
        x = hybrid_layer(x, c, ada_w[l], ada_b[l], norm1_w[l], w_in[l], gdn_conv_w[l], gdn_A_log[l],
                         gdn_dt_bias[l], gdn_out_norm_w[l], nsa_q_norm_w[l], nsa_k_norm_cmp[l],
                         nsa_k_norm_slc[l], nsa_k_norm_win[l], cmp_k_pos[l], cmp_k_w1[l], cmp_k_w2[l],
                         cmp_v_pos[l], cmp_v_w1[l], cmp_v_w2[l], w_out[l], norm2_w[l], ffn_w_up[l],
                         ffn_conv_w[l], ffn_conv_b[l], ffn_w_down[l])
    return x


CHUNK = 64
N_META = 16
META_PAD = (CHUNK - N_META % CHUNK) % CHUNK
RMS_EPS = 1e-6
GLA_HEADS = 4
GLA_DK = D_MODEL // 8
GLA_DV = D_MODEL // 4
GLA_GATE_RANK = 16
GLA_GATE_NORM = 16.0
GLA_QK = GLA_HEADS * GLA_DK
GLA_VW = GLA_HEADS * GLA_DV
SSD_D_INNER = 2 * D_MODEL
SSD_HEADDIM = 64
SSD_HEADS = SSD_D_INNER // SSD_HEADDIM
SSD_GROUPS = 4
SSD_HPG = SSD_HEADS // SSD_GROUPS
SSD_STATE = 128
SSD_CONV = 4
SSD_BC = SSD_GROUPS * SSD_STATE
SSD_XBC = SSD_D_INNER + 2 * SSD_BC
PEER_HEADS = 8
PEER_N_KEYS = 128
PEER_N_EXPERTS = PEER_N_KEYS * PEER_N_KEYS
PEER_KEY_DIM = 256
PEER_HALF = PEER_KEY_DIM // 2
PEER_TOPK = 16
PEER_BLOCK = 256
IN_SPLITS_2 = (GLA_QK, GLA_QK, GLA_VW, GLA_VW, GLA_GATE_RANK, SSD_D_INNER, SSD_XBC, SSD_HEADS, D_MODEL, D_MODEL)
IN_WIDTH = GLA_QK * 2 + GLA_VW * 2 + GLA_GATE_RANK + SSD_D_INNER + SSD_XBC + SSD_HEADS + 2 * D_MODEL


def rmsnorm_2(x, w):
    xf = x.astype(jnp.float32)
    y = xf * lax.rsqrt(jnp.mean(xf * xf, axis=-1, keepdims=True) + RMS_EPS)
    return (y * w.astype(jnp.float32)).astype(x.dtype)

def split_cols(t, sizes):
    out, start = [], 0
    for s in sizes:
        out.append(t[..., start:start + s])
        start += s
    return out

def pad_front(t):
    return jnp.pad(t, [(0, 0), (META_PAD, 0)] + [(0, 0)] * (t.ndim - 2))

def to_chunks(t):
    b, lp = t.shape[:2]
    return jnp.moveaxis(t.reshape(b, lp // CHUNK, CHUNK, *t.shape[2:]), 1, 0)

def from_chunks(t):
    t = jnp.moveaxis(t, 0, 1)
    return t.reshape(t.shape[0], -1, *t.shape[3:])

def causal_dwconv_2(u, w, b):
    L = u.shape[1]
    up = jnp.pad(u, ((0, 0), (SSD_CONV - 1, 0), (0, 0)))
    return sum(up[:, i:i + L] * w[i] for i in range(SSD_CONV)) + b

def gla_chunk_step(S, inp):
    q, k, v, lg = inp
    G = jnp.cumsum(lg, axis=1)
    eG, eGn = jnp.exp(G), jnp.exp(-G)
    a_causal = jnp.einsum('bthk,bshk->bhts', q * eG, k * eGn)
    a_ahead = jnp.einsum('bthk,bshk->bhts', q * eGn, k * eG)
    tri = jnp.tril(jnp.ones((CHUNK, CHUNK), dtype=bool))
    att = jnp.where(tri, a_causal, a_ahead)
    o = jnp.einsum('bhts,bshv->bthv', att, v) + jnp.einsum('bthk,bhkv->bthv', q * eG, S)
    G_last = G[:, -1]
    S = S * jnp.exp(G_last)[..., None] + jnp.einsum('bshk,bshv->bhkv', k * jnp.exp(G_last[:, None] - G), v)
    return S, o

def gla_chunked(q, k, v, lg):
    S0 = jnp.zeros((q.shape[0], GLA_HEADS, GLA_DK, GLA_DV), jnp.float32)
    _, o = lax.scan(gla_chunk_step, S0, (to_chunks(q), to_chunks(k), to_chunks(v), to_chunks(lg)))
    return from_chunks(o)

def ssd_chunk_step(S, inp):
    xdt, a, Bc, Cc = inp
    acum = jnp.cumsum(a, axis=1)
    seg = jnp.exp(-jnp.abs(acum[:, :, None] - acum[:, None, :]))
    cb = jnp.einsum('btgn,bsgn->btsg', Cc, Bc)
    y = jnp.einsum('btsgr,btsg,bsgrp->btgrp', seg, cb, xdt)
    y = y + jnp.einsum('btgn,bgrpn,btgr->btgrp', Cc, S, jnp.exp(acum))
    to_end = jnp.exp(acum[:, -1:] - acum)
    S = S * jnp.exp(acum[:, -1])[..., None, None] + jnp.einsum('bsgn,bsgr,bsgrp->bgrpn', Bc, to_end, xdt)
    return S, y

def ssd_chunked(xdt, a, Bm, Cm):
    S0 = jnp.zeros((xdt.shape[0], SSD_GROUPS, SSD_HPG, SSD_HEADDIM, SSD_STATE), jnp.float32)
    _, y = lax.scan(ssd_chunk_step, S0, (to_chunks(xdt), to_chunks(a), to_chunks(Bm), to_chunks(Cm)))
    return from_chunks(y)

def hybrid_mixer(hn, w_in, gla_w_gate2, gla_b_gate, gla_norm_w, conv_w, conv_b, dt_bias, a_log, d_skip,
                 ssd_norm_w, w_up_gla, w_up_ssd, w_out):
    Bsz, L, _ = hn.shape
    f32 = jnp.float32
    proj = hn @ w_in
    q, k, v, g_out, g_low, z, xbc, dt_raw, gate_a, gate_b = split_cols(proj, IN_SPLITS_2)

    log_g = jax.nn.log_sigmoid((g_low @ gla_w_gate2 + gla_b_gate).astype(f32)) / GLA_GATE_NORM
    hd = lambda t, n: t.reshape(Bsz, L, GLA_HEADS, n)
    o = gla_chunked(pad_front(hd(q, GLA_DK) * GLA_DK ** -0.5), pad_front(hd(k, GLA_DK)),
                    pad_front(hd(v, GLA_DV)), pad_front(hd(log_g, GLA_DK)))[:, META_PAD:]
    o = rmsnorm_2(o, gla_norm_w) * jax.nn.silu(hd(g_out, GLA_DV))
    y_a = o.reshape(Bsz, L, GLA_VW).astype(hn.dtype) @ w_up_gla

    xbc = jax.nn.silu(causal_dwconv_2(xbc, conv_w, conv_b))
    xs, Bm, Cm = split_cols(xbc, (SSD_D_INNER, SSD_BC, SSD_BC))
    dt = jax.nn.softplus(dt_raw.astype(f32) + dt_bias)
    a = dt * (-jnp.exp(a_log.astype(f32)))
    grp = lambda t: t.reshape(Bsz, L, SSD_GROUPS, SSD_HPG)
    xs_h = xs.reshape(Bsz, L, SSD_GROUPS, SSD_HPG, SSD_HEADDIM)
    y = ssd_chunked(pad_front(xs_h * grp(dt)[..., None]), pad_front(grp(a)),
                    pad_front(Bm.reshape(Bsz, L, SSD_GROUPS, SSD_STATE)),
                    pad_front(Cm.reshape(Bsz, L, SSD_GROUPS, SSD_STATE)))[:, META_PAD:]
    y = y + d_skip.reshape(SSD_GROUPS, SSD_HPG)[:, :, None] * xs_h
    y = y.reshape(Bsz, L, SSD_D_INNER) * jax.nn.silu(z)
    y = rmsnorm_2(y.reshape(Bsz, L, SSD_GROUPS, SSD_D_INNER // SSD_GROUPS),
                ssd_norm_w.reshape(SSD_GROUPS, -1)).reshape(Bsz, L, SSD_D_INNER)
    y_b = y.astype(hn.dtype) @ w_up_ssd

    mixed = jax.nn.sigmoid(gate_a) * y_a + jax.nn.sigmoid(gate_b) * y_b
    return (mixed @ w_out).astype(hn.dtype)

def peer_ffn(h, w_q, sub_keys, u_tab, v_tab):
    T = h.shape[0]
    pad = (-T) % PEER_BLOCK
    hp = jnp.pad(h, ((0, pad), (0, 0))).reshape(-1, PEER_BLOCK, D_MODEL)

    def block(hb):
        n = hb.shape[0]
        q = (hb @ w_q).reshape(n, PEER_HEADS, 2, PEER_HALF)
        s = jnp.einsum('nhid,hikd->nhik', q, sub_keys).astype(jnp.float32)
        s_top, i_top = lax.top_k(s, PEER_TOPK)
        cand = s_top[:, :, 0, :, None] + s_top[:, :, 1, None, :]
        cand_idx = i_top[:, :, 0, :, None] * PEER_N_KEYS + i_top[:, :, 1, None, :]
        best, pos = lax.top_k(cand.reshape(n, PEER_HEADS, PEER_TOPK * PEER_TOPK), PEER_TOPK)
        idx = jnp.take_along_axis(cand_idx.reshape(n, PEER_HEADS, -1), pos, axis=-1)
        w = jax.nn.softmax(best, axis=-1)
        u = jnp.take(u_tab, idx, axis=0)
        act = jax.nn.gelu(jnp.einsum('nhkd,nd->nhk', u, hb).astype(jnp.float32))
        out = jnp.einsum('nhk,nhkd->nd', w * act, jnp.take(v_tab, idx, axis=0))
        return out.astype(hb.dtype)

    return lax.map(block, hp).reshape(-1, D_MODEL)[:T]

def second_inputs(seed: int = 0) -> dict:
    key = jax.random.key(seed)
    ks = jax.random.split(key, 24)
    f32 = jnp.float32
    nrm = lambda k, shape, std: jax.random.normal(k, shape, f32) * std
    gain = lambda k, shape: 1.0 + 0.02 * jax.random.normal(k, shape, f32)
    Dp = DEPTH
    dt0 = jnp.exp(jax.random.uniform(ks[9], (Dp, SSD_HEADS), f32, math.log(1e-3), math.log(1e-1)))
    dt_bias = dt0 + jnp.log(-jnp.expm1(-dt0))
    a_log = jnp.log(jax.random.uniform(ks[10], (Dp, SSD_HEADS), f32, 1.0, 16.0))
    return {
        'x': nrm(ks[0], (BATCH, SEQ, D_MODEL), 1.0),
        'meta_tokens': nrm(ks[1], (N_META, D_MODEL), 1.0),
        'ln_mix_w': gain(ks[2], (Dp, D_MODEL)),
        'w_in': nrm(ks[3], (Dp, D_MODEL, IN_WIDTH), D_MODEL ** -0.5),
        'gla_w_gate2': nrm(ks[4], (Dp, GLA_GATE_RANK, GLA_QK), GLA_GATE_RANK ** -0.5),
        'gla_b_gate': nrm(ks[5], (Dp, GLA_QK), 0.1),
        'gla_norm_w': gain(ks[6], (Dp, GLA_DV)),
        'ssd_conv_w': nrm(ks[7], (Dp, SSD_CONV, SSD_XBC), SSD_CONV ** -0.5),
        'ssd_conv_b': nrm(ks[8], (Dp, SSD_XBC), 0.02),
        'ssd_dt_bias': dt_bias,
        'ssd_a_log': a_log,
        'ssd_d': gain(ks[11], (Dp, SSD_HEADS)),
        'ssd_norm_w': gain(ks[12], (Dp, SSD_D_INNER)),
        'w_up_gla': nrm(ks[13], (Dp, GLA_VW, D_MODEL), GLA_VW ** -0.5),
        'w_up_ssd': nrm(ks[14], (Dp, SSD_D_INNER, D_MODEL), SSD_D_INNER ** -0.5),
        'w_out': nrm(ks[15], (Dp, D_MODEL, D_MODEL), D_MODEL ** -0.5),
        'ln_ffn_w': gain(ks[16], (Dp, D_MODEL)),
        'peer_w_q': nrm(ks[17], (Dp, D_MODEL, PEER_HEADS * PEER_KEY_DIM), D_MODEL ** -0.5),
        'peer_sub_keys': nrm(ks[18], (Dp, PEER_HEADS, 2, PEER_N_KEYS, PEER_HALF), PEER_HALF ** -0.5),
        'peer_u': nrm(ks[19], (Dp, PEER_N_EXPERTS, D_MODEL), D_MODEL ** -0.5),
        'peer_v': nrm(ks[20], (Dp, PEER_N_EXPERTS, D_MODEL), PEER_HEADS ** -0.5),
        'ln_final_w': gain(ks[21], (D_MODEL,)),
    }

def second_block(x, meta_tokens, ln_mix_w, w_in, gla_w_gate2, gla_b_gate, gla_norm_w, ssd_conv_w, ssd_conv_b,
              ssd_dt_bias, ssd_a_log, ssd_d, ssd_norm_w, w_up_gla, w_up_ssd, w_out, ln_ffn_w,
              peer_w_q, peer_sub_keys, peer_u, peer_v, ln_final_w):
    Bsz = x.shape[0]
    meta = jnp.broadcast_to(meta_tokens[None].astype(x.dtype), (Bsz, N_META, D_MODEL))
    h = jnp.concatenate([meta, x], axis=1)
    for l in range(DEPTH):
        hn = rmsnorm_2(h, ln_mix_w[l])
        h = h + hybrid_mixer(hn, w_in[l], gla_w_gate2[l], gla_b_gate[l], gla_norm_w[l], ssd_conv_w[l],
                             ssd_conv_b[l], ssd_dt_bias[l], ssd_a_log[l], ssd_d[l], ssd_norm_w[l],
                             w_up_gla[l], w_up_ssd[l], w_out[l])
        if l == DEPTH - 1:
            h = h[:, N_META:]
        hn = rmsnorm_2(h, ln_ffn_w[l])
        ffn = peer_ffn(hn.reshape(-1, D_MODEL), peer_w_q[l], peer_sub_keys[l], peer_u[l], peer_v[l])
        h = h + ffn.reshape(h.shape)
    return rmsnorm_2(h, ln_final_w)


def setup_inputs(seed=0):
    out = dict(first_inputs(seed))
    for name, value in second_inputs(seed + 1).items():
        if name != "x":
            out[name + "_2"] = value
    return out


def reference(
    x, c, ada_w, ada_b, norm1_w, w_in, gdn_conv_w, gdn_A_log, gdn_dt_bias, gdn_out_norm_w,
    nsa_q_norm_w, nsa_k_norm_cmp, nsa_k_norm_slc, nsa_k_norm_win, cmp_k_pos, cmp_k_w1, cmp_k_w2,
    cmp_v_pos, cmp_v_w1, cmp_v_w2, w_out, norm2_w, ffn_w_up, ffn_conv_w, ffn_conv_b, ffn_w_down,
    meta_tokens_2, ln_mix_w_2, w_in_2, gla_w_gate2_2, gla_b_gate_2, gla_norm_w_2, ssd_conv_w_2,
    ssd_conv_b_2, ssd_dt_bias_2, ssd_a_log_2, ssd_d_2, ssd_norm_w_2, w_up_gla_2, w_up_ssd_2,
    w_out_2, ln_ffn_w_2, peer_w_q_2, peer_sub_keys_2, peer_u_2, peer_v_2, ln_final_w_2,
):
    x = first_block(
        x, c, ada_w, ada_b, norm1_w, w_in, gdn_conv_w, gdn_A_log, gdn_dt_bias, gdn_out_norm_w,
        nsa_q_norm_w, nsa_k_norm_cmp, nsa_k_norm_slc, nsa_k_norm_win, cmp_k_pos, cmp_k_w1,
        cmp_k_w2, cmp_v_pos, cmp_v_w1, cmp_v_w2, w_out, norm2_w, ffn_w_up, ffn_conv_w,
        ffn_conv_b, ffn_w_down,
    )
    return second_block(
        x, meta_tokens_2, ln_mix_w_2, w_in_2, gla_w_gate2_2, gla_b_gate_2, gla_norm_w_2,
        ssd_conv_w_2, ssd_conv_b_2, ssd_dt_bias_2, ssd_a_log_2, ssd_d_2, ssd_norm_w_2,
        w_up_gla_2, w_up_ssd_2, w_out_2, ln_ffn_w_2, peer_w_q_2, peer_sub_keys_2, peer_u_2,
        peer_v_2, ln_final_w_2,
    )


_drawn_inputs = setup_inputs


def setup_inputs(seed=0):
    import zlib

    import numpy as np

    out = dict(_drawn_inputs(seed))
    spreads = {}
    factors = {'norm1_w': 4.274,
     'gdn_out_norm_w': 5.154,
     'nsa_q_norm_w': 8.0,
     'nsa_k_norm_cmp': 29.367,
     'nsa_k_norm_slc': 8.0,
     'nsa_k_norm_win': 8.0,
     'cmp_k_pos': 8.0,
     'cmp_v_pos': 61.259,
     'norm2_w': 3.692,
     'ffn_conv_b': 3.82,
     'gla_b_gate_2': 2.83,
     'gla_norm_w_2': 98.561,
     'ssd_d_2': 200.0,
     'ssd_norm_w_2': 182.304,
     'ln_final_w_2': 22.825,
     'ln_mix_w_2': 3.583,
     'ssd_conv_b_2': 32.753,
     'ln_ffn_w_2': 64.0}
    for name, (base, spread) in spreads.items():
        noise = np.random.default_rng([zlib.crc32(name.encode()), seed]).standard_normal(out[name].shape)
        drawn = base * np.exp(spread * noise) if base else spread * noise
        out[name] = __import__('jax').numpy.asarray(drawn.astype(out[name].dtype))
    for name, factor in factors.items():
        out[name] = (out[name] * factor).astype(out[name].dtype)
    return out
```

```python
import concourse.bass as bass
from concourse import mybir
from contextlib import ExitStack

F32 = mybir.dt.float32
U32 = mybir.dt.uint32
ALU = mybir.AluOpType
ACT = mybir.ActivationFunctionType
AX = mybir.AxisListType
PE, SC, VE, GP, SY = "tensor", "scalar", "vector", "gpsimd", "sync"
NEG = -1e30
EPS = 1e-6
DBG = None


class Queues:

    def __init__(self, nc, ctx):
        self.nc, self.ctx = nc, ctx
        self.q = {e: [] for e in (PE, SC, VE, GP, SY)}
        self.hold = {e: [] for e in self.q}
        self.dma_sems = {}
        self.counts = {}

    def add(self, eng, fn, w=(), free=False):
        q = self.q[eng]
        waits = [t for t in w if t is not None] + self.hold[eng]
        self.hold[eng] = []
        if not free and eng in (SC, VE, GP):
            for n in range(len(q) - 1, -1, -1):
                if q[n][2] is None:
                    waits.append((eng, n))
                    break
        q.append((fn, waits, None))
        return (eng, len(q) - 1)

    def dma(self, eng, sem, out, in_, w=()):
        if sem not in self.dma_sems:
            self.dma_sems[sem] = self.ctx.enter_context(self.nc.semaphore("d_" + sem))
            self.counts[sem] = 0
        self.counts[sem] += 16
        waits = [t for t in w if t is not None] + self.hold[eng]
        self.hold[eng] = []
        self.q[eng].append((lambda e: e.dma_start(out, in_), waits, sem))
        return (sem, self.counts[sem])

    def last(self, *engs):
        out = []
        for e in engs:
            for n in range(len(self.q[e]) - 1, -1, -1):
                if self.q[e][n][2] is None:
                    out.append((e, n))
                    break
        return out

    def barrier(self, extra=()):
        marks = {e: self.last(e) for e in (PE, SC, VE, GP)}
        for e in marks:
            self.hold[e] += [t for x in marks if x != e or e != PE for t in marks[x]] + list(extra)
        return [t for x in marks.values() for t in x]

    def emit(self, block):
        used = set()
        for q in self.q.values():
            for _, waits, _ in q:
                used |= {t for t in waits if t[0] in self.q}
        sems = {e: self.ctx.enter_context(self.nc.semaphore("s_" + e)) for e in self.q}
        value, total = {}, {}
        for e, q in self.q.items():
            n = 0
            for i in range(len(q)):
                if (e, i) in used:
                    n += 1
                    value[(e, i)] = n
        for e, q in self.q.items():
            def body(eng, e=e, q=q):
                seen = {}
                for i, (fn, waits, dsem) in enumerate(q):
                    need = {}
                    for t in waits:
                        v = value[t] if t[0] in self.q else t[1]
                        need[t[0]] = max(need.get(t[0], 0), v)
                    for s, v in need.items():
                        if seen.get(s, 0) < v:
                            eng.wait_ge(sems[s] if s in self.q else self.dma_sems[s], v)
                            seen[s] = v
                    if fn is None:
                        continue
                    ins = fn(eng)
                    if dsem is not None:
                        ins.then_inc(self.dma_sems[dsem], 16)
                    elif (e, i) in value:
                        ins.then_inc(sems[e], 1)
            {PE: block.tensor, SC: block.scalar, VE: block.vector, GP: block.gpsimd, SY: block.sync}[e](body)


class Slots:

    def __init__(self, bufs):
        self.bufs = bufs
        self.free = list(range(len(bufs)))
        self.readers = [[] for _ in bufs]

    def take(self):
        i = self.free.pop(0)
        r, self.readers[i] = self.readers[i], []
        return i, self.bufs[i], r

    def done(self, i, *toks):
        if i not in self.free:
            self.free.append(i)
        self.readers[i] += list(toks)


CONST = {}


def const_array():
    import numpy as np
    CONST.clear()
    p = np.arange(128)[:, None]
    i = np.arange(128)[None, :]
    ch = (p // 64) == (i // 64)
    parts = [("ident", p == i), ("ones", np.ones((128, 128))), ("upper", p <= i), ("strict", p < i),
             ("cum64", ch & (p <= i)), ("same64", ch)]
    for l in range(7):
        s = 1 << l
        parts.append((f"lvl{l}", (p // (2 * s) == i // (2 * s)) & (i % (2 * s) >= s) & (p % (2 * s) < s)))
    parts.append(("causal", np.where(i > p, NEG, 0.0)))
    t = np.arange(512)[None, :]
    parts.append(("notfirst", np.broadcast_to(t % 64 != 0, (128, 512))))
    parts.append(("col01", np.concatenate([p // 64 == 0, p // 64 == 1], 1)))
    n = np.arange(31)[None, None, :]
    q = np.arange(4)[None, :, None] * 128 + p[:, :, None]
    ok = (n * 16 + 31 <= q)
    parts.append(("cmpadd", np.where(ok, 0.0, NEG).reshape(128, 124)))
    parts.append(("cmpmul", ok.reshape(128, 124)))
    parts.append(("iota", np.broadcast_to(i, (128, 128))))
    off = 0
    for name, a in parts:
        CONST[name] = (off, a.shape[1])
        off += a.shape[1]
    return np.concatenate([a.astype(np.float32) for _, a in parts], axis=1)


def mask_array():
    import numpy as np
    s = np.arange(128)[:, None]
    t = np.arange(512)[None, :]
    same = (s // 64) == ((t % 128) // 64)
    a = np.concatenate([same & (s <= t % 128), same & (s > t % 128)], axis=1)
    return a.astype(np.uint32)


def build(nc, D, shapes):
    with ExitStack() as ctx:
        _build(nc, D, ctx)


def _build(nc, D, ctx):
    Q = Queues(nc, ctx)

    def sb(name, shape, dt=F32, c=ctx):
        return c.enter_context(nc.sbuf_tensor(name, shape, dt))

    ncst = D["consts"].shape[1]
    cst = sb("cst", [128, ncst])
    C = {k: cst[:, o:o + n] for k, (o, n) in CONST.items()}
    colw = D["cols"].shape[1]
    cols = sb("cols", [128, colw])
    cc = {k: cols[:, o:o + n] for k, (o, n) in COLS.items()}
    xT = sb("xT", [128, 8, 512])
    hT = sb("hT", [128, 8, 512])
    mT = sb("mT", [128, 8, 16])
    hm = sb("hm", [128, 8, 16])
    modc = sb("modc", [128, 48])
    scl = sb("scl", [128, 16])
    ring = [sb(f"ring{i}", [128, 4096]) for i in range(3)]
    bank = [ctx.enter_context(nc.psum_tensor(f"bank{i}", [128, 512], F32)) for i in range(8)]
    B = Slots(bank)
    R = Slots(ring)
    ident = C["ident"]

    def mm(out, pairs, w=(), start=True, stop=True, check=True):
        n = len(pairs)
        for i, (a, b) in enumerate(pairs):
            t = Q.add(PE, lambda e, a=a, b=b, s=start and i == 0, z=stop and i == n - 1: e.matmul(
                out, a, b, start=s, stop=z, skip_group_check=not check), w if i == 0 else ())
        return t

    def tr(out, in_, w=()):
        k = in_.shape[0]
        return Q.add(PE, lambda e: e.transpose(out, in_, ident[0:k, 0:k]), w)

    def act(out, in_, fn, w=(), free=False, **kw):
        return Q.add(SC, lambda e: e.activation(out, in_, fn, **kw), w, free)

    def tt(out, a, b, op, w=(), free=False, eng=VE):
        return Q.add(eng, lambda e: e.tensor_tensor(out, a, b, op), w, free)

    def ts(out, a, s1, op0, s2=None, op1=None, w=(), free=False, eng=VE):
        if op1 is None:
            return Q.add(eng, lambda e: e.tensor_scalar(out, a, s1, None, op0), w, free)
        return Q.add(eng, lambda e: e.tensor_scalar(out, a, s1, s2, op0, op1), w, free)

    def stt(out, a, s, b, op0, op1, w=(), free=False):
        return Q.add(VE, lambda e: e.scalar_tensor_tensor(out=out, in0=a, scalar=s, in1=b, op0=op0, op1=op1),
                     w, free)

    def recip(out, a, w=(), free=False):
        return Q.add(VE, lambda e: e.reciprocal(out, a), w, free)

    def copy(out, a, w=(), free=False, eng=VE):
        if eng == SC:
            return act(out, a, ACT.Copy, w, free)
        return Q.add(eng, lambda e: e.tensor_copy(out, a), w, free)

    def red(out, a, op, w=(), free=False):
        return Q.add(VE, lambda e: e.tensor_reduce(out, a, AX.X, op), w, free)

    def bc(ap, n):
        a = ap.unsqueeze(2)
        return a.to_broadcast([a.shape[0], a.shape[1], n])

    def rep(ap, n):
        a = ap.unsqueeze(1)
        return a.to_broadcast([a.shape[0], n, a.shape[2]])

    M, A_, S_ = ALU.mult, ALU.add, ALU.subtract

    stream = []

    def weights(name, idx, n):
        i, buf, free = R.take()
        t = Q.dma(SY, f"ring{i}", buf[:, 0:n], D[name][idx][:, 0:n], free)
        stream.append((i, buf, t))

    def next_w():
        return stream.pop(0)

    plan = []
    for s in range(12):
        plan.append(("ada", s, 4096))
    for s in range(6):
        plan.append(("win1", s, 4096))
    plan.append(("win1t", 0, 8 * 276))
    plan.append(("cmpw1", 0, 4096))
    plan.append(("cmpw1", 1, 4096))
    plan.append(("cmpw2", 0, 256))
    for s in range(2):
        plan.append(("wout1", s, 4096))
    for s in range(11):
        plan.append(("wup", s, 4096))
    for s in range(8):
        plan.append(("wdn", s, 2816))
    for s in range(2):
        plan.append(("qk2", s, 4096))
    plan.append(("glow", 0, 128))
    for s in range(2):
        plan.append(("v2", s, 4096))
    for n in ("gout2", "gatea", "upgla"):
        for s in range(2):
            plan.append((n, s, 4096))
    plan.append(("dt2", 0, 256))
    for g in range(4):
        plan.append(("xs2", g, 4096))
        plan.append(("bc2", g, 2048))
        plan.append(("z2", g, 4096))
    for s in range(2):
        plan.append(("gateb", s, 4096))
    for s in range(4):
        plan.append(("upssd", s, 4096))
    for s in range(2):
        plan.append(("wout2", s, 4096))
    for s in range(4):
        plan.append(("wq", s, 4096))
    plan.append(("subk", 0, 2048))
    for s in range(64):
        plan.append(("uv", s, 4096))

    def slot(name, idx):
        i, buf, t = next_w()
        order.append((name, idx))
        assert loaded[len(order) - 1] == (name, idx), (loaded[len(order) - 1], name, idx)
        return i, buf, t

    loaded = [(a, b) for a, b, _ in plan]
    order = []

    def release(i, tok):
        R.done(i, tok)
        if plan:
            weights(*plan.pop(0))

    k0 = Q.dma(SC, "c0", cst[:, :], D["consts"])
    k0 = Q.dma(SC, "c0", cols[:, :], D["cols"])
    k0 = Q.dma(SC, "c0", mT[:, :, :], D["metaT"])
    k1 = Q.dma(SC, "c1", xT[:, :, :], D["xT"])
    g2w = sb("g2w", [16, 512])
    k2 = Q.dma(SC, "c2", g2w[:, :], D["gate2w"])
    for _ in range(3):
        weights(*plan.pop(0))
    for e in (PE, VE, GP):
        Q.hold[e] += [k0]
    Q.hold[SC] += [k0]

    dumped = []

    def dump(name, ap):
        if DBG == name:
            toks = Q.last(PE, SC, VE, GP)
            d = D["dbg"]
            shp = list(ap.shape)
            n = 1
            for v in shp[1:]:
                n *= v
            dst = d[0:shp[0], 0:n]
            if len(shp) == 3:
                dst = dst.rearrange("p (a b) -> p a b", b=shp[2])
            Q.dma(SY, "dbg", dst, ap, toks)
            dumped.append(1)
            return True
        return False

    def norm_stats(src, T, N, out, tmp, w=()):
        k = len(src)
        i, ps, fr = B.take()
        for j, s in enumerate(src):
            a = act(tmp[j % 2][:, 0:T], s, ACT.Square, (list(w) if j == 0 else []) +
                    ([pes[-2]] if j >= 2 else []), free=j > 0)
            if j == 0:
                pes = []
            pes.append(mm(ps[:, 0:T], [(C["ones"], tmp[j % 2][:, 0:T])], [a] + (fr if j == 0 else []),
                          start=j == 0, stop=j == k - 1))
        ts(out, ps[:, 0:T], 1.0 / N, M, EPS, A_, w=[pes[-1]])
        v = recip(out, out)
        B.done(i, v)
        return act(out, out, ACT.Sqrt, [v])

    def linear(name, nslots, per, kt, rhs, consume, w=(), T=512, meta=None):
        n = 0
        for s in range(nslots):
            i, buf, t = slot(name, s)
            v = buf[:, 0:per * kt * 128].rearrange("p (a k n) -> p a k n", a=per, k=kt)
            for a in range(per):
                bi, ps, fr = B.take()
                if meta is not None:
                    m = mm(ps[:, 0:16], [(v[:, a, k, :], meta(k)) for k in range(kt)], [t] + fr + list(w))
                    B.done(bi, consume(n, ps, m, True))
                    bi, ps, fr = B.take()
                m = mm(ps[:, 0:T], [(v[:, a, k, :], rhs(k)) for k in range(kt)], [t] + fr + list(w))
                if meta is not None:
                    B.done(bi, consume(n, ps, m, False))
                else:
                    B.done(bi, consume(n, ps, m))
                n += 1
            release(i, m)

    finish = lambda: Q.emit(ctx.enter_context(nc.Block()))

    def endit():
        Q.q[SY].append((None, [("dbg", Q.counts["dbg"])], None))
        finish()

    with ExitStack() as ar:
        row = sb("modrow", [1, 2, 512], F32, ar)
        scv = sb("scv", [128, 8], F32, ar)
        tmp = [sb(f"n1t{j}", [128, 512], F32, ar) for j in range(2)]
        rstd = sb("n1r", [128, 512], F32, ar)
        a0 = act(scv[:, :], cc["c"], ACT.Silu)
        bi, pm, fr = B.take()
        cprev = []
        for s in range(12):
            i, buf, t = slot("ada", s)
            v = buf[:, :].rearrange("p (k n) -> p k n", k=8)
            pi, ps, f2 = B.take()
            m = mm(ps[0:1, :], [(scv[:, k:k + 1], v[:, k, :]) for k in range(8)], [t, a0] + f2)
            release(i, m)
            cp = copy(row[0:1, s % 2, :], ps[0:1, :], [m] + (cprev[s - 2:s - 1] if s >= 2 else []), eng=VE)
            B.done(pi, cp)
            for j in range(4):
                m = Q.add(PE, lambda e, s=s, j=j: e.matmul(
                    pm[:, 4 * s + j:4 * s + j + 1], row[0:1, s % 2, 128 * j:128 * j + 128],
                    C["ones"][0:1, 0:1], start=(s == 0 and j == 0), stop=True, skip_group_check=True), [cp])
            cprev.append(m)
        v = tt(modc[:, :], pm[:, 0:48], cc["adab"], A_, [m])
        B.done(bi, v)
        stt(scl[:, 0:8], modc[:, 8:16], 1.0, cc["norm1"], A_, M)
        stt(scl[:, 8:16], modc[:, 32:40], 1.0, cc["norm2"], A_, M)
        n = norm_stats([xT[:, k, :] for k in range(8)], 512, 1024, rstd[:, :], tmp, [k1])
        for k in range(8):
            stt(hT[:, k, :], xT[:, k, :], scl[:, k:k + 1], rstd[:, :], M, M, [n], free=k > 0)
        for k in range(8):
            hready = ts(hT[:, k, :], hT[:, k, :], modc[:, k:k + 1], A_, free=k > 0)
        if dump("h1", hT[:, :, :]):
            return endit()
        Q.barrier()

    with ExitStack() as ar:
        qkv = sb("qkv", [128, 12, 512], F32, ar)
        gz = sb("gz", [128, 4, 512], F32, ar)
        nsq = sb("nsq", [128, 4, 512], F32, ar)
        kvc = sb("kvc", [128, 2, 512], F32, ar)
        kk2 = sb("kk2", [128, 2, 512], F32, ar)
        tm = sb("tm", [128, 4, 276], F32, ar)
        kcmp = sb("kcmp", [128, 32], F32, ar)
        vcmp = sb("vcmp", [32, 128], F32, ar)
        mix = hT
        with ExitStack() as a2:
            cv = Slots([sb(f"cv{j}", [128, 512], F32, a2) for j in range(2)])
            sq = Slots([sb(f"sq{j}", [128, 512], F32, a2) for j in range(2)])
            rs = Slots([sb(f"rs{j}", [128, 512], F32, a2) for j in range(2)])

            def unit(dst, src, scale, eps, rdy, wcol=None, out_scale=1.0, T=512):
                si, s, f = sq.take()
                a = act(s[:, 0:T], src, ACT.Square, [rdy] + f)
                bi, ps, fr = B.take()
                m = mm(ps[:, 0:T], [(C["ones"], s[:, 0:T])], [a] + fr)
                sq.done(si, m)
                ri, r, f = rs.take()
                v = ts(r[:, 0:T], ps[:, 0:T], scale, M, eps, A_, w=[m] + f)
                B.done(bi, v)
                v = recip(r[:, 0:T], r[:, 0:T])
                a = act(r[:, 0:T], r[:, 0:T], ACT.Sqrt, [v])
                v = stt(dst, src, wcol if wcol is not None else out_scale, r[:, 0:T], M, M, [a])
                rs.done(ri, v)
                return v

            def take1(n, ps, m):
                if n < 12:
                    ci, c, f = cv.take()
                    w = cc["conv1"][:, 4 * n:4 * n + 4]
                    ts(c[:, :], ps[:, :], w[:, 3:4], M, w=[m] + f)
                    for d in (1, 2, 3):
                        v = stt(c[:, d:512], ps[:, 0:512 - d], w[:, 3 - d:4 - d], c[:, d:512], M, A_)
                    a = act(qkv[:, n, :], c[:, :], ACT.Silu, [v])
                    cv.done(ci, a)
                    return v
                if n < 16:
                    return act(gz[:, n - 12, :], ps[:, :], ACT.Silu, [m])
                if n < 20:
                    return copy(nsq[:, n - 16, :], ps[:, :], [m], eng=SC)
                if n < 22:
                    return copy(kvc[:, n - 20, :], ps[:, :], [m])
                return copy(kk2[:, n - 22, :], ps[:, :], [m], eng=SC)

            linear("win1", 6, 4, 8, lambda k: hT[:, k, :], take1, [hready])
            i, buf, t = slot("win1t", 0)
            wt = buf[:, 0:8 * 276].rearrange("p (k n) -> p k n", k=8)
            for j in range(4):
                bi, ps, fr = B.take()
                m = mm(ps[:, 0:276], [(hT[:, k, 128 * j:128 * j + 128], wt[:, k, :]) for k in range(8)], [t] + fr)
                B.done(bi, copy(tm[:, j, :], ps[:, 0:276], [m]))
            release(i, m)
            sil = Q.last(SC)[0]
            for n in range(8):
                unit(qkv[:, n, :], qkv[:, n, :], 1.0, EPS, sil, out_scale=(128 ** -0.5 if n < 4 else 1.0))
            for n in range(4):
                unit(nsq[:, n, :], nsq[:, n, :], 1 / 128, EPS, sil, cc["qn"])
            unit(kk2[:, 0, :], kk2[:, 0, :], 1 / 128, EPS, sil, cc["kslc"])
            unit(kk2[:, 1, :], kk2[:, 1, :], 1 / 128, EPS, sil, cc["kwin"])
            blk = sb("blk", [128, 32, 31], F32, a2)
            hid = sb("hid", [128, 32], F32, a2)
            mw = None
            for c in range(2):
                i, buf, t = slot("cmpw1", c)
                w1 = buf[:, :].rearrange("p (a n) -> p a n", a=32)
                src = kvc[:, c, 0:512].rearrange("p (n s) -> p s n", s=16)
                pos = cc["kpos" if c == 0 else "vpos"]
                tt(blk[:, 0:16, :], src[:, :, 0:31], bc(pos[:, 0:16], 31), A_, Q.last(PE))
                v = tt(blk[:, 16:32, :], src[:, :, 1:32], bc(pos[:, 16:32], 31), A_)
                bi, ps, fr = B.take()
                m = mm(ps[:, 0:31], [(w1[:, a, :], blk[:, a, :]) for a in range(32)], [t, v] + fr)
                release(i, m)
                a = act(hid[:, 0:31], ps[:, 0:31], ACT.Silu, [m] + Q.last(PE))
                B.done(bi, a)
                if c == 0:
                    i2 = None
                    hidk = sb("hidk", [128, 32], F32, a2)
                    akey = copy(hidk[:, 0:31], hid[:, 0:31], [a])
            i2, w2, t2 = slot("cmpw2", 0)
            bi, ps, fr = B.take()
            m = mm(ps[:, 0:31], [(w2[:, 0:128], hidk[:, 0:31])], [t2, akey] + fr)
            v = copy(kcmp[:, 0:31], ps[:, 0:31], [m])
            B.done(bi, v)
            unit(kcmp[:, 0:31], kcmp[:, 0:31], 1 / 128, EPS, v, cc["kcmpn"], T=31)
            bi, ps, fr = B.take()
            m = mm(ps[0:31, 0:128], [(hid[:, 0:31], w2[:, 128:256])], [a] + fr)
            release(i2, m)
            B.done(bi, copy(vcmp[0:31, :], ps[0:31, 0:128], [m]))
            if dump("qkv", qkv[:, :, :]) or dump("kcmp", kcmp[:, 0:31]) or dump("vcmp", vcmp[0:31, :]) \
                    or dump("nsq", nsq[:, :, :]) or dump("kk2", kk2[:, :, :]) or dump("tm", tm[:, :, :]):
                return endit()
            Q.barrier()

        with ExitStack() as a2:
            def big(name):
                return sb(name, [128, 4, 128], F32, a2)
            sm = {k: sb("g_" + k, [128, 4, 4], F32, a2) for k in
                  ("g", "beta", "u", "v", "gc", "gt", "egc", "kds", "gl", "bg")}
            gA = tm[:, :, 256:260]
            gB = tm[:, :, 260:264]
            nA = sb("nA", [128, 4], F32, a2)
            act(nA[:, :], cc["alog"], ACT.Exp)
            ts(nA[:, :], nA[:, :], -1.0, M, w=Q.last(SC))
            v = tt(sm["u"][:, :, :], gA, rep(cc["dtb1"], 4), A_)
            act(sm["v"][:, :, :], sm["u"][:, :, :], ACT.Abs, [v])
            act(sm["v"][:, :, :], sm["v"][:, :, :], ACT.Exp, scale=-1.0)
            a = act(sm["v"][:, :, :], sm["v"][:, :, :], ACT.Ln, bias=1.0)
            stt(sm["u"][:, :, :], sm["u"][:, :, :], 0.0, sm["v"][:, :, :], ALU.max, A_, [a])
            g = tt(sm["g"][:, :, :], sm["u"][:, :, :], rep(nA[:, :], 4), M)
            a = act(sm["beta"][:, :, :], gB, ACT.Sigmoid)
            bi, ps, fr = B.take()
            m = mm(ps[:, 0:16], [(C["upper"], sm["g"][:, :, :].rearrange("p a b -> p (a b)"))], [g, a] + fr)
            v = copy(sm["gc"][:, :, :].rearrange("p a b -> p (a b)"), ps[:, 0:16], [m])
            B.done(bi, v)
            bi, ps, fr = B.take()
            m = mm(ps[:, 0:16], [(C["ones"], sm["g"][:, :, :].rearrange("p a b -> p (a b)"))], fr)
            v = copy(sm["gt"][:, :, :].rearrange("p a b -> p (a b)"), ps[:, 0:16], [m])
            B.done(bi, v)
            v = tt(sm["kds"][:, :, :], sm["gt"][:, :, :], sm["gc"][:, :, :], S_)
            act(sm["kds"][:, :, :], sm["kds"][:, :, :], ACT.Exp, [v])
            act(sm["gl"][:, :, :], sm["gt"][:, :, :], ACT.Exp)
            a = act(sm["egc"][:, :, :], sm["gc"][:, :, :], ACT.Exp)
            tt(sm["bg"][:, :, :], sm["beta"][:, :, :], sm["egc"][:, :, :], M, [a])

            kt_, vb, kbe, kd = big("kt_"), big("vb"), big("kbe"), big("kd")
            gcb, egb, btb, dtm, AT, aT = big("gcb"), big("egb"), big("btb"), big("dtm"), big("AT"), big("aT")
            X, XT, BT, Y, wT, u, vn, qd = (big(n_) for n_ in ("X", "XT", "BT", "Y", "wT", "u", "vn", "qd"))
            St = big("St")

            def four(fn, w=()):
                bi, ps, fr = B.take()
                for h in range(4):
                    lst = fn(h)
                    for n_, (l, r) in enumerate(lst):
                        m = Q.add(PE, lambda e, l=l, r=r, h=h, s=(h == 0 and n_ == 0): e.matmul(
                            ps[:, 128 * h:128 * h + 128], l, r, start=s, stop=True, skip_group_check=True),
                            (list(w) + fr) if h == 0 and n_ == 0 else ())
                return bi, ps[:, :].rearrange("p (a b) -> p a b", a=4), m

            for mt in range(4):
                c0 = 128 * mt
                kT = lambda h: qkv[:, 4 + h, c0:c0 + 128]
                qT = lambda h: qkv[:, h, c0:c0 + 128]
                for what in (4, 8):
                    bi, ps, fr = B.take()
                    for h in range(4):
                        m = tr(ps[:, 128 * h:128 * h + 128], qkv[:, what + h, c0:c0 + 128],
                               (fr + Q.last(VE, SC)) if h == 0 else ())
                    p3 = ps[:, :].rearrange("p (a b) -> p a b", a=4)
                    if what == 4:
                        tt(kbe[:, :, :], p3, bc(sm["bg"][:, mt, :], 128), M, [m] + Q.last(PE))
                        v = tt(kd[:, :, :], p3, bc(sm["kds"][:, mt, :], 128), M, free=True)
                    else:
                        v = tt(vb[:, :, :], p3, bc(sm["beta"][:, mt, :], 128), M, [m] + Q.last(PE))
                    B.done(bi, v)
                bi, p3, m = four(lambda h: [(sm["g"][:, mt, h:h + 1].to_broadcast([128, 128]), C["upper"])])
                act(egb[:, :, :], p3, ACT.Exp, [m] + Q.last(VE))
                v = tt(dtm[:, :, :], p3, bc(sm["gc"][:, mt, :], 128), S_, [m] + Q.last(SC))
                B.done(bi, v)
                v = ts(dtm[:, :, :], dtm[:, :, :], 0.0, ALU.min)
                a = act(dtm[:, :, :], dtm[:, :, :], ACT.Exp, [v])
                tt(dtm[:, :, :], dtm[:, :, :], rep(C["upper"], 4), M, [a])
                bi, p3, m = four(lambda h: [(sm["beta"][:, mt, h:h + 1].to_broadcast([128, 128]), ident)])
                v = tt(btb[:, :, :], p3, rep(C["strict"], 4), M, [m])
                B.done(bi, v)
                v = tt(btb[:, :, :], btb[:, :, :], dtm[:, :, :], M)
                bi, p3, m = four(lambda h: [(kT(h), kT(h))])
                v = tt(AT[:, :, :], p3, btb[:, :, :], M, [m])
                B.done(bi, v)
                bi, p3, m = four(lambda h: [(kT(h), qT(h))])
                v = tt(aT[:, :, :], p3, dtm[:, :, :], M, [m] + Q.last(PE))
                B.done(bi, v)
                tt(qd[:, :, :], qkv[:, 0:4, c0:c0 + 128], egb[:, :, :], M, Q.last(SC))
                tt(BT[:, :, :], AT[:, :, :], rep(C["lvl0"], 4), M)
                v = tt(XT[:, :, :], rep(ident, 4), BT[:, :, :], S_)
                bi, ps, fr = B.take()
                for h in range(4):
                    m = tr(ps[:, 128 * h:128 * h + 128], XT[:, h, :], ([v] + fr) if h == 0 else ())
                v = copy(X[:, :, :], ps[:, :].rearrange("p (a b) -> p a b", a=4), [m])
                B.done(bi, v)
                for l in range(1, 7):
                    v = tt(BT[:, :, :], AT[:, :, :], rep(C[f"lvl{l}"], 4), M, Q.last(PE))
                    bi, p3, m = four(lambda h: [(BT[:, h, :], X[:, h, :])], [v])
                    v = copy(Y[:, :, :], p3, [m])
                    B.done(bi, v)
                    bi, p3, m = four(lambda h: [(Y[:, h, :], XT[:, h, :])], [v])
                    if l < 6:
                        b2, p4, m2 = four(lambda h: [(XT[:, h, :], Y[:, h, :])])
                    else:
                        m2 = m
                    v = tt(XT[:, :, :], XT[:, :, :], p3, S_, [m2])
                    B.done(bi, v)
                    if l < 6:
                        v = tt(X[:, :, :], X[:, :, :], p4, S_, [m2])
                        B.done(b2, v)
                bi, p3, m = four(lambda h: [(kbe[:, h, :], XT[:, h, :])], [v])
                v = copy(wT[:, :, :], p3, [m])
                B.done(bi, v)
                bi, p3, m = four(lambda h: [(XT[:, h, :], vb[:, h, :])])
                v = copy(u[:, :, :], p3, [m])
                B.done(bi, v)
                if mt > 0:
                    bi, p3, m = four(lambda h: [(wT[:, h, :], St[:, h, :])], [v])
                    v = tt(vn[:, :, :], u[:, :, :], p3, S_, [m])
                    B.done(bi, v)
                    V_ = vn
                else:
                    V_ = u
                bi, p3, m = four(lambda h: ([(St[:, h, :], qd[:, h, :])] if mt > 0 else []) +
                                 [(V_[:, h, :], aT[:, h, :])], [v])
                v = copy(mix[:, 0:4, c0:c0 + 128], p3, [m])
                B.done(bi, v)
                if mt < 3:
                    bi, p3, m = four(lambda h: [(kd[:, h, :], V_[:, h, :])])
                    if mt == 0:
                        v = copy(St[:, :, :], p3, [m])
                    else:
                        tt(St[:, :, :], St[:, :, :], bc(sm["gl"][:, mt, :], 128), M, [m])
                        v = tt(St[:, :, :], St[:, :, :], p3, A_)
                    B.done(bi, v)
            Q.barrier()
            sq = Slots([sb(f"gsq{j}", [128, 512], F32, a2) for j in range(2)])
            rs = Slots([sb(f"grs{j}", [128, 512], F32, a2) for j in range(2)])
            for h in range(4):
                si, s, f = sq.take()
                a = act(s[:, :], mix[:, h, :], ACT.Square, f)
                bi, ps, fr = B.take()
                m = mm(ps[:, :], [(C["ones"], s[:, :])], [a] + fr)
                sq.done(si, m)
                ri, r, f = rs.take()
                v = ts(r[:, :], ps[:, :], 1 / 128, M, EPS, A_, w=[m] + f)
                B.done(bi, v)
                v = recip(r[:, :], r[:, :])
                a = act(r[:, :], r[:, :], ACT.Sqrt, [v])
                stt(mix[:, h, :], mix[:, h, :], cc["gdnn"], r[:, :], M, M, [a])
                rs.done(ri, tt(mix[:, h, :], mix[:, h, :], gz[:, h, :], M))
            if dump("gdn", mix[:, 0:4, :]):
                return endit()
            Q.barrier()

        with ExitStack() as a2:
            Pb = Slots([sb(f"P{j}", [128, 512], F32, a2) for j in range(3)])
            PT = Slots([sb(f"PT{j}", [128, 512], F32, a2) for j in range(3)])
            st = sb("st", [128, 48, 4], F32, a2)
            gates = sb("gates", [128, 4, 12], F32, a2)
            act(gates[:, :, :], tm[:, :, 264:276], ACT.Sigmoid)
            gtok = Q.last(SC)[0]
            SCL = 128 ** -0.5
            nst = 0
            for mt in range(4):
                L = 128 * (mt + 1)
                for h in range(4):
                    qT = nsq[:, h, 128 * mt:128 * mt + 128]
                    pvs = []
                    for br in range(3):
                        n_ = 31 if br == 0 else L
                        rhs = kcmp[:, 0:31] if br == 0 else kk2[:, br - 1, 0:L]
                        bi, ps, fr = B.take()
                        m = mm(ps[:, 0:n_], [(qT, rhs)], fr)
                        s4 = st[:, nst, :]
                        nst += 1
                        if br == 0:
                            add = C["cmpadd"][:, 31 * mt:31 * mt + 31]
                            tt(ps[:, 0:31], ps[:, 0:31], add, A_, [m], free=True)
                        else:
                            tt(ps[:, L - 128:L], ps[:, L - 128:L], C["causal"], A_, [m], free=True)
                        red(s4[:, 0:1], ps[:, 0:n_], ALU.max)
                        v = ts(s4[:, 1:2], s4[:, 0:1], -1e25, ALU.max, -SCL, M)
                        pi, P, f = Pb.take()
                        a = act(P[:, 0:n_], ps[:, 0:n_], ACT.Exp, [v] + f, free=True, bias=s4[:, 1:2],
                                scale=SCL, accum_out=s4[:, 2:3])
                        B.done(bi, a)
                        v = ts(s4[:, 3:4], s4[:, 2:3], 1e-30, ALU.max, w=[a, gtok])
                        recip(s4[:, 3:4], s4[:, 3:4])
                        tt(s4[:, 3:4], s4[:, 3:4], gates[:, mt, 3 * h + br:3 * h + br + 1], M)
                        if br == 0:
                            v = stt(P[:, 0:31], P[:, 0:31], s4[:, 3:4], C["cmpmul"][:, 31 * mt:31 * mt + 31], M, M)
                        else:
                            v = ts(P[:, 0:n_], P[:, 0:n_], s4[:, 3:4], M)
                        bi, ps, fr = B.take()
                        ti, T_, tf = PT.take()
                        if br == 0:
                            m = tr(ps[0:31, 0:128], P[:, 0:31], [v] + fr)
                            v = copy(T_[0:31, 0:128], ps[0:31, 0:128], [m] + tf, eng=SC, free=True)
                            pvs.append((vcmp[0:31, :], T_[0:31, 0:128], v, ti))
                        else:
                            for j in range(mt + 1):
                                m = tr(ps[:, 128 * j:128 * j + 128], P[:, 128 * j:128 * j + 128],
                                       ([v] + fr) if j == 0 else ())
                            v = copy(T_[:, 0:L], ps[:, 0:L], [m] + tf, eng=SC, free=True)
                            for j in range(mt + 1):
                                pvs.append((tm[:, j, 128 * (br - 1):128 * br], T_[:, 128 * j:128 * j + 128], v, ti))
                        Pb.done(pi, m)
                        B.done(bi, v)
                    bi, ps, fr = B.take()
                    for n_, (l, r, v, ti) in enumerate(pvs):
                        m = mm(ps[:, 0:128], [(l, r)], [v] + (fr if n_ == 0 else []), start=n_ == 0,
                               stop=n_ == len(pvs) - 1)
                        PT.done(ti, m)
                    B.done(bi, copy(mix[:, 4 + h, 128 * mt:128 * mt + 128], ps[:, 0:128], [m], free=True))
            if dump("mixed", mix[:, :, :]):
                return endit()
            Q.barrier()

    def res1(gate):
        def f(n, ps, m):
            return stt(xT[:, n, :], ps[:, :], modc[:, gate + n:gate + n + 1], xT[:, n, :], M, A_, [m], free=True)
        return f

    linear("wout1", 2, 4, 8, lambda k: hT[:, k, :], res1(16))
    if dump("x1", xT[:, :, :]):
        return endit()
    Q.barrier()
    with ExitStack() as ar:
        tmp = [sb(f"n2t{j}", [128, 512], F32, ar) for j in range(2)]
        rstd = sb("n2r", [128, 512], F32, ar)
        ff = sb("ff", [128, 22, 512], F32, ar)
        n = norm_stats([xT[:, k, :] for k in range(8)], 512, 1024, rstd[:, :], tmp)
        for k in range(8):
            stt(hT[:, k, :], xT[:, k, :], scl[:, 8 + k:9 + k], rstd[:, :], M, M, [n], free=k > 0)
        for k in range(8):
            hready = ts(hT[:, k, :], hT[:, k, :], modc[:, 24 + k:25 + k], A_, free=k > 0)
        cv = Slots([sb(f"fcv{j}", [128, 512], F32, ar) for j in range(3)])

        def ffn(n, ps, m):
            ci, c, f = cv.take()
            w = cc["fconv"][:, 4 * n:4 * n + 4]
            ts(c[:, :], ps[:, :], w[:, 2:3], M, w[:, 3:4], A_, w=[m] + f)
            stt(c[:, 1:512], ps[:, 0:511], w[:, 1:2], c[:, 1:512], M, A_)
            v = stt(c[:, 2:512], ps[:, 0:510], w[:, 0:1], c[:, 2:512], M, A_)
            if n % 2 == 0:
                a = act(ff[:, n // 2, :], c[:, :], ACT.Silu, [v], free=True)
                ffa[n // 2] = a
                cv.done(ci, a)
            else:
                cv.done(ci, tt(ff[:, n // 2, :], ff[:, n // 2, :], c[:, :], M, [ffa[n // 2]]))
            return v

        ffa = {}
        linear("wup", 11, 4, 8, lambda k: hT[:, k, :], ffn, [hready])
        linear("wdn", 8, 1, 22, lambda k: ff[:, k, :], res1(40), Q.last(VE))
        if dump("x2", xT[:, :, :]):
            return endit()
        Q.barrier()
    def norm_to(src, msrc, wcol, dst, mdst, ar):
        tmp = [sb(f"nt{j}{wcol}", [128, 512], F32, ar) for j in range(2)]
        rstd = sb(f"nr{wcol}", [128, 512], F32, ar)
        rst2 = sb(f"nm{wcol}", [128, 16], F32, ar)
        n = norm_stats([src[:, k, :] for k in range(8)], 512, 1024, rstd[:, :], tmp)
        if msrc is not None:
            n = norm_stats([msrc[:, k, :] for k in range(8)], 16, 1024, rst2[:, :], tmp, Q.last(PE))
            for k in range(8):
                stt(mdst[:, k, :], msrc[:, k, :], cc[wcol][:, k:k + 1], rst2[:, :], M, M, [n], free=k > 0)
        for k in range(8):
            r = stt(dst[:, k, :], src[:, k, :], cc[wcol][:, k:k + 1], rstd[:, :], M, M, [n], free=True)
        return r

    with ExitStack() as ar:
        hready = norm_to(xT, mT, "lnmix", hT, hm, ar)
        Q.barrier()

    hk = lambda k: hT[:, k, :]
    mk = lambda k: hm[:, k, :]
    mid = ctx.enter_context(ExitStack())
    mixT = sb("mixT", [128, 8, 512], F32, mid)

    with ExitStack() as ar:
        qk = sb("qk", [128, 8, 512], F32, ar)
        km = sb("km", [128, 4, 16], F32, ar)
        glo = sb("glo", [16, 528], F32, ar)
        vt = sb("vt", [128, 4, 1024], F32, ar)
        vm = sb("vm", [16, 1024], F32, ar)
        G = sb("G", [128, 4, 512], F32, ar)
        Gm = sb("Gm", [128, 4, 16], F32, ar)
        oT = sb("oT", [128, 8, 512], F32, ar)
        msk = sb("msk", [128, 1024], U32, ar)
        kmsk = Q.dma(SY, "msk", msk[:, :], D["masks"], Q.last(PE, SC, VE, GP))

        def take_qk(n, ps, m, meta):
            if meta:
                return copy(km[:, n - 4, :], ps[:, 0:16], [m]) if n >= 4 else None
            if n < 4:
                return act(qk[:, n, :], ps[:, :], ACT.Copy, [m], free=True, scale=128 ** -0.5)
            return copy(qk[:, n, :], ps[:, :], [m], free=True)

        def linear2(name, nslots, per, kt, take, first=0):
            n = 0
            for s in range(nslots):
                i, buf, t = slot(name, s)
                v = buf[:, 0:per * kt * 128].rearrange("p (a k n) -> p a k n", a=per, k=kt)
                for a in range(per):
                    if n >= first:
                        bi, ps, fr = B.take()
                        m = mm(ps[:, 0:16], [(v[:, a, k, :], mk(k)) for k in range(kt)], [t] + fr)
                        B.done(bi, take(n, ps, m, True))
                    bi, ps, fr = B.take()
                    m = mm(ps[:, :], [(v[:, a, k, :], hk(k)) for k in range(kt)], [t] + fr)
                    B.done(bi, take(n, ps, m, False))
                    n += 1
                release(i, m)

        linear2("qk2", 2, 4, 8, take_qk, 4)
        i, buf, t = slot("glow", 0)
        wg = buf[:, 0:128].rearrange("p (k n) -> p k n", k=8)
        bi, ps, fr = B.take()
        m = mm(ps[0:16, :], [(wg[:, k, :], hk(k)) for k in range(8)], [t] + fr)
        B.done(bi, copy(glo[:, 0:512], ps[0:16, :], [m]))
        bi, ps, fr = B.take()
        m = mm(ps[0:16, 0:16], [(wg[:, k, :], mk(k)) for k in range(8)], fr)
        glt = copy(glo[:, 512:528], ps[0:16, 0:16], [m])
        B.done(bi, glt)
        release(i, m)
        for h in range(4):
            bi, ps, fr = B.take()
            m = mm(ps[:, :], [(g2w[:, 128 * h:128 * h + 128], glo[:, 0:512])], [glt, k2] + fr)
            v = ts(G[:, h, :], ps[:, :], cc["bgate"][:, h:h + 1], A_, w=[m])
            B.done(bi, v)
            bi, ps, fr = B.take()
            m = mm(ps[:, 0:16], [(g2w[:, 128 * h:128 * h + 128], glo[:, 512:528])], fr)
            gz_ = ts(Gm[:, h, :], ps[:, 0:16], cc["bgate"][:, h:h + 1], A_, w=[m])
            B.done(bi, gz_)
        for s in range(2):
            i, buf, t = slot("v2", s)
            wv = buf[:, :].rearrange("p (k n) -> p k n", k=8)
            for j in range(4):
                bi, ps, fr = B.take()
                m = mm(ps[:, :], [(hT[:, k, 128 * j:128 * j + 128], wv[:, k, :]) for k in range(8)], [t] + fr)
                B.done(bi, copy(vt[:, j, 512 * s:512 * s + 512], ps[:, :], [m], eng=SC, free=True))
            bi, ps, fr = B.take()
            m = mm(ps[0:16, :], [(mk(k), wv[:, k, :]) for k in range(8)], fr)
            B.done(bi, copy(vm[:, 512 * s:512 * s + 512], ps[0:16, :], [m], eng=SC, free=True))
            release(i, m)
        with ExitStack() as a2:
            lt = sb("lt", [128, 2048], F32, a2)
            for z_, n_, first in ((G[:, :, :].rearrange("p a b -> p (a b)"), 2048, True),
                                  (Gm[:, :, :].rearrange("p a b -> p (a b)"), 64, False)):
                l_ = lt[:, 0:n_]
                act(l_, z_, ACT.Abs, [gz_] + Q.last(VE))
                act(l_, l_, ACT.Exp, scale=-1.0)
                a = act(l_, l_, ACT.Ln, bias=1.0)
                v = stt(z_, z_, 0.0, l_, ALU.min, S_, [a])
                v = ts(z_, z_, 1 / 16, M)
            for h in range(4):
                Q.add(VE, lambda e, h=h: e.tensor_tensor_scan(lt[:, 512 * h:512 * h + 512], C["notfirst"],
                                                              G[:, h, :], 0.0, M, A_), free=h > 0)
            for h in range(4):
                v = Q.add(VE, lambda e, h=h: e.tensor_tensor_scan(Gm[:, h, :], C["ones"][:, 0:16],
                                                                  Gm[:, h, :], 0.0, M, A_), free=h > 0)
            copy(G[:, :, :].rearrange("p a b -> p (a b)"), lt[:, :])
            Q.barrier()
        with ExitStack() as a2:
            names = ("eG", "eN", "qe", "qn", "ke", "kn")
            Es = {n_: [sb(f"gl_{n_}{j}", [128, 512], F32, a2) for j in range(2 if n_ in ("qe",) else 1)]
                  for n_ in names}
            kdt = sb("kdt", [128, 2, 512], F32, a2)
            att = Es["eG"][0]
            kdm = sb("kdm", [128, 16], F32, a2)
            kdmt = sb("kdmt", [16, 128], F32, a2)
            S = sb("Sg", [128, 8, 256], F32, a2)
            gl = sb("glg", [128, 8], F32, a2)
            qe0 = kn0 = None
            for h in range(4):
                Gh = G[:, h, :]
                qh, kh = qk[:, h, :], qk[:, 4 + h, :]
                E = {n_: Es[n_][0] for n_ in names}
                prev = Q.last(PE, VE)
                act(E["eG"][:, :], Gh, ACT.Exp, prev)
                a = act(E["eN"][:, :], Gh, ACT.Exp, scale=-1.0, free=True)
                tt(E["qe"][:, :], qh, E["eG"][:, :], M, [a] + prev)
                tt(E["qn"][:, :], qh, E["eN"][:, :], M, free=True)
                tt(E["ke"][:, :], kh, E["eG"][:, :], M, free=True)
                v1 = tt(E["kn"][:, :], kh, E["eN"][:, :], M, free=True)
                g3 = Gh.rearrange("p (c t) -> p c t", c=8)
                e3 = E["eG"][:, :].rearrange("p (c t) -> p c t", c=8)
                copy(gl[:, :].unsqueeze(2), e3[:, :, 63:64])
                v = tt(E["eN"][:, :].rearrange("p (c t) -> p c t", c=8), g3[:, :, 63:64].to_broadcast([128, 8, 64]),
                       g3, S_)
                a = act(E["eN"][:, :], E["eN"][:, :], ACT.Exp, [v])
                v = tt(E["eN"][:, :], E["eN"][:, :], kh, M, [a])
                vmt = ts(kdm[:, :], Gm[:, h, :], Gm[:, h, 15:16], S_, -1.0, M)
                a = act(kdm[:, :], kdm[:, :], ACT.Exp, [vmt])
                vmt = tt(kdm[:, :], kdm[:, :], km[:, h, :], M, [a])
                bi, ps, fr = B.take()
                m = tr(ps[0:16, 0:128], kdm[:, :], [vmt] + fr)
                c_ = copy(kdmt[:, :], ps[0:16, 0:128], [m])
                B.done(bi, c_)
                bi, ps, fr = B.take()
                m = mm(ps[:, 0:256], [(kdmt[:, :], vm[:, 256 * h:256 * h + 256])], [c_] + fr)
                B.done(bi, copy(S[:, 0, :], ps[:, 0:256], [m]))
                bi, ps, fr = B.take()
                for j in range(4):
                    m = tr(ps[:, 128 * j:128 * j + 128], E["eN"][:, 128 * j:128 * j + 128],
                           ([v] + fr) if j == 0 else ())
                ts(kdt[:, 0, :], ps[:, :], C["col01"][:, 0:1], M, w=[m])
                v = ts(kdt[:, 1, :], ps[:, :], C["col01"][:, 1:2], M, free=True)
                B.done(bi, v)
                b1, p1, f1 = B.take()
                b2, p2, f2 = B.take()
                for j in range(4):
                    c = slice(128 * j, 128 * j + 128)
                    mm(p1[:, c], [(E["kn"][:, c], E["qe"][:, c])], [v1] + f1, start=j == 0, check=False)
                    m = mm(p2[:, c], [(E["ke"][:, c], E["qn"][:, c])], f2, start=j == 0, check=False)
                Q.add(VE, lambda e: e.memset(att[:, :], 0.0))
                Q.add(VE, lambda e, p1=p1: e.copy_predicated(att[:, :], msk[:, 0:512], p1[:, :]), [m, kmsk])
                va = Q.add(VE, lambda e, p2=p2: e.copy_predicated(att[:, :], msk[:, 512:1024], p2[:, :]))
                B.done(b1, va)
                B.done(b2, va)
                for c2 in range(4):
                    bi, ps, fr = B.take()
                    for c in range(2 * c2, min(2 * c2 + 2, 7)):
                        m = mm(ps[:, 256 * (c % 2):256 * (c % 2) + 256],
                               [(kdt[:, c % 2, 128 * c2:128 * c2 + 128], vt[:, c2, 256 * h:256 * h + 256])],
                               [v] + fr, start=c % 2 == 0, check=False)
                    for c in range(2 * c2, min(2 * c2 + 2, 7)):
                        vs = stt(S[:, c + 1, :], S[:, c, :], gl[:, c:c + 1], ps[:, 256 * (c % 2):256 * (c % 2) + 256],
                                 M, A_, [m])
                    B.done(bi, vs)
                for dv in range(2):
                    bi, ps, fr = B.take()
                    for j in range(4):
                        m = mm(ps[:, 128 * j:128 * j + 128],
                               [(vt[:, j, 256 * h + 128 * dv:256 * h + 128 * dv + 128],
                                 att[:, 128 * j:128 * j + 128])], [va] + fr, start=j == 0, stop=False, check=False)
                    for c in range(8):
                        m = mm(ps[:, 64 * c:64 * c + 64], [(S[:, c, 128 * dv:128 * dv + 128],
                                                            E["qe"][:, 64 * c:64 * c + 64])], [vs],
                               start=False, check=False)
                    B.done(bi, copy(oT[:, 2 * h + dv, :], ps[:, :], [m], eng=SC))
            Q.barrier()
        with ExitStack() as a2:
            sq = Slots([sb(f"osq{j}", [128, 512], F32, a2) for j in range(2)])
            rr = [sb(f"orr{j}", [128, 512], F32, a2) for j in range(2)]
            sg = Slots([sb(f"osg{j}", [128, 512], F32, a2) for j in range(2)])
            for h in range(4):
                bi, ps, fr = B.take()
                for dv in range(2):
                    si, s, f = sq.take()
                    a = act(s[:, :], oT[:, 2 * h + dv, :], ACT.Square, f, free=True)
                    m = mm(ps[:, :], [(C["ones"], s[:, :])], [a] + fr, start=dv == 0, stop=dv == 1)
                    sq.done(si, m)
                r = rr[h % 2]
                ts(r[:, :], ps[:, :], 1 / 256, M, EPS, A_, w=[m])
                v = recip(r[:, :], r[:, :])
                B.done(bi, v)
                a = act(r[:, :], r[:, :], ACT.Sqrt, [v])
                for dv in range(2):
                    o_ = oT[:, 2 * h + dv, :]
                    stt(o_, o_, cc["glan"][:, dv:dv + 1], r[:, :], M, M, [a], free=dv > 0)

            def take_g(n, ps, m):
                si, s, f = sg.take()
                a = act(s[:, :], ps[:, :], ACT.Silu, [m] + f, free=True)
                sg.done(si, tt(oT[:, n, :], oT[:, n, :], s[:, :], M, [a]))
                return a

            linear("gout2", 2, 4, 8, hk, take_g)
            linear("gatea", 2, 4, 8, hk, lambda n, ps, m: act(mixT[:, n, :], ps[:, :], ACT.Sigmoid, [m], free=True))
            if dump("oT", oT[:, :, :]):
                return endit()
            linear("upgla", 2, 4, 8, lambda k: oT[:, k, :],
                   lambda n, ps, m: tt(mixT[:, n, :], mixT[:, n, :], ps[:, :], M, [m] + Q.last(SC)), Q.last(VE))
            Q.barrier()
    if dump("yaT", mixT[:, :, :]):
        return endit()

    with ExitStack() as ar:
        yT = sb("yT", [128, 16, 512], F32, ar)
        with ExitStack() as a2:
            dtt = sb("dtt", [128, 5, 32], F32, a2)
            av = sb("av", [128, 5, 32], F32, a2)
            ac = sb("ac", [128, 5, 32], F32, a2)
            dtx = sb("dtx", [128, 5, 32], F32, a2)
            te = sb("te", [128, 9, 32], F32, a2)
            al2 = sb("al2", [128, 4, 64], F32, a2)
            eal = sb("eal", [128, 8, 32], F32, a2)
            eac = sb("eac", [128, 4, 32], F32, a2)
            i, buf, t = slot("dt2", 0)
            wd = buf[:, 0:256].rearrange("p (k n) -> p k n", k=8)
            z0 = Q.add(VE, lambda e: e.memset(dtt[:, 4, :], 0.0))
            z0 = Q.add(VE, lambda e: e.memset(av[:, 4, :], 0.0))
            bi, ps, fr = B.take()
            for j in range(5):
                o_ = ps[:, 32 * j:32 * j + 32] if j < 4 else ps[0:16, 128:160]
                l_ = (lambda k: hT[:, k, 128 * j:128 * j + 128]) if j < 4 else mk
                for k in range(8):
                    m = mm(o_, [(l_(k), wd[:, k, :])], [t] + fr, start=k == 0 and j == 0, stop=k == 7, check=False)
            release(i, m)
            v = tt(dtt[:, 0:4, :], ps[:, 0:128].rearrange("p (a b) -> p a b", a=4), rep(cc["dtb2"], 4), A_, [m])
            v = tt(dtt[0:16, 4, :], ps[0:16, 128:160], cc["dtb2"][0:16, :], A_)
            B.done(bi, v)
            act(dtx[:, :, :], dtt[:, :, :], ACT.Abs, [v])
            act(dtx[:, :, :], dtx[:, :, :], ACT.Exp, scale=-1.0)
            a = act(dtx[:, :, :], dtx[:, :, :], ACT.Ln, bias=1.0)
            a = act(eac[:, 0, :], cc["alog2"], ACT.Exp)
            stt(dtt[:, :, :], dtt[:, :, :], 0.0, dtx[:, :, :], ALU.max, A_, [a])
            ts(eac[:, 1, :], eac[:, 0, :], -1.0, M)
            tt(av[:, 0:4, :], dtt[:, 0:4, :], rep(eac[:, 1, :], 4), M)
            tt(av[0:16, 4, :], dtt[0:16, 4, :], eac[0:16, 1, :], M)
            ts(al2[:, :, 0:32], av[:, 0:4, :], C["col01"][:, 0:1], M, free=False)
            v = ts(al2[:, :, 32:64], av[:, 0:4, :], C["col01"][:, 1:2], M)
            bi, ps, fr = B.take()
            avf = av[:, :, :].rearrange("p a b -> p (a b)")
            m = mm(ps[:, 0:160], [(C["cum64"], avf)], [v] + fr, check=False)
            m = mm(ps[:, 160:320], [(C["same64"], avf)], check=False, start=False)
            v = copy(ac[:, :, :].rearrange("p a b -> p (a b)"), ps[:, 0:160], [m])
            v = tt(dtx[:, :, :].rearrange("p a b -> p (a b)"), ps[:, 160:320],
                   ac[:, :, :].rearrange("p a b -> p (a b)"), S_)
            B.done(bi, v)
            act(dtx[:, :, :], dtx[:, :, :], ACT.Exp, [v])
            a = act(eac[:, :, :], ac[:, 0:4, :], ACT.Exp)
            tt(dtx[:, :, :], dtx[:, :, :], dtt[:, :, :], M, [a])
            t8 = te[:, 0:8, :].rearrange("p (m c) h -> p m c h", c=2)
            ts(t8[:, :, 0, :], dtx[:, 0:4, :], C["col01"][:, 0:1], M)
            ts(t8[:, :, 1, :], dtx[:, 0:4, :], C["col01"][:, 1:2], M)
            v = copy(te[:, 8, :], dtx[:, 4, :])
            bi, ps, fr = B.take()
            m = mm(ps[:, 0:256], [(C["ones"], al2[:, :, :].rearrange("p a b -> p (a b)"))], fr)
            a = act(eal[:, :, :].rearrange("p a b -> p (a b)"), ps[:, 0:256], ACT.Exp, [m])
            B.done(bi, a)

            raw = Slots([sb(f"raw{j}", [128, 532], F32, a2) for j in range(2)])
            for r in raw.bufs:
                rz = Q.add(VE, lambda e, r=r: e.memset(r[:, 0:3], 0.0))
            cvo = Slots([sb(f"cvo{j}", [128, 528], F32, a2) for j in range(2)])
            xsg = sb("xsg", [128, 5, 512], F32, a2)
            BT_ = sb("BTg", [128, 528], F32, a2)
            CT_ = sb("CTg", [128, 528], F32, a2)
            CTm = sb("CTm", [128, 2, 512], F32, a2)
            Bt = sb("Bt", [128, 5, 128], F32, a2)
            cb = sb("cb", [128, 4, 128], F32, a2)
            yz = sb("yz", [128, 4, 512], F32, a2)
            SS = Slots([sb(f"SS{j}", [128, 512], F32, a2) for j in range(2)])
            xd = sb("xd", [128, 512], F32, a2)
            xe = Slots([sb(f"xe{j}", [128, 512], F32, a2) for j in range(2)])
            sg = sb("sgm", [128, 8, 128], F32, a2)
            zt = sb("zt", [128, 512], F32, a2)
            yt = sb("yt", [128, 512], F32, a2)
            y2 = zt
            ms = sb("ms", [128, 4], F32, a2)

            def b8(ap, n=64):
                return bc(ap, n)

            cz = Q.add(VE, lambda e: e.memset(CTm[:, :, :], 0.0))
            for g in range(4):
                hs = slice(8 * g, 8 * g + 8)

                def conv_out(tile_no, dst):
                    st8 = {}

                    def take(n, ps, m, meta):
                        if meta:
                            ri, r, f = raw.take()
                            st8["r"] = (ri, r)
                            return copy(r[:, 3:19], ps[:, 0:16], [m, rz] + f, eng=SC, free=True)
                        ri, r = st8["r"]
                        a = copy(r[:, 19:531], ps[:, :], [m], eng=SC, free=True)
                        tn = tile_no(n)
                        w = cc["conv2"][:, 5 * tn:5 * tn + 5]
                        o_, dn = dst(n)
                        ts(o_[:, 0:528], r[:, 3:531], w[:, 3:4], M, w[:, 4:5], A_, w=[a] + dn)
                        for d in (1, 2, 3):
                            v = stt(o_[:, 0:528], r[:, 3 - d:531 - d], w[:, 3 - d:4 - d], o_[:, 0:528], M, A_)
                        raw.done(ri, v)
                        act(o_[:, 0:528], o_[:, 0:528], ACT.Silu, [v], free=True)
                        return a
                    return take

                cur = {}

                def xs_dst(n):
                    ci, c, f = cvo.take()
                    cur["c"] = (ci, c)
                    return c, f

                base = conv_out(lambda n: 4 * g + n, xs_dst)

                def xs_take(n, ps, m, meta):
                    r = base(n, ps, m, meta)
                    if meta:
                        return r
                    ci, c = cur["c"]
                    sil = Q.last(SC)
                    bi, pt, fr = B.take()
                    for j in range(4):
                        mt_ = tr(pt[:, 128 * j:128 * j + 128], c[:, 16 + 128 * j:144 + 128 * j],
                                 (sil + fr) if j == 0 else ())
                    v = copy(xsg[:, 0:4, 128 * n:128 * n + 128], pt[:, :].rearrange("p (a b) -> p a b", a=4),
                             [mt_] + gprev)
                    B.done(bi, v)
                    bi, pt, fr = B.take()
                    mt_ = tr(pt[0:16, 0:128], c[:, 0:16], fr)
                    v = copy(xsg[0:16, 4, 128 * n:128 * n + 128], pt[0:16, 0:128], [mt_])
                    B.done(bi, v)
                    cvo.done(ci, mt_)
                    return r

                gprev = Q.last(PE, VE, GP)
                linear2("xs2", 1, 4, 8, xs_take) if False else None
                for name, nm, per, take in (
                        ("xs2", g, 4, xs_take),
                        ("bc2", g, 2, conv_out(lambda n: (16 if n == 0 else 20) + g,
                                               lambda n: (BT_ if n == 0 else CT_, gprev)))):
                    i, buf, t = slot(name, nm)
                    v_ = buf[:, 0:per * 1024].rearrange("p (a k n) -> p a k n", a=per, k=8)
                    for a_ in range(per):
                        bi, ps, fr = B.take()
                        m = mm(ps[:, 0:16], [(v_[:, a_, k, :], mk(k)) for k in range(8)], [t] + fr)
                        B.done(bi, take(a_, ps, m, True))
                        bi, ps, fr = B.take()
                        m = mm(ps[:, :], [(v_[:, a_, k, :], hk(k)) for k in range(8)], [t] + fr)
                        if a_ == per - 1:
                            release(i, m)
                        B.done(bi, take(a_, ps, m, False))
                sil = Q.last(SC)
                for q_ in range(2):
                    half = lambda ap: ap.rearrange("p (m c t) -> p m c t", m=4, c=2)[:, :, q_, :]
                    vct = copy(half(CTm[:, q_, :]), half(CT_[:, 16:528]), sil + gprev + [cz])
                bi, ps, fr = B.take()
                for j in range(4):
                    m = tr(ps[:, 128 * j:128 * j + 128], BT_[:, 16 + 128 * j:144 + 128 * j], (sil + fr) if j == 0 else ())
                v = copy(Bt[:, 0:4, :], ps[:, :].rearrange("p (a b) -> p a b", a=4), [m])
                B.done(bi, v)
                bi, ps, fr = B.take()
                m = tr(ps[0:16, 0:128], BT_[:, 0:16], fr)
                v = copy(Bt[0:16, 4, :], ps[0:16, 0:128], [m])
                B.done(bi, v)
                bi, ps, fr = B.take()
                for j in range(4):
                    c = slice(16 + 128 * j, 144 + 128 * j)
                    m = mm(ps[:, 128 * j:128 * j + 128], [(BT_[:, c], CT_[:, c])], fr, start=j == 0, check=False)
                v = tt(cb[:, :, :], ps[:, :].rearrange("p (a b) -> p a b", a=4), rep(C["same64"], 4), M, [m])
                B.done(bi, v)
                x3 = lambda ap: ap.rearrange("p (h d) -> p h d", h=8)
                xi, x_, f = xe.take()
                v = tt(x3(x_[0:16, :]), x3(xsg[0:16, 4, :]), b8(te[0:16, 8, hs]), M, f)
                bi, ps, fr = B.take()
                m = mm(ps[:, :], [(Bt[0:16, 4, :], x_[0:16, :])], [v] + fr)
                xe.done(xi, m)
                s0i, s0, f = SS.take()
                vS = copy(s0[:, :], ps[:, :], [m] + f)
                B.done(bi, vS)
                iz, bz, tz = slot("z2", g)
                wz = bz[:, :].rearrange("p (k n) -> p k n", k=8)
                for j in range(4):
                    zb, pz, fr = B.take()
                    mz = mm(pz[:, :], [(hT[:, k, 128 * j:128 * j + 128], wz[:, k, :]) for k in range(8)], [tz] + fr)
                    va = []
                    for q4 in range(2):
                        bi, ps, fr = B.take()
                        for h in range(4):
                            hh = 8 * g + 4 * q4 + h
                            m = mm(ps[:, 128 * h:128 * h + 128],
                                   [(av[:, j, hh:hh + 1].to_broadcast([128, 128]), C["cum64"])], fr,
                                   start=h == 0, check=False)
                        v = tt(sg[:, 4 * q4:4 * q4 + 4, :], ps[:, :].rearrange("p (a b) -> p a b", a=4),
                               bc(ac[:, j, 8 * g + 4 * q4:8 * g + 4 * q4 + 4], 128), S_,
                               [m] + (Q.last(PE) if q4 == 0 else []))
                        B.done(bi, v)
                    act(sg[:, :, :], sg[:, :, :], ACT.Abs, [v])
                    a = act(sg[:, :, :], sg[:, :, :], ACT.Exp, scale=-1.0)
                    v = tt(sg[:, :, :], sg[:, :, :], rep(cb[:, j, :], 8), M, [a])
                    v = tt(x3(xd[:, :]), x3(xsg[:, j, :]), b8(dtt[:, j, hs]), M)
                    yb, py, fr = B.take()
                    for h in range(8):
                        m = mm(py[:, 64 * h:64 * h + 64], [(sg[:, h, :], xd[:, 64 * h:64 * h + 64])], [v] + fr,
                               start=h == 0, check=False)
                    my = m
                    ib, pi_, fr2 = B.take()
                    for cpar in range(2):
                        c = 2 * j + cpar
                        m = mm(pi_[:, :], [(CTm[:, cpar, 128 * j:128 * j + 128], s0[:, :])], [vS, vct] + fr2,
                               start=cpar == 0, stop=cpar == 1)
                        SS.done(s0i, m)
                        if c < 7:
                            xi, x_, f = xe.take()
                            v = tt(x3(x_[:, :]), x3(xsg[:, j, :]), b8(te[:, c, hs]), M, f)
                            bi, ps, fr = B.take()
                            m2 = mm(ps[:, :], [(Bt[:, j, :], x_[:, :])], [v] + fr)
                            xe.done(xi, m2)
                            s1i, s1, f = SS.take()
                            tt(x3(s1[:, :]), x3(s0[:, :]), b8(eal[:, c, hs]), M, f)
                            vS = tt(s1[:, :], s1[:, :], ps[:, :], A_, [m2])
                            B.done(bi, vS)
                            SS.done(s0i, vS)
                            s0i, s0 = s1i, s1
                    v = tt(x3(yt[:, :]), x3(pi_[:, :]), b8(eac[:, j, hs]), M, [m])
                    B.done(ib, v)
                    v = tt(yt[:, :], yt[:, :], py[:, :], A_, [my])
                    B.done(yb, v)
                    tt(x3(y2[:, :]), x3(xsg[:, j, :]), b8(cc["dsk"][:, hs]), M)
                    v = tt(yt[:, :], yt[:, :], y2[:, :], A_)
                    a = act(zt[:, :], pz[:, :], ACT.Silu, [mz] + Q.last(VE))
                    B.done(zb, a)
                    v = tt(yz[:, j, :], yt[:, :], zt[:, :], M, [a])
                    a = act(zt[:, :], yz[:, j, :], ACT.Square, [v], accum_out=ms[:, 0:1])
                    ts(ms[:, 1:2], ms[:, 0:1], 1 / 512, M, EPS, A_, w=[a])
                    v = recip(ms[:, 2:3], ms[:, 1:2])
                    a = act(ms[:, 3:4], ms[:, 2:3], ACT.Sqrt, [v])
                    v = ts(yz[:, j, :], yz[:, j, :], ms[:, 3:4], M, w=[a])
                release(iz, mz)
                for n_ in range(4):
                    bi, ps, fr = B.take()
                    for j in range(4):
                        m = tr(ps[:, 128 * j:128 * j + 128], yz[:, j, 128 * n_:128 * n_ + 128],
                               ([v] + fr) if j == 0 else ())
                    B.done(bi, act(yT[:, 4 * g + n_, :], ps[:, :], ACT.Copy, [m], free=True,
                                   scale=cc["ssdn"][:, 4 * g + n_:4 * g + n_ + 1]))
            Q.barrier()
        if dump("yn", yT[:, :, :]):
            return endit()
        with ExitStack() as a2:
            gb = sb("gb", [128, 8, 512], F32, a2)
            linear("gateb", 2, 4, 8, hk, lambda n, ps, m: act(gb[:, n, :], ps[:, :], ACT.Sigmoid, [m], free=True))

            def take_y(n, ps, m):
                v = tt(gb[:, n, :], gb[:, n, :], ps[:, :], M, [m] + Q.last(SC))
                tt(mixT[:, n, :], mixT[:, n, :], gb[:, n, :], A_)
                return v

            linear("upssd", 4, 2, 16, lambda k: yT[:, k, :], take_y)
            if dump("mixed2", mixT[:, :, :]):
                return endit()
            linear("wout2", 2, 4, 8, lambda k: mixT[:, k, :],
                   lambda n, ps, m: tt(xT[:, n, :], xT[:, n, :], ps[:, :], A_, [m], free=True), Q.last(VE))
            Q.barrier()
    mid.close()
    if dump("x3", xT[:, :, :]):
        return endit()
    with ExitStack() as ar:
        hready = norm_to(xT, None, "lnffn", hT, None, ar)
        Q.barrier()

    ijw = sb("ijw", [128, 3, 512])
    with ExitStack() as ar:
        qT = sb("pqT", [128, 16, 512], F32, ar)
        linear("wq", 4, 4, 8, hk, lambda n, ps, m: copy(qT[:, n, :], ps[:, :], [m], eng=SC, free=True))
        i, buf, t = slot("subk", 0)
        sk = buf[:, 0:2048].rearrange("p (a n) -> p a n", a=16)
        s_ = sb("s_", [128, 16, 128], F32, ar)
        s2 = sb("s2", [128, 16, 128], F32, ar)
        top = sb("top", [128, 16, 16], F32, ar)
        tix = sb("tix", [128, 16, 16], U32, ar)
        tif = sb("tif", [128, 16, 16], F32, ar)
        cand = sb("cand", [128, 8, 256], F32, ar)
        cnd2 = s_
        best = sb("best", [128, 8, 16], F32, ar)
        pix = sb("pix", [128, 8, 16], U32, ar)
        pa = sb("pa", [128, 8, 16], U32, ar)
        paf = sb("paf", [128, 2, 128], F32, ar)
        eq = sb("eq", [128, 8, 256], F32, ar)
        sel = sb("sel", [128, 3, 128], F32, ar)
        red8 = sb("red8", [128, 2, 8], F32, ar)

        def top16(vals, idx, src, scratch, n):
            Q.add(VE, lambda e: e.max(vals[:, 0:8], src))
            Q.add(VE, lambda e: e.max_index(idx[:, 0:8], vals[:, 0:8], src))
            Q.add(VE, lambda e: e.match_replace(scratch, vals[:, 0:8], src, -3e38), free=True)
            Q.add(VE, lambda e: e.max(vals[:, 8:16], scratch))
            Q.add(VE, lambda e: e.max_index(idx[:, 8:16], vals[:, 8:16], scratch))

        for j in range(4):
            for q4 in range(4):
                bi, ps, fr = B.take()
                for a_ in range(4):
                    n_ = 4 * q4 + a_
                    m = mm(ps[:, 128 * a_:128 * a_ + 128], [(qT[:, n_, 128 * j:128 * j + 128], sk[:, n_, :])],
                           [t] + Q.last(SC) + fr, start=a_ == 0, check=False)
                B.done(bi, copy(s_[:, 4 * q4:4 * q4 + 4, :], ps[:, :].rearrange("p (a b) -> p a b", a=4), [m]))
            if j == 3:
                release(i, m)
            for n_ in range(16):
                top16(top[:, n_, :], tix[:, n_, :], s_[:, n_, :], s2[:, n_, :], 128)
            copy(tif[:, :, :], tix[:, :, :])
            t4 = top[:, :, :].rearrange("p (h i) k -> p h i k", i=2)
            f4 = tif[:, :, :].rearrange("p (h i) k -> p h i k", i=2)
            for h in range(8):
                tt(cand[:, h, :].rearrange("p (a b) -> p a b", a=16), bc(top[:, 2 * h, :], 16),
                   rep(top[:, 2 * h + 1, :], 16), A_, free=h > 0)
            cn = s2[:, :, :].rearrange("p (h x) k -> p h (x k)", h=8)
            for h in range(8):
                top16(best[:, h, :], pix[:, h, :], cand[:, h, :], cn[:, h, :], 256)
            ts(pa[:, :, :], pix[:, :, :], 4, ALU.logical_shift_right)
            copy(paf[:, 0, :], pa[:, :, :].rearrange("p a b -> p (a b)"))
            ts(pa[:, :, :], pix[:, :, :], 15, ALU.bitwise_and)
            copy(paf[:, 1, :], pa[:, :, :].rearrange("p a b -> p (a b)"))
            for c in range(2):
                for h in range(8):
                    e3 = eq[:, h, :].rearrange("p (k a) -> p k a", k=16)
                    tt(e3, bc(paf[:, c, 16 * h:16 * h + 16], 16), rep(C["iota"][:, 0:16], 16), ALU.is_equal,
                       free=h > 0)
                for h in range(8):
                    e3 = eq[:, h, :].rearrange("p (k a) -> p k a", k=16)
                    tt(e3, e3, rep(tif[:, 2 * h + c, :], 16), M, free=h > 0)
                red(sel[:, c, :], eq[:, :, :].rearrange("p h (k a) -> p (h k) a", a=16), A_,
                    w=Q.last(PE) if c == 0 else ())
            w3 = sel[:, 2, :].rearrange("p (h k) -> p h k", h=8)
            v = tt(w3, best[:, :, :], best[:, :, 0:1].to_broadcast([128, 8, 16]), S_)
            a = act(w3, w3, ACT.Exp, [v])
            red(red8[:, 0, :], w3, A_, w=[a])
            recip(red8[:, 1, :], red8[:, 0, :])
            v = tt(w3, w3, bc(red8[:, 1, :], 16), M)
            bi, ps, fr = B.take()
            for c in range(3):
                m = tr(ps[:, 128 * c:128 * c + 128], sel[:, c, :], ([v] + fr) if c == 0 else ())
            v = copy(ijw[:, :, 128 * j:128 * j + 128], ps[:, 0:384].rearrange("p (a b) -> p a b", a=3), [m])
            B.done(bi, v)
        Q.barrier()
    if dump("wT", ijw[:, :, :]):
        return endit()

    with ExitStack() as ar:
        W = sb("W", [128, 512, 44], F32, ar)
        A8 = Slots([sb(f"A8{j}", [128, 128], F32, ar) for j in range(4)])
        B8 = Slots([sb(f"B8{j}", [128, 44], F32, ar) for j in range(4)])
        gg = Slots([sb(f"gg{j}", [128, 512], F32, ar) for j in range(2)])
        Pp = Slots([sb(f"Pp{j}", [128, 512], F32, ar) for j in range(4)])
        j0 = 0
        for nj in (44, 42, 42):
            Wv = W[:, :, :].rearrange("p t j -> p (t j)")
            per = 8
            for t0 in range(0, 512, per):
                bi, ps, fr = B.take()
                for x in range(per):
                    tok = t0 + x
                    ai, a_, f = A8.take()
                    va = ts(a_[:, :], C["iota"], ijw[:, 0, tok:tok + 1], ALU.is_equal,
                            ijw[:, 2, tok:tok + 1], M, w=f, free=True)
                    bi8, b_, f = B8.take()
                    vb_ = ts(b_[:, 0:nj], C["iota"][:, j0:j0 + nj], ijw[:, 1, tok:tok + 1], ALU.is_equal,
                             w=f, free=True)
                    m = mm(ps[:, nj * x:nj * x + nj], [(a_[:, :], b_[:, 0:nj])], [va, vb_] + fr,
                           start=x == 0, check=False)
                    A8.done(ai, m)
                    B8.done(bi8, m)
                vw = act(W[:, t0:t0 + per, 0:nj], ps[:, 0:per * nj].rearrange("p (t j) -> p t j", t=per), ACT.Copy,
                         [m] + Q.last(VE), free=True)
                B.done(bi, vw)
            for s in range(nj // 2):
                i, buf, t = slot("uv", (j0 + 2 * s) // 2)
                pps = []
                for x in range(2):
                    jj = 2 * s + x
                    u_ = buf[:, 2048 * x:2048 * x + 1024].rearrange("p (k n) -> p k n", k=8)
                    bi, ps, fr = B.take()
                    m = mm(ps[:, :], [(u_[:, k, :], hT[:, k, :]) for k in range(8)], [t] + fr)
                    gi, g_, f = gg.take()
                    a = act(g_[:, :], ps[:, :], ACT.Gelu_apprx_tanh, [m] + f, free=True)
                    B.done(bi, a)
                    pi, p_, f = Pp.take()
                    v = tt(p_[:, :], g_[:, :], W[:, :, jj], M, [a, vw] + f, free=True)
                    gg.done(gi, v)
                    pps.append((pi, p_, v))
                pend = (i, buf, pps)

                def second(pend):
                    i, buf, pps = pend
                    for d in range(8):
                        bi, ps, fr = B.take()
                        m = mm(ps[:, :], [(buf[:, 2048 * x + 1024 + 128 * d:2048 * x + 1152 + 128 * d], pps[x][1][:, :])
                                          for x in range(2)], [pps[0][2], pps[1][2]] + fr)
                        B.done(bi, tt(xT[:, d, :], xT[:, d, :], ps[:, :], A_, [m]))
                    for pi, _, _ in pps:
                        Pp.done(pi, m)
                    release(i, m)

                if s > 0:
                    second(prev)
                prev = pend
            second(prev)
            j0 += nj
        Q.barrier()
    with ExitStack() as ar:
        norm_to(xT, None, "lnfin", hT, None, ar)
        Q.dma(SY, "out", D["out"], hT[:, :, :], Q.last(VE))
        Q.q[SY].append((None, [("out", 16)], None))
    finish()




def _layout(I):
    import numpy as np
    f = {k: np.asarray(v) for k, v in I.items()}
    g = {k: (v[0] if v.shape[0] == 1 else v) for k, v in f.items()}

    def fm(W, per):
        K, N = W.shape
        a = W.reshape(K // 128, 128, N // 128 // per, per, 128)
        return np.ascontiguousarray(a.transpose(2, 1, 3, 0, 4)).reshape(N // 128 // per, 128, -1)

    def tmj(W, n):
        K, N = W.shape
        a = W.reshape(K // 128, 128, N // n, n)
        return np.ascontiguousarray(a.transpose(2, 1, 0, 3)).reshape(N // n, 128, -1)

    def col(v):
        return np.ascontiguousarray(v.reshape(-1, 128).T)

    def row(v):
        return np.ascontiguousarray(np.broadcast_to(v.reshape(1, -1), (128, v.size)))

    o = {}
    w = g["w_in"]
    o["ada"] = tmj(g["ada_w"], 512)
    o["win1"] = fm(np.concatenate([w[:, 0:2048], w[:, 2056:2568], w[:, 2568:2696], w[:, 2696:2824],
                                   w[:, 2824:2952], w[:, 3080:3208]], axis=1), 4)
    o["win1t"] = tmj(np.concatenate([w[:, 2952:3080], w[:, 3208:3336], w[:, 2048:2056], w[:, 3336:3348]], axis=1), 276)
    o["cmpw1"] = np.stack([g[n].reshape(32, 128, 128).transpose(1, 0, 2).reshape(128, 4096)
                           for n in ("cmp_k_w1", "cmp_v_w1")])
    o["cmpw2"] = np.concatenate([g["cmp_k_w2"], g["cmp_v_w2"]], axis=1)[None]
    o["wout1"] = fm(g["w_out"], 4)
    up = g["ffn_w_up"].reshape(1024, 2, 22, 128).transpose(0, 2, 1, 3).reshape(1024, 5632)
    o["wup"] = fm(up, 4)
    o["wdn"] = fm(g["ffn_w_down"], 1)
    w = g["w_in_2"]
    o["qk2"] = fm(w[:, 0:1024], 4)
    o["v2"] = tmj(w[:, 1024:2048], 512)
    o["gout2"] = fm(w[:, 2048:3072], 4)
    o["glow"] = tmj(w[:, 3072:3088], 16)
    z, xbc = w[:, 3088:5136], w[:, 5136:8208]
    o["z2"] = tmj(z, 512)
    o["xs2"] = fm(xbc[:, 0:2048], 4)
    bcw = np.stack([xbc[:, 2048:2560].reshape(1024, 4, 128), xbc[:, 2560:3072].reshape(1024, 4, 128)], axis=2)
    o["bc2"] = fm(bcw.reshape(1024, 1024), 2)
    o["dt2"] = tmj(w[:, 8208:8240], 32)
    o["gatea"] = fm(w[:, 8240:9264], 4)
    o["gateb"] = fm(w[:, 9264:10288], 4)
    o["upgla"] = fm(g["w_up_gla_2"], 4)
    o["upssd"] = fm(g["w_up_ssd_2"], 2)
    o["wout2"] = fm(g["w_out_2"], 4)
    o["wq"] = fm(g["peer_w_q_2"], 4)
    o["subk"] = np.ascontiguousarray(g["peer_sub_keys_2"].reshape(16, 128, 128).transpose(2, 0, 1)).reshape(1, 128, 2048)
    u = g["peer_u_2"].reshape(128, 128, 8, 128).transpose(1, 3, 2, 0)
    v = g["peer_v_2"].reshape(128, 128, 1024).transpose(1, 0, 2)
    uv = np.concatenate([u.reshape(128, 128, 1024), v], axis=2)
    o["uv"] = np.ascontiguousarray(uv.reshape(64, 2, 128, 2048).transpose(0, 2, 1, 3)).reshape(64, 128, 4096)
    o["gate2w"] = g["gla_w_gate2_2"]
    o["xT"] = np.ascontiguousarray(g["x"].reshape(512, 8, 128).transpose(2, 1, 0))
    o["metaT"] = np.ascontiguousarray(f["meta_tokens_2"].reshape(16, 8, 128).transpose(2, 1, 0))
    parts = [("c", col(g["c"])), ("adab", col(g["ada_b"])), ("norm1", col(g["norm1_w"])),
             ("norm2", col(g["norm2_w"])),
             ("conv1", g["gdn_conv_w"].reshape(4, 12, 128).transpose(2, 1, 0).reshape(128, 48)),
             ("qn", col(g["nsa_q_norm_w"])), ("kslc", col(g["nsa_k_norm_slc"])),
             ("kwin", col(g["nsa_k_norm_win"])), ("kcmpn", col(g["nsa_k_norm_cmp"])),
             ("kpos", g["cmp_k_pos"].T), ("vpos", g["cmp_v_pos"].T),
             ("alog", row(g["gdn_A_log"])), ("dtb1", row(g["gdn_dt_bias"])), ("gdnn", col(g["gdn_out_norm_w"])),
             ("fconv", np.concatenate([g["ffn_conv_w"], g["ffn_conv_b"][None]], 0).reshape(4, 2, 22, 128)
              .transpose(3, 2, 1, 0).reshape(128, 176)),
             ("lnmix", col(g["ln_mix_w_2"])), ("lnffn", col(g["ln_ffn_w_2"])), ("lnfin", col(f["ln_final_w_2"])),
             ("bgate", col(g["gla_b_gate_2"])), ("glan", col(g["gla_norm_w_2"])), ("ssdn", col(g["ssd_norm_w_2"])),
             ("dtb2", row(g["ssd_dt_bias_2"])), ("alog2", row(g["ssd_a_log_2"])), ("dsk", row(g["ssd_d_2"])),
             ("conv2", np.concatenate([g["ssd_conv_w_2"], g["ssd_conv_b_2"][None]], 0).reshape(5, 24, 128)
              .transpose(2, 1, 0).reshape(128, 120))]
    COLS.clear()
    off = 0
    for name, a in parts:
        COLS[name] = (off, a.shape[1])
        off += a.shape[1]
    o["cols"] = np.ascontiguousarray(np.concatenate([a for _, a in parts], axis=1))
    o["consts"] = const_array()
    o["masks"] = mask_array()
    return {k: np.ascontiguousarray(v) for k, v in o.items()}


COLS = {}


def kernel(**inputs):
    import numpy as _np
    import concourse.bacc as _bacc
    from concourse import mybir as _mybir
    from concourse.bass_utils import run_bass_kernel_spmd as _run

    arrays = _layout(inputs)
    nc = _bacc.Bacc("TRN2", target_bir_lowering=False, num_devices=1)
    D = {}
    for name, a in arrays.items():
        D[name] = nc.dram_tensor("in_" + name, a.shape, _mybir.dt.from_np(a.dtype), kind="ExternalInput").ap()
    D["out"] = nc.dram_tensor("out_0", (128, 8, 512), _mybir.dt.float32, kind="ExternalOutput").ap()
    if DBG is not None:
        D["dbg"] = nc.dram_tensor("dbg", (128, 8192), _mybir.dt.float32, kind="ExternalOutput").ap()
    build(nc, D, None)
    r = _run(nc, [{"in_" + k: v for k, v in arrays.items()}], core_ids=[0])
    got = r.results[0]["out_0"]
    return _np.ascontiguousarray(got.transpose(2, 1, 0)).reshape(1, 512, 1024)
```

```python
import concourse.bass as bass
from concourse import mybir
from contextlib import ExitStack

F32 = mybir.dt.float32
R32 = mybir.dt.float32r
U32 = mybir.dt.uint32
ALU = mybir.AluOpType
ACT = mybir.ActivationFunctionType
AX = mybir.AxisListType
PE, SC, VE, GP, SY = "tensor", "scalar", "vector", "gpsimd", "sync"
NEG = -1e30
EPS = 1e-6
DBG = None


class Queues:

    def __init__(self, nc, ctx):
        self.nc, self.ctx = nc, ctx
        self.q = {e: [] for e in (PE, SC, VE, GP, SY)}
        self.hold = {e: [] for e in self.q}
        self.dma_sems = {}
        self.counts = {}

    def add(self, eng, fn, w=(), free=False):
        q = self.q[eng]
        waits = [t for t in w if t is not None] + self.hold[eng]
        self.hold[eng] = []
        if not free and eng in (SC, VE, GP):
            for n in range(len(q) - 1, -1, -1):
                if q[n][2] is None:
                    waits.append((eng, n))
                    break
        q.append((fn, waits, None))
        return (eng, len(q) - 1)

    def dma(self, eng, sem, out, in_, w=()):
        if sem not in self.dma_sems:
            self.dma_sems[sem] = self.ctx.enter_context(self.nc.semaphore("d_" + sem))
            self.counts[sem] = 0
        self.counts[sem] += 16
        waits = [t for t in w if t is not None] + self.hold[eng]
        self.hold[eng] = []
        self.q[eng].append((lambda e: e.dma_start(out, in_), waits, sem))
        return (sem, self.counts[sem])

    def last(self, *engs):
        out = []
        for e in engs:
            for n in range(len(self.q[e]) - 1, -1, -1):
                if self.q[e][n][2] is None:
                    out.append((e, n))
                    break
        return out

    def barrier(self, extra=()):
        marks = {e: self.last(e) for e in (PE, SC, VE, GP)}
        for e in marks:
            self.hold[e] += [t for x in marks if x != e or e != PE for t in marks[x]] + list(extra)
        return [t for x in marks.values() for t in x]

    def emit(self, block):
        used = set()
        for q in self.q.values():
            for _, waits, _ in q:
                used |= {t for t in waits if t[0] in self.q}
        sems = {e: self.ctx.enter_context(self.nc.semaphore("s_" + e)) for e in self.q}
        value, total = {}, {}
        for e, q in self.q.items():
            n = 0
            for i in range(len(q)):
                if (e, i) in used:
                    n += 1
                    value[(e, i)] = n
        for e, q in self.q.items():
            def body(eng, e=e, q=q):
                seen = {}
                for i, (fn, waits, dsem) in enumerate(q):
                    need = {}
                    for t in waits:
                        v = value[t] if t[0] in self.q else t[1]
                        need[t[0]] = max(need.get(t[0], 0), v)
                    for s, v in need.items():
                        if seen.get(s, 0) < v:
                            eng.wait_ge(sems[s] if s in self.q else self.dma_sems[s], v)
                            seen[s] = v
                    if fn is None:
                        continue
                    ins = fn(eng)
                    if dsem is not None:
                        ins.then_inc(self.dma_sems[dsem], 16)
                    elif (e, i) in value:
                        ins.then_inc(sems[e], 1)
            {PE: block.tensor, SC: block.scalar, VE: block.vector, GP: block.gpsimd, SY: block.sync}[e](body)


class Slots:

    def __init__(self, bufs):
        self.bufs = bufs
        self.free = list(range(len(bufs)))
        self.readers = [[] for _ in bufs]

    def take(self):
        i = self.free.pop(0)
        r, self.readers[i] = self.readers[i], []
        return i, self.bufs[i], r

    def done(self, i, *toks):
        if i not in self.free:
            self.free.append(i)
        self.readers[i] += list(toks)


CONST = {}


def const_array():
    import numpy as np
    CONST.clear()
    p = np.arange(128)[:, None]
    i = np.arange(128)[None, :]
    ch = (p // 64) == (i // 64)
    parts = [("ident", p == i), ("ones", np.ones((128, 128))), ("upper", p <= i), ("strict", p < i),
             ("cum64", ch & (p <= i)), ("same64", ch)]
    for l in range(7):
        s = 1 << l
        parts.append((f"lvl{l}", (p // (2 * s) == i // (2 * s)) & (i % (2 * s) >= s) & (p % (2 * s) < s)))
    parts.append(("causal", np.where(i > p, NEG, 0.0)))
    t = np.arange(512)[None, :]
    parts.append(("notfirst", np.broadcast_to(t % 64 != 0, (128, 512))))
    parts.append(("col01", np.concatenate([p // 64 == 0, p // 64 == 1], 1)))
    n = np.arange(31)[None, None, :]
    q = np.arange(4)[None, :, None] * 128 + p[:, :, None]
    ok = (n * 16 + 31 <= q)
    parts.append(("cmpadd", np.where(ok, 0.0, NEG).reshape(128, 124)))
    parts.append(("cmpmul", ok.reshape(128, 124)))
    parts.append(("iota", np.broadcast_to(i, (128, 128))))
    off = 0
    for name, a in parts:
        CONST[name] = (off, a.shape[1])
        off += a.shape[1]
    return np.concatenate([a.astype(np.float32) for _, a in parts], axis=1)


def mask_array():
    import numpy as np
    s = np.arange(128)[:, None]
    t = np.arange(512)[None, :]
    same = (s // 64) == ((t % 128) // 64)
    a = np.concatenate([same & (s <= t % 128), same & (s > t % 128)], axis=1)
    return a.astype(np.uint32)


def build(nc, D, shapes):
    with ExitStack() as ctx:
        _build(nc, D, ctx)


def _build(nc, D, ctx):
    Q = Queues(nc, ctx)

    def sb(name, shape, dt=F32, c=ctx):
        return c.enter_context(nc.sbuf_tensor(name, shape, dt))

    ncst = D["consts"].shape[1]
    cst = sb("cst", [128, ncst])
    C = {k: cst[:, o:o + n] for k, (o, n) in CONST.items()}
    colw = D["cols"].shape[1]
    cols = sb("cols", [128, colw])
    cc = {k: cols[:, o:o + n] for k, (o, n) in COLS.items()}
    hh = sb("hh", [128, 8, 512], R32)
    hl = sb("hl", [128, 8, 512], R32)
    mT = sb("mT", [128, 8, 16])
    hmh = sb("hmh", [128, 8, 16], R32)
    hml = sb("hml", [128, 8, 16], R32)
    modc = sb("modc", [128, 48])
    scl = sb("scl", [128, 16])
    ring = [sb(f"ring{i}", [128, 2048]) for i in range(4)]
    wh = [sb(f"wh{i}", [128, 2048], R32) for i in range(2)]
    wl = [sb(f"wl{i}", [128, 2048], R32) for i in range(2)]
    bank = [ctx.enter_context(nc.psum_tensor(f"bank{i}", [128, 512], F32)) for i in range(8)]
    B = Slots(bank)
    R = Slots(ring)
    WS = Slots(list(zip(wh, wl)))
    ident = C["ident"]

    def mm(out, pairs, w=(), start=True, stop=True, check=True):
        n = len(pairs)
        for i, (a, b) in enumerate(pairs):
            t = Q.add(PE, lambda e, a=a, b=b, s=start and i == 0, z=stop and i == n - 1: e.matmul(
                out, a, b, start=s, stop=z, skip_group_check=not check), w if i == 0 else ())
        return t

    def mm3(out, pairs, w=(), start=True, stop=True, check=True):
        lst = []
        for (ah, al), (bh, bl) in pairs:
            lst += [(ah, bh), (ah, bl), (al, bh)]
        return mm(out, lst, w, start, stop, check)

    def tr(out, in_, w=()):
        k = in_.shape[0]
        return Q.add(PE, lambda e: e.transpose(out, in_, ident[0:k, 0:k]), w)

    def act(out, in_, fn, w=(), free=False, **kw):
        return Q.add(SC, lambda e: e.activation(out, in_, fn, **kw), w, free)

    def tt(out, a, b, op, w=(), free=False, eng=VE):
        return Q.add(eng, lambda e: e.tensor_tensor(out, a, b, op), w, free)

    def ts(out, a, s1, op0, s2=None, op1=None, w=(), free=False, eng=VE):
        if op1 is None:
            return Q.add(eng, lambda e: e.tensor_scalar(out, a, s1, None, op0), w, free)
        return Q.add(eng, lambda e: e.tensor_scalar(out, a, s1, s2, op0, op1), w, free)

    def stt(out, a, s, b, op0, op1, w=(), free=False):
        return Q.add(VE, lambda e: e.scalar_tensor_tensor(out=out, in0=a, scalar=s, in1=b, op0=op0, op1=op1),
                     w, free)

    def recip(out, a, w=(), free=False):
        return Q.add(VE, lambda e: e.reciprocal(out, a), w, free)

    def copy(out, a, w=(), free=False, eng=VE):
        if eng == SC:
            return act(out, a, ACT.Copy, w, free)
        return Q.add(eng, lambda e: e.tensor_copy(out, a), w, free)

    def red(out, a, op, w=(), free=False):
        return Q.add(VE, lambda e: e.tensor_reduce(out, a, AX.X, op), w, free)

    def bc(ap, n):
        a = ap.unsqueeze(2)
        return a.to_broadcast([a.shape[0], a.shape[1], n])

    def rep(ap, n):
        a = ap.unsqueeze(1)
        return a.to_broadcast([a.shape[0], n, a.shape[2]])

    M, A_, S_ = ALU.mult, ALU.add, ALU.subtract

    def split(hi, lo, src, w=(), eng=VE, f=False):
        a = act(hi, src, ACT.Copy, w, free=f)
        return tt(lo, src, hi.bitcast(F32), S_, [a], free=True, eng=eng)

    plan = []

    def want(name, lo_, hi_, n, parts=True):
        for s in range(lo_, hi_):
            plan.append((name, s, n, parts))

    want("ada", 0, 8, 2048, False)
    want("win1", 0, 12, 2048)
    want("win1t", 0, 1, 2048)
    want("win1g", 0, 1, 160)
    want("cmpw1", 0, 4, 2048, False)
    want("cmpw2", 0, 1, 256, False)
    want("ada", 8, 24, 2048, False)
    want("wout1", 0, 4, 2048)
    for g in range(2):
        want("wup", 11 * g, 11 * g + 11, 2048)
        want("wdn", 8 * g, 8 * g + 8, 1408)
    want("qk2", 0, 4, 2048)
    want("glow", 0, 1, 1024)
    want("v2", 0, 4, 2048)
    want("gout2", 0, 4, 2048)
    want("gatea", 0, 4, 2048)
    want("upgla", 0, 4, 2048)
    want("dt2", 0, 1, 256)
    for g in range(4):
        want("xs2", 2 * g, 2 * g + 2, 2048)
        want("bc2", g, g + 1, 2048)
        want("z2", 2 * g, 2 * g + 2, 2048)
    want("upssd", 0, 8, 2048)
    want("gateb", 0, 4, 2048)
    want("wout2", 0, 4, 2048)
    want("wq", 0, 8, 2048)
    want("subk", 0, 1, 2048, False)
    want("u", 0, 64, 2048)
    want("v", 0, 64, 2048)
    order = [(a, b) for a, b, _, _ in plan]
    stream, ready = [], []

    def weights():
        name, idx, n, parts = plan.pop(0)
        i, buf, free = R.take()
        t = Q.dma(SY, f"ring{i}", buf[:, 0:n], D[name][idx][:, 0:n], free)
        stream.append((i, buf, t, n, parts))

    def freed(i, tok):
        R.done(i, tok)
        if plan:
            weights()

    def prepare():
        if not stream:
            return
        i, buf, t, n, parts = stream.pop(0)
        if not parts:
            ready.append((("raw", i), buf, [t]))
            return
        wi, (h_, l_), free = WS.take()
        a = act(h_[:, 0:n], buf[:, 0:n], ACT.Copy, [t] + free, free=True)
        g = Q.add(GP, lambda e: e.tensor_tensor(l_[:, 0:n], buf[:, 0:n], h_[:, 0:n].bitcast(F32), S_),
                  [a] + free, True)
        ready.append((("parts", wi), (h_, l_), [a, g]))
        freed(i, g)

    def slot(name, idx):
        assert order.pop(0) == (name, idx), (name, idx)
        if not ready:
            prepare()
        r = ready.pop(0)
        if len(WS.free) and not ready and stream and (r[0][0] == "parts" or not stream[0][4]):
            prepare()
        elif len(WS.free) and not ready:
            prepare()
        return r

    def release(key, tok):
        if key[0] == "raw":
            freed(key[1], tok)
        else:
            WS.done(key[1], tok)

    k0 = Q.dma(SC, "c0", cst[:, :], D["consts"])
    k0 = Q.dma(SC, "c0", cols[:, :], D["cols"])
    k0 = Q.dma(SC, "c0", mT[:, :, :], D["metaT"])
    xd_ = nc.dram_tensor("x_spill", (128, 8, 512), F32).ap()
    xa_ = nc.dram_tensor("a_spill", (128, 8, 512), F32).ap()
    yd_ = nc.dram_tensor("y_spill", (128, 8, 512), F32).ap()

    def load(name, c, src, w=()):
        t_ = sb(name, [128, 8, 512], F32, c)
        return t_, Q.dma(SY, name, t_[:, :, :], src, w)
    for _ in range(4):
        weights()
    for e in (PE, VE, GP):
        Q.hold[e] += [k0]
    Q.hold[SC] += [k0]

    dumped = []

    def dump(name, ap):
        if DBG == name:
            toks = Q.last(PE, SC, VE, GP)
            d = D["dbg"]
            shp = list(ap.shape)
            n = 1
            for v in shp[1:]:
                n *= v
            dst = d[0:shp[0], 0:n]
            if len(shp) == 3:
                dst = dst.rearrange("p (a b) -> p a b", b=shp[2])
            Q.dma(SY, "dbg", dst, ap, toks)
            dumped.append(1)
            return True
        return False

    def norm_stats(src, T, N, out, tmp, w=()):
        k = len(src)
        i, ps, fr = B.take()
        for j, s in enumerate(src):
            a = act(tmp[j % 2][:, 0:T], s, ACT.Square, (list(w) if j == 0 else []) +
                    ([pes[-2]] if j >= 2 else []), free=j > 0)
            if j == 0:
                pes = []
            pes.append(mm(ps[:, 0:T], [(C["ones"], tmp[j % 2][:, 0:T])], [a] + (fr if j == 0 else []),
                          start=j == 0, stop=j == k - 1))
        ts(out, ps[:, 0:T], 1.0 / N, M, EPS, A_, w=[pes[-1]])
        v = recip(out, out)
        B.done(i, v)
        return act(out, out, ACT.Sqrt, [v])

    def linear(name, ntiles, per, kt, rhs, consume, w=(), first=None, s0=0):
        n = 0
        for s in range(ntiles // per):
            i, (h_, l_), t = slot(name, s0 + s)
            vh, vl = (x[:, 0:per * kt * 128].rearrange("p (a k n) -> p a k n", a=per, k=kt) for x in (h_, l_))
            for a in range(per):
                tile_ = lambda k: (vh[:, a, k, :], vl[:, a, k, :])
                if first is not None and n >= first:
                    bi, ps, fr = B.take()
                    m = mm3(ps[:, 0:16], [(tile_(k), mk(k)) for k in range(kt)], t + fr)
                    B.done(bi, consume(n, ps, m, True))
                bi, ps, fr = B.take()
                m = mm3(ps[:, :], [(tile_(k), rhs(k)) for k in range(kt)], t + fr + list(w))
                if a == per - 1:
                    release(i, m)
                B.done(bi, consume(n, ps, m) if first is None else consume(n, ps, m, False))
                n += 1

    hk = lambda k: (hh[:, k, :], hl[:, k, :])
    mk = lambda k: (hmh[:, k, :], hml[:, k, :])
    hkt = lambda k, j: (hh[:, k, 128 * j:128 * j + 128], hl[:, k, 128 * j:128 * j + 128])

    def norm_to(src, msrc, wcol, ar, shift=None, out=None):
        uniq.append(1)
        tmp = [sb(f"nt{j}_{len(uniq)}", [128, 512], F32, ar) for j in range(2)]
        tq = Slots([sb(f"nq{j}_{len(uniq)}", [128, 512], F32, ar) for j in range(3)])
        rstd = sb(f"nr{len(uniq)}", [128, 512], F32, ar)
        n = norm_stats([src[:, k, :] for k in range(8)], 512, 1024, rstd[:, :], tmp)
        for k in range(8):
            if out is not None:
                r = stt(out[:, k, :], src[:, k, :], wcol[:, k:k + 1], rstd[:, :], M, M, [n], free=True)
                continue
            qi, q, f = tq.take()
            v = stt(q[:, :], src[:, k, :], wcol[:, k:k + 1], rstd[:, :], M, M, [n] + f, free=True)
            if shift is not None:
                v = ts(q[:, :], q[:, :], shift[:, k:k + 1], A_)
            r = split(hh[:, k, :], hl[:, k, :], q[:, :], [v], f=True)
            tq.done(qi, r)
        if msrc is not None:
            rst2 = sb("nm", [128, 16], F32, ar)
            q16 = sb("nm16", [128, 8, 16], F32, ar)
            n = norm_stats([msrc[:, k, :] for k in range(8)], 16, 1024, rst2[:, :], tmp, Q.last(PE))
            for k in range(8):
                v = stt(q16[:, k, :], msrc[:, k, :], wcol[:, k:k + 1], rst2[:, :], M, M, [n], free=k > 0)
            r = split(hmh[:, :, :], hml[:, :, :], q16[:, :, :], [v])
        return r

    uniq = []

    def together(*gens):
        gens = [[g, n, 0.0] for g, n in gens]
        while gens:
            for x in list(gens):
                x[2] += x[1]
                while x[2] >= 1:
                    x[2] -= 1
                    if next(x[0], 0) == 0:
                        gens.remove(x)
                        break

    finish = lambda: Q.emit(ctx.enter_context(nc.Block()))

    def endit():
        Q.q[SY].append((None, [("dbg", Q.counts["dbg"])], None))
        finish()

    scv = sb("scv", [128, 8])

    def modulation(s0, s1, row):
        bi, pm, fr = B.take()
        cprev = []
        for s in range(s0, s1):
            i, buf, t = slot("ada", s)
            v = buf[:, :].rearrange("p (k n) -> p k n", k=8)
            pi, ps, f2 = B.take()
            m = mm(ps[0:1, 0:256], [(scv[:, k:k + 1], v[:, k, :]) for k in range(8)], t + [a0] + f2)
            release(i, m)
            cp = copy(row[0:1, s % 2, :], ps[0:1, 0:256], [m] + cprev[-2:-1], eng=VE)
            B.done(pi, cp)
            yield
            for j in range(2):
                m = Q.add(PE, lambda e, c=2 * (s - s0) + j, s=s, j=j: e.matmul(
                    pm[:, c:c + 1], row[0:1, s % 2, 128 * j:128 * j + 128],
                    C["ones"][0:1, 0:1], start=c == 0, stop=True, skip_group_check=True), [cp] + fr)
            cprev.append(m)
        B.done(bi, tt(modc[:, 2 * s0:2 * s1], pm[:, 0:2 * (s1 - s0)], cc["adab"][:, 2 * s0:2 * s1], A_, [m]))

    with ExitStack() as ar:
        xT, k1 = load("x0", ar, D["xT"])
        row = sb("modrow", [1, 2, 256], F32, ar)
        a0 = act(scv[:, :], cc["c"], ACT.Silu)
        for _ in modulation(0, 8, row):
            pass
        v = stt(scl[:, 0:8], modc[:, 8:16], 1.0, cc["norm1"], A_, M)
        Q.hold[SC] += [v, k1]
        hready = norm_to(xT, None, scl[:, 0:8], ar, modc[:, 0:8])
        Q.barrier()

    with ExitStack() as ar:
        qkv = sb("qkv", [128, 12, 512], F32, ar)
        gz = sb("gz", [128, 4, 512], F32, ar)
        nsq = sb("nsq", [128, 4, 512], F32, ar)
        kk2 = sb("kk2", [128, 2, 512], F32, ar)
        tm = sb("tm", [128, 4, 276], F32, ar)
        kcmp = sb("kcmp", [128, 32], F32, ar)
        vcmp = sb("vcmp", [32, 128], F32, ar)
        mix = sb("mix", [128, 4, 512], F32, ar)
        with ExitStack() as a2:
            cv = Slots([sb(f"cv{j}", [128, 512], F32, a2) for j in range(2)])
            rs = Slots([sb(f"rs{j}", [128, 512], F32, a2) for j in range(4)])
            kvc = mix[:, 0:2, :]

            def units(lst, rdy, T=512):
                st_ = []
                for src, scale, fac in lst:
                    ri, r, f = rs.take()
                    st_.append((ri, r[:, 0:T], act(r[:, 0:T], src, ACT.Square, rdy + f, free=True)))
                mms = []
                for ri, r, a in st_:
                    bi, ps, fr = B.take()
                    mms.append((bi, ps, mm(ps[:, 0:T], [(C["ones"], r)], [a] + fr)))
                vs = []
                for (ri, r, _), (bi, ps, m), (src, scale, fac) in zip(st_, mms, lst):
                    v = ts(r, ps[:, 0:T], scale, M, EPS, A_, w=[m], free=True)
                    B.done(bi, v)
                for ri, r, _ in st_:
                    vs.append(recip(r, r))
                as_ = [act(r, r, ACT.Sqrt, [v], free=True) for (ri, r, _), v in zip(st_, vs)]
                for (ri, r, _), a, (src, scale, fac) in zip(st_, as_, lst):
                    v = stt(src, src, fac, r, M, M, [a], free=True)
                    rs.done(ri, v)
                return v

            def take1(n, ps, m):
                if n < 12:
                    ci, c, f = cv.take()
                    w = cc["conv1"][:, 4 * n:4 * n + 4]
                    ts(c[:, :], ps[:, :], w[:, 3:4], M, w=[m] + f)
                    for d in (1, 2, 3):
                        v = stt(c[:, d:512], ps[:, 0:512 - d], w[:, 3 - d:4 - d], c[:, d:512], M, A_)
                    a = act(qkv[:, n, :], c[:, :], ACT.Silu, [v])
                    cv.done(ci, a)
                    return v
                if n < 16:
                    return act(gz[:, n - 12, :], ps[:, :], ACT.Silu, [m])
                if n < 20:
                    return copy(nsq[:, n - 16, :], ps[:, :], [m], eng=SC)
                if n < 22:
                    return copy(kvc[:, n - 20, :], ps[:, :], [m])
                return copy(kk2[:, n - 22, :], ps[:, :], [m], eng=SC)

            def take_all(n, ps, m):
                v = take1(n, ps, m)
                if n in (5, 9):
                    units([(qkv[:, x, :], 1.0, 128 ** -0.5 if n == 5 else 1.0)
                           for x in range(n - 5, n - 1)], Q.last(SC))
                if n == 21:
                    units([(nsq[:, x, :], 1 / 128, cc["qn"]) for x in range(4)], Q.last(SC))
                return v

            linear("win1", 24, 2, 8, hk, take_all, [hready])
            units([(kk2[:, 0, :], 1 / 128, cc["kslc"]), (kk2[:, 1, :], 1 / 128, cc["kwin"])], Q.last(SC))
            for name, off, n_ in (("win1t", 0, 256), ("win1g", 256, 20)):
                i, (h_, l_), t = slot(name, 0)
                vh, vl = (x[:, 0:8 * n_].rearrange("p (k n) -> p k n", k=8) for x in (h_, l_))
                for j in range(4):
                    bi, ps, fr = B.take()
                    m = mm3(ps[:, 0:n_], [(hkt(k, j), (vh[:, k, :], vl[:, k, :])) for k in range(8)], t + fr)
                    B.done(bi, copy(tm[:, j, off:off + n_], ps[:, 0:n_], [m]))
                release(i, m)
            blk = mix[:, 2:4, :].rearrange("p a b -> p (a b)")[:, 0:992].rearrange("p (a n) -> p a n", a=32)
            hid = sb("hid", [128, 32], F32, a2)
            hidk = sb("hidk", [128, 32], F32, a2)
            for c in range(2):
                src = kvc[:, c, 0:512].rearrange("p (n s) -> p s n", s=16)
                pos = cc["kpos" if c == 0 else "vpos"]
                tt(blk[:, 0:16, :], src[:, :, 0:31], bc(pos[:, 0:16], 31), A_, Q.last(PE))
                v = tt(blk[:, 16:32, :], src[:, :, 1:32], bc(pos[:, 16:32], 31), A_)
                bi, ps, fr = B.take()
                for half in range(2):
                    i, buf, t = slot("cmpw1", 2 * c + half)
                    w1 = buf[:, :].rearrange("p (a n) -> p a n", a=16)
                    m = mm(ps[:, 0:31], [(w1[:, a, :], blk[:, 16 * half + a, :]) for a in range(16)], t + [v] + fr,
                           start=half == 0, stop=half == 1)
                    release(i, m)
                a = act((hidk, hid)[c][:, 0:31], ps[:, 0:31], ACT.Silu, [m])
                if c == 0:
                    akey = a
                B.done(bi, a)
            i2, w2, t2 = slot("cmpw2", 0)
            bi, ps, fr = B.take()
            m = mm(ps[:, 0:31], [(w2[:, 0:128], hidk[:, 0:31])], t2 + [akey] + fr)
            v = copy(kcmp[:, 0:31], ps[:, 0:31], [m])
            B.done(bi, v)
            units([(kcmp[:, 0:31], 1 / 128, cc["kcmpn"])], [v], T=31)
            bi, ps, fr = B.take()
            m = mm(ps[0:31, 0:128], [(hid[:, 0:31], w2[:, 128:256])], [a] + fr)
            release(i2, m)
            B.done(bi, copy(vcmp[0:31, :], ps[0:31, 0:128], [m]))
            if dump("qkv", qkv[:, :, :]) or dump("kcmp", kcmp[:, 0:31]) or dump("vcmp", vcmp[0:31, :]) \
                    or dump("nsq", nsq[:, :, :]) or dump("kk2", kk2[:, :, :]) or dump("tm", tm[:, :, :]):
                return endit()
            Q.barrier()

        with ExitStack() as a2:
            def big(name):
                return sb(name, [128, 4, 128], F32, a2)
            sm = {k: sb("g_" + k, [128, 4, 4], F32, a2) for k in
                  ("g", "beta", "u", "v", "gc", "gt", "egc", "kds", "gl", "bg")}
            gA = tm[:, :, 256:260]
            gB = tm[:, :, 260:264]
            nA = sb("nA", [128, 4], F32, a2)
            act(nA[:, :], cc["alog"], ACT.Exp)
            ts(nA[:, :], nA[:, :], -1.0, M, w=Q.last(SC))
            v = tt(sm["u"][:, :, :], gA, rep(cc["dtb1"], 4), A_)
            act(sm["v"][:, :, :], sm["u"][:, :, :], ACT.Abs, [v])
            act(sm["v"][:, :, :], sm["v"][:, :, :], ACT.Exp, scale=-1.0)
            a = act(sm["v"][:, :, :], sm["v"][:, :, :], ACT.Ln, bias=1.0)
            stt(sm["u"][:, :, :], sm["u"][:, :, :], 0.0, sm["v"][:, :, :], ALU.max, A_, [a])
            g = tt(sm["g"][:, :, :], sm["u"][:, :, :], rep(nA[:, :], 4), M)
            a = act(sm["beta"][:, :, :], gB, ACT.Sigmoid)
            bi, ps, fr = B.take()
            m = mm(ps[:, 0:16], [(C["upper"], sm["g"][:, :, :].rearrange("p a b -> p (a b)"))], [g, a] + fr)
            v = copy(sm["gc"][:, :, :].rearrange("p a b -> p (a b)"), ps[:, 0:16], [m])
            B.done(bi, v)
            bi, ps, fr = B.take()
            m = mm(ps[:, 0:16], [(C["ones"], sm["g"][:, :, :].rearrange("p a b -> p (a b)"))], fr)
            v = copy(sm["gt"][:, :, :].rearrange("p a b -> p (a b)"), ps[:, 0:16], [m])
            B.done(bi, v)
            v = tt(sm["kds"][:, :, :], sm["gt"][:, :, :], sm["gc"][:, :, :], S_)
            act(sm["kds"][:, :, :], sm["kds"][:, :, :], ACT.Exp, [v])
            act(sm["gl"][:, :, :], sm["gt"][:, :, :], ACT.Exp)
            a = act(sm["egc"][:, :, :], sm["gc"][:, :, :], ACT.Exp)
            tt(sm["bg"][:, :, :], sm["beta"][:, :, :], sm["egc"][:, :, :], M, [a])

            vb, kbe, kd = big("vb"), big("kbe"), big("kd")
            egb, btb, dtm, AT, aT = big("egb"), big("btb"), big("dtm"), big("AT"), big("aT")
            X, XT, BT, Y, qd = (big(n_) for n_ in ("X", "XT", "BT", "Y", "qd"))
            wT, u, vn = btb, egb, kbe
            St = big("St")

            def four(fn, w=()):
                bi, ps, fr = B.take()
                for h in range(4):
                    lst = fn(h)
                    for n_, (l, r) in enumerate(lst):
                        m = Q.add(PE, lambda e, l=l, r=r, h=h, s=(h == 0 and n_ == 0): e.matmul(
                            ps[:, 128 * h:128 * h + 128], l, r, start=s, stop=True, skip_group_check=True),
                            (list(w) + fr) if h == 0 and n_ == 0 else ())
                return bi, ps[:, :].rearrange("p (a b) -> p a b", a=4), m

            def gdn():
                for mt in range(4):
                    c0 = 128 * mt
                    kT = lambda h: qkv[:, 4 + h, c0:c0 + 128]
                    qT = lambda h: qkv[:, h, c0:c0 + 128]
                    for what in (4, 8):
                        yield
                        bi, ps, fr = B.take()
                        for h in range(4):
                            m = tr(ps[:, 128 * h:128 * h + 128], qkv[:, what + h, c0:c0 + 128],
                                   (fr + Q.last(VE, SC)) if h == 0 else ())
                        p3 = ps[:, :].rearrange("p (a b) -> p a b", a=4)
                        if what == 4:
                            tt(kbe[:, :, :], p3, bc(sm["bg"][:, mt, :], 128), M, [m] + Q.last(PE))
                            v = tt(kd[:, :, :], p3, bc(sm["kds"][:, mt, :], 128), M, free=True)
                        else:
                            v = tt(vb[:, :, :], p3, bc(sm["beta"][:, mt, :], 128), M, [m] + Q.last(PE))
                        B.done(bi, v)
                    yield
                    bi, p3, m = four(lambda h: [(sm["g"][:, mt, h:h + 1].to_broadcast([128, 128]), C["upper"])])
                    act(egb[:, :, :], p3, ACT.Exp, [m] + Q.last(VE, PE))
                    v = tt(dtm[:, :, :], p3, bc(sm["gc"][:, mt, :], 128), S_, [m] + Q.last(SC))
                    B.done(bi, v)
                    v = ts(dtm[:, :, :], dtm[:, :, :], 0.0, ALU.min)
                    a = act(dtm[:, :, :], dtm[:, :, :], ACT.Exp, [v])
                    tt(dtm[:, :, :], dtm[:, :, :], rep(C["upper"], 4), M, [a])
                    yield
                    bi, p3, m = four(lambda h: [(sm["beta"][:, mt, h:h + 1].to_broadcast([128, 128]), ident)])
                    v = tt(btb[:, :, :], p3, rep(C["strict"], 4), M, [m])
                    B.done(bi, v)
                    v = tt(btb[:, :, :], btb[:, :, :], dtm[:, :, :], M)
                    yield
                    bi, p3, m = four(lambda h: [(kT(h), kT(h))])
                    v = tt(AT[:, :, :], p3, btb[:, :, :], M, [m])
                    B.done(bi, v)
                    yield
                    bi, p3, m = four(lambda h: [(kT(h), qT(h))])
                    v = tt(aT[:, :, :], p3, dtm[:, :, :], M, [m] + Q.last(PE))
                    B.done(bi, v)
                    tt(qd[:, :, :], qkv[:, 0:4, c0:c0 + 128], egb[:, :, :], M, Q.last(SC))
                    tt(BT[:, :, :], AT[:, :, :], rep(C["lvl0"], 4), M)
                    v = tt(XT[:, :, :], rep(ident, 4), BT[:, :, :], S_)
                    yield
                    bi, ps, fr = B.take()
                    for h in range(4):
                        m = tr(ps[:, 128 * h:128 * h + 128], XT[:, h, :], ([v] + fr) if h == 0 else ())
                    v = copy(X[:, :, :], ps[:, :].rearrange("p (a b) -> p a b", a=4), [m])
                    B.done(bi, v)
                    for l in range(1, 7):
                        v = tt(BT[:, :, :], AT[:, :, :], rep(C[f"lvl{l}"], 4), M, Q.last(PE))
                        yield
                        bi, p3, m = four(lambda h: [(BT[:, h, :], X[:, h, :])], [v])
                        v = copy(Y[:, :, :], p3, [m])
                        B.done(bi, v)
                        yield
                        bi, p3, m = four(lambda h: [(Y[:, h, :], XT[:, h, :])], [v])
                        if l < 6:
                            b2, p4, m2 = four(lambda h: [(XT[:, h, :], Y[:, h, :])])
                        else:
                            m2 = m
                        v = tt(XT[:, :, :], XT[:, :, :], p3, S_, [m2])
                        B.done(bi, v)
                        if l < 6:
                            v = tt(X[:, :, :], X[:, :, :], p4, S_, [m2])
                            B.done(b2, v)
                    yield
                    bi, p3, m = four(lambda h: [(kbe[:, h, :], XT[:, h, :])], [v])
                    v = copy(wT[:, :, :], p3, [m])
                    B.done(bi, v)
                    yield
                    bi, p3, m = four(lambda h: [(XT[:, h, :], vb[:, h, :])])
                    v = copy(u[:, :, :], p3, [m])
                    B.done(bi, v)
                    if mt > 0:
                        yield
                        bi, p3, m = four(lambda h: [(wT[:, h, :], St[:, h, :])], [v])
                        v = tt(vn[:, :, :], u[:, :, :], p3, S_, [m])
                        B.done(bi, v)
                        V_ = vn
                    else:
                        V_ = u
                    yield
                    bi, p3, m = four(lambda h: ([(St[:, h, :], qd[:, h, :])] if mt > 0 else []) +
                                     [(V_[:, h, :], aT[:, h, :])], [v])
                    v = copy(mix[:, 0:4, c0:c0 + 128], p3, [m])
                    B.done(bi, v)
                    if mt < 3:
                        yield
                        bi, p3, m = four(lambda h: [(kd[:, h, :], V_[:, h, :])])
                        if mt == 0:
                            v = copy(St[:, :, :], p3, [m])
                        else:
                            tt(St[:, :, :], St[:, :, :], bc(sm["gl"][:, mt, :], 128), M, [m])
                            v = tt(St[:, :, :], St[:, :, :], p3, A_)
                        B.done(bi, v)

            def gdn_out():
                sq = Slots([x[:, :, :].rearrange("p a b -> p (a b)") for x in (kbe, kd)])
                rs = Slots([x[:, :, :].rearrange("p a b -> p (a b)") for x in (AT, aT)])
                w_ = Q.last(PE)
                for h in range(4):
                    si, s, f = sq.take()
                    a = act(s[:, :], mix[:, h, :], ACT.Square, f + w_ + Q.last(VE))
                    bi, ps, fr = B.take()
                    m = mm(ps[:, :], [(C["ones"], s[:, :])], [a] + fr)
                    sq.done(si, m)
                    yield
                    ri, r, f = rs.take()
                    v = ts(r[:, :], ps[:, :], 1 / 128, M, EPS, A_, w=[m] + f)
                    B.done(bi, v)
                    v = recip(r[:, :], r[:, :])
                    a = act(r[:, :], r[:, :], ACT.Sqrt, [v])
                    yield
                    stt(mix[:, h, :], mix[:, h, :], cc["gdnn"], r[:, :], M, M, [a])
                    v = tt(mix[:, h, :], mix[:, h, :], gz[:, h, :], M)
                    rs.done(ri, split(hh[:, h, :], hl[:, h, :], mix[:, h, :], [v]))

            Pb = Slots([sb(f"P{j}", [128, 512], F32, a2) for j in range(2)])
            PC = Slots([sb("PC", [32, 128], F32, a2)])
            PT = Slots([sb(f"PT{j}", [128, 512], F32, a2) for j in range(2)])
            st = sb("st", [128, 48, 4], F32, a2)
            gates = sb("gates", [128, 4, 12], F32, a2)
            act(gates[:, :, :], tm[:, :, 264:276], ACT.Sigmoid)
            gtok = Q.last(SC)[0]
            SCL = 128 ** -0.5
            def attention():
                nst = 0
                for mt in range(4):
                    L = 128 * (mt + 1)
                    for h in range(4):
                        qT = nsq[:, h, 128 * mt:128 * mt + 128]
                        pvs = []
                        for br in range(3):
                            n_ = 31 if br == 0 else L
                            rhs = kcmp[:, 0:31] if br == 0 else kk2[:, br - 1, 0:L]
                            bi, ps, fr = B.take()
                            m = mm(ps[:, 0:n_], [(qT, rhs)], fr)
                            s4 = st[:, nst, :]
                            nst += 1
                            if br == 0:
                                add = C["cmpadd"][:, 31 * mt:31 * mt + 31]
                                tt(ps[:, 0:31], ps[:, 0:31], add, A_, [m], free=True)
                            else:
                                tt(ps[:, L - 128:L], ps[:, L - 128:L], C["causal"], A_, [m], free=True)
                            red(s4[:, 0:1], ps[:, 0:n_], ALU.max)
                            v = ts(s4[:, 1:2], s4[:, 0:1], -1e25, ALU.max, -SCL, M)
                            pi, P, f = Pb.take()
                            yield
                            a = act(P[:, 0:n_], ps[:, 0:n_], ACT.Exp, [v] + f, free=True, bias=s4[:, 1:2],
                                    scale=SCL, accum_out=s4[:, 2:3])
                            B.done(bi, a)
                            v = ts(s4[:, 3:4], s4[:, 2:3], 1e-30, ALU.max, w=[a, gtok])
                            recip(s4[:, 3:4], s4[:, 3:4])
                            tt(s4[:, 3:4], s4[:, 3:4], gates[:, mt, 3 * h + br:3 * h + br + 1], M)
                            if br == 0:
                                v = stt(P[:, 0:31], P[:, 0:31], s4[:, 3:4], C["cmpmul"][:, 31 * mt:31 * mt + 31], M, M)
                            else:
                                v = ts(P[:, 0:n_], P[:, 0:n_], s4[:, 3:4], M)
                            yield
                            bi, ps, fr = B.take()
                            ring_ = PC if br == 0 else PT
                            ti, T_, tf = ring_.take()
                            if br == 0:
                                m = tr(ps[0:31, 0:128], P[:, 0:31], [v] + fr)
                                v = copy(T_[0:31, 0:128], ps[0:31, 0:128], [m] + tf, eng=SC, free=True)
                                pvs.append((vcmp[0:31, :], T_[0:31, 0:128], v, ti, ring_))
                            else:
                                for j in range(mt + 1):
                                    m = tr(ps[:, 128 * j:128 * j + 128], P[:, 128 * j:128 * j + 128],
                                           ([v] + fr) if j == 0 else ())
                                v = copy(T_[:, 0:L], ps[:, 0:L], [m] + tf, eng=SC, free=True)
                                for j in range(mt + 1):
                                    pvs.append((tm[:, j, 128 * (br - 1):128 * br], T_[:, 128 * j:128 * j + 128], v, ti, ring_))
                            Pb.done(pi, m)
                            yield
                            B.done(bi, v)
                        bi, ps, fr = B.take()
                        for n_, (l, r, v, ti, ring_) in enumerate(pvs):
                            m = mm(ps[:, 0:128], [(l, r)], [v] + (fr if n_ == 0 else []), start=n_ == 0,
                                   stop=n_ == len(pvs) - 1)
                            ring_.done(ti, m)
                        c_ = slice(128 * mt, 128 * mt + 128)
                        a = copy(hh[:, 4 + h, c_], ps[:, 0:128], [m], eng=SC, free=True)
                        B.done(bi, tt(hl[:, 4 + h, c_], ps[:, 0:128], hh[:, 4 + h, c_].bitcast(F32), S_, [a], free=True))
                        yield

            def both():
                yield from gdn()
                yield from gdn_out()

            row = sb("modrow2", [1, 2, 256], F32, a2)
            together((both(), 3), (attention(), 4), (modulation(8, 24, row), 0.4))
            v = stt(scl[:, 8:16], modc[:, 32:40], 1.0, cc["norm2"], A_, M)
            if dump("mixed", hh[:, :, :].bitcast(F32)):
                return endit()
            Q.barrier()

    free0 = Q.last(PE, SC, VE, GP)
    with ExitStack() as ar:
        xT, k1 = load("x1", ar, D["xT"], free0)
        Q.hold[VE] += [k1]

        def res1(gate):
            def f(n, ps, m):
                return stt(xT[:, n, :], ps[:, :], modc[:, gate + n:gate + n + 1], xT[:, n, :], M, A_, [m], free=True)
            return f

        linear("wout1", 8, 2, 8, hk, res1(16))
        if dump("x1", xT[:, :, :]):
            return endit()
        Q.barrier()
        with ExitStack() as a2:
            hready = norm_to(xT, None, scl[:, 8:16], a2, modc[:, 24:32])
            Q.barrier()
        ffh = sb("ffh", [128, 11, 512], R32, ar)
        ffl = sb("ffl", [128, 11, 512], R32, ar)
        cv = Slots([sb(f"fcv{j}", [128, 512], F32, ar) for j in range(6)])

        def ffn(half, war):
            def f_(n, ps, m):
                ci, c, f = cv.take()
                w = cc["fconv"][:, 4 * (n + 22 * half):4 * (n + 22 * half) + 4]
                ts(c[:, :], ps[:, :], w[:, 2:3], M, w[:, 3:4], A_, w=[m] + f)
                stt(c[:, 1:512], ps[:, 0:511], w[:, 1:2], c[:, 1:512], M, A_)
                v = stt(c[:, 2:512], ps[:, 0:510], w[:, 0:1], c[:, 2:512], M, A_)
                if n % 2 == 0:
                    a = act(c[:, :], c[:, :], ACT.Silu, [v], free=True)
                    ffa[0] = (ci, c, a)
                else:
                    ai, ca, a = ffa[0]
                    v2 = tt(c[:, :], ca[:, :], c[:, :], M, [a])
                    cv.done(ai, v2)
                    cv.done(ci, split(ffh[:, n // 2, :], ffl[:, n // 2, :], c[:, :], [v2] + war, eng=GP, f=True))
                return v
            return f_

        ffa = {}
        for half in range(2):
            linear("wup", 22, 2, 8, hk, ffn(half, Q.last(PE) if half else []), [hready], s0=11 * half)
            linear("wdn", 8, 1, 11, lambda k: (ffh[:, k, :], ffl[:, k, :]), res1(40), Q.last(GP), s0=8 * half)
        if dump("x2", xT[:, :, :]):
            return endit()
        Q.barrier()
        hready = norm_to(xT, mT, cc["lnmix"], ar)
        xsp = Q.dma(SY, "xsp", xd_, xT[:, :, :], Q.last(VE))
        Q.barrier([xsp])
    with ExitStack() as ar:
        qk = sb("qk", [128, 8, 512], F32, ar)
        oT = sb("oT", [128, 8, 512], F32, ar)
        am = ar.enter_context(ExitStack())
        km = sb("km", [128, 4, 16], F32, am)
        glo = sb("glo", [16, 528], F32, am)
        vt = sb("vt", [128, 4, 1024], F32, am)
        vm = sb("vm", [16, 1024], F32, am)
        G = sb("G", [128, 4, 512], F32, am)
        lt = oT[:, 0:4, :].rearrange("p a b -> p (a b)")
        g2w = sb("g2w", [16, 512], F32, am)
        k2 = Q.dma(SY, "g2w", g2w[:, :], D["gate2w"], Q.last(PE, SC, VE, GP))
        Gm = sb("Gm", [128, 4, 16], F32, am)
        msk = sb("msk", [128, 1024], U32, am)
        kmsk = Q.dma(SY, "msk", msk[:, :], D["masks"], Q.last(PE, SC, VE, GP))

        def take_qk(n, ps, m, meta):
            if meta:
                return copy(km[:, n - 4, :], ps[:, 0:16], [m]) if n >= 4 else None
            if n < 4:
                return act(qk[:, n, :], ps[:, :], ACT.Copy, [m], free=True, scale=128 ** -0.5)
            return copy(qk[:, n, :], ps[:, :], [m], free=True)

        linear("qk2", 8, 2, 8, hk, take_qk, first=4)
        i, (h_, l_), t = slot("glow", 0)
        vh, vl = (x[:, 0:1024].rearrange("p (k n) -> p k n", k=8) for x in (h_, l_))
        bi, ps, fr = B.take()
        m = mm3(ps[:, :], [((vh[:, k, :], vl[:, k, :]), hk(k)) for k in range(8)], t + fr)
        B.done(bi, copy(glo[:, 0:512], ps[0:16, :], [m]))
        bi, ps, fr = B.take()
        m = mm3(ps[:, 0:16], [((vh[:, k, :], vl[:, k, :]), mk(k)) for k in range(8)], fr)
        glt = copy(glo[:, 512:528], ps[0:16, 0:16], [m])
        B.done(bi, glt)
        release(i, m)
        for h in range(4):
            bi, ps, fr = B.take()
            m = mm(ps[:, :], [(g2w[:, 128 * h:128 * h + 128], glo[:, 0:512])], [glt, k2] + fr)
            v = ts(G[:, h, :], ps[:, :], cc["bgate"][:, h:h + 1], A_, w=[m])
            B.done(bi, v)
            bi, ps, fr = B.take()
            m = mm(ps[:, 0:16], [(g2w[:, 128 * h:128 * h + 128], glo[:, 512:528])], fr)
            gz_ = ts(Gm[:, h, :], ps[:, 0:16], cc["bgate"][:, h:h + 1], A_, w=[m])
            B.done(bi, gz_)
        vmf = lt[:, 0:128].rearrange("p (a n) -> p a n", a=8)
        for s in range(4):
            i, (h_, l_), t = slot("v2", s)
            vh, vl = (x[:, :].rearrange("p (k n) -> p k n", k=8) for x in (h_, l_))
            for j in range(4):
                bi, ps, fr = B.take()
                m = mm3(ps[:, 0:256], [(hkt(k, j), (vh[:, k, :], vl[:, k, :])) for k in range(8)], t + fr)
                B.done(bi, copy(vt[:, j, 256 * s:256 * s + 256], ps[:, 0:256], [m], eng=SC, free=True))
            for c in range(2):
                bi, ps, fr = B.take()
                cs = slice(128 * c, 128 * c + 128)
                m = mm3(ps[:, 0:16], [((vh[:, k, cs], vl[:, k, cs]), mk(k)) for k in range(8)], fr)
                v = copy(vmf[:, 2 * s + c, :], ps[:, 0:16], [m])
                B.done(bi, v)
            release(i, m)
        for c in range(2):
            bi, ps, fr = B.take()
            for x in range(4):
                m = tr(ps[0:16, 128 * x:128 * x + 128], vmf[:, 4 * c + x, :], [v] + fr)
            B.done(bi, copy(vm[:, 512 * c:512 * c + 512], ps[0:16, :], [m]))
        Q.barrier()
        with ExitStack() as a2:
            for z_, n_, first in ((G[:, :, :].rearrange("p a b -> p (a b)"), 2048, True),
                                  (Gm[:, :, :].rearrange("p a b -> p (a b)"), 64, False)):
                l_ = lt[:, 0:n_]
                act(l_, z_, ACT.Abs, [gz_] + Q.last(VE))
                act(l_, l_, ACT.Exp, scale=-1.0)
                a = act(l_, l_, ACT.Ln, bias=1.0)
                v = stt(z_, z_, 0.0, l_, ALU.min, S_, [a])
                v = ts(z_, z_, 1 / 16, M)
            for h in range(4):
                Q.add(VE, lambda e, h=h: e.tensor_tensor_scan(lt[:, 512 * h:512 * h + 512], C["notfirst"],
                                                              G[:, h, :], 0.0, M, A_), free=h > 0)
            for h in range(4):
                v = Q.add(VE, lambda e, h=h: e.tensor_tensor_scan(Gm[:, h, :], C["ones"][:, 0:16],
                                                                  Gm[:, h, :], 0.0, M, A_), free=h > 0)
            copy(G[:, :, :].rearrange("p a b -> p (a b)"), lt[:, :])
            Q.barrier()
        with ExitStack() as a2:
            names = ("eG", "eN", "qe", "qn", "ke", "kn")
            Es = {n_: [sb(f"gl_{n_}{j}", [128, 512], F32, a2) for j in range(2 if n_ in ("qe",) else 1)]
                  for n_ in names}
            kdt = sb("kdt", [128, 2, 512], F32, a2)
            att = Es["eG"][0]
            kdm = sb("kdm", [128, 16], F32, a2)
            kdmt = sb("kdmt", [16, 128], F32, a2)
            S = sb("Sg", [128, 8, 256], F32, a2)
            gl = sb("glg", [128, 8], F32, a2)
            qe0 = kn0 = None
            for h in range(4):
                Gh = G[:, h, :]
                qh, kh = qk[:, h, :], qk[:, 4 + h, :]
                E = {n_: Es[n_][0] for n_ in names}
                prev = Q.last(PE, VE)
                act(E["eG"][:, :], Gh, ACT.Exp, prev)
                a = act(E["eN"][:, :], Gh, ACT.Exp, scale=-1.0, free=True)
                tt(E["qe"][:, :], qh, E["eG"][:, :], M, [a] + prev)
                tt(E["qn"][:, :], qh, E["eN"][:, :], M, free=True)
                tt(E["ke"][:, :], kh, E["eG"][:, :], M, free=True)
                v1 = tt(E["kn"][:, :], kh, E["eN"][:, :], M, free=True)
                g3 = Gh.rearrange("p (c t) -> p c t", c=8)
                e3 = E["eG"][:, :].rearrange("p (c t) -> p c t", c=8)
                copy(gl[:, :].unsqueeze(2), e3[:, :, 63:64])
                v = tt(E["eN"][:, :].rearrange("p (c t) -> p c t", c=8), g3[:, :, 63:64].to_broadcast([128, 8, 64]),
                       g3, S_)
                a = act(E["eN"][:, :], E["eN"][:, :], ACT.Exp, [v])
                v = tt(E["eN"][:, :], E["eN"][:, :], kh, M, [a])
                vmt = ts(kdm[:, :], Gm[:, h, :], Gm[:, h, 15:16], S_, -1.0, M)
                a = act(kdm[:, :], kdm[:, :], ACT.Exp, [vmt])
                vmt = tt(kdm[:, :], kdm[:, :], km[:, h, :], M, [a])
                bi, ps, fr = B.take()
                m = tr(ps[0:16, 0:128], kdm[:, :], [vmt] + fr)
                c_ = copy(kdmt[:, :], ps[0:16, 0:128], [m])
                B.done(bi, c_)
                bi, ps, fr = B.take()
                m = mm(ps[:, 0:256], [(kdmt[:, :], vm[:, 256 * h:256 * h + 256])], [c_] + fr)
                B.done(bi, copy(S[:, 0, :], ps[:, 0:256], [m]))
                bi, ps, fr = B.take()
                for j in range(4):
                    m = tr(ps[:, 128 * j:128 * j + 128], E["eN"][:, 128 * j:128 * j + 128],
                           ([v] + fr) if j == 0 else ())
                ts(kdt[:, 0, :], ps[:, :], C["col01"][:, 0:1], M, w=[m])
                v = ts(kdt[:, 1, :], ps[:, :], C["col01"][:, 1:2], M, free=True)
                B.done(bi, v)
                b1, p1, f1 = B.take()
                b2, p2, f2 = B.take()
                for j in range(4):
                    c = slice(128 * j, 128 * j + 128)
                    mm(p1[:, c], [(E["kn"][:, c], E["qe"][:, c])], [v1] + f1, start=j == 0, check=False)
                    m = mm(p2[:, c], [(E["ke"][:, c], E["qn"][:, c])], f2, start=j == 0, check=False)
                Q.add(VE, lambda e: e.memset(att[:, :], 0.0))
                Q.add(VE, lambda e, p1=p1: e.copy_predicated(att[:, :], msk[:, 0:512], p1[:, :]), [m, kmsk])
                va = Q.add(VE, lambda e, p2=p2: e.copy_predicated(att[:, :], msk[:, 512:1024], p2[:, :]))
                B.done(b1, va)
                B.done(b2, va)
                for c2 in range(4):
                    bi, ps, fr = B.take()
                    for c in range(2 * c2, min(2 * c2 + 2, 7)):
                        m = mm(ps[:, 256 * (c % 2):256 * (c % 2) + 256],
                               [(kdt[:, c % 2, 128 * c2:128 * c2 + 128], vt[:, c2, 256 * h:256 * h + 256])],
                               [v] + fr, start=c % 2 == 0, check=False)
                    for c in range(2 * c2, min(2 * c2 + 2, 7)):
                        vs = stt(S[:, c + 1, :], S[:, c, :], gl[:, c:c + 1], ps[:, 256 * (c % 2):256 * (c % 2) + 256],
                                 M, A_, [m])
                    B.done(bi, vs)
                for dv in range(2):
                    bi, ps, fr = B.take()
                    for j in range(4):
                        m = mm(ps[:, 128 * j:128 * j + 128],
                               [(vt[:, j, 256 * h + 128 * dv:256 * h + 128 * dv + 128],
                                 att[:, 128 * j:128 * j + 128])], [va] + fr, start=j == 0, stop=False, check=False)
                    for c in range(8):
                        m = mm(ps[:, 64 * c:64 * c + 64], [(S[:, c, 128 * dv:128 * dv + 128],
                                                            E["qe"][:, 64 * c:64 * c + 64])], [vs],
                               start=False, check=False)
                    B.done(bi, copy(oT[:, 2 * h + dv, :], ps[:, :], [m], eng=SC))
            Q.barrier()
        with ExitStack() as a2:
            sq = Slots([sb(f"osq{j}", [128, 512], F32, a2) for j in range(2)])
            rr = [sb(f"orr{j}", [128, 512], F32, a2) for j in range(2)]
            sg = Slots([sb(f"osg{j}", [128, 512], F32, a2) for j in range(2)])
            for h in range(4):
                bi, ps, fr = B.take()
                for dv in range(2):
                    si, s, f = sq.take()
                    a = act(s[:, :], oT[:, 2 * h + dv, :], ACT.Square, f, free=True)
                    m = mm(ps[:, :], [(C["ones"], s[:, :])], [a] + fr, start=dv == 0, stop=dv == 1)
                    sq.done(si, m)
                r = rr[h % 2]
                ts(r[:, :], ps[:, :], 1 / 256, M, EPS, A_, w=[m])
                v = recip(r[:, :], r[:, :])
                B.done(bi, v)
                a = act(r[:, :], r[:, :], ACT.Sqrt, [v])
                for dv in range(2):
                    o_ = oT[:, 2 * h + dv, :]
                    stt(o_, o_, cc["glan"][:, dv:dv + 1], r[:, :], M, M, [a], free=dv > 0)

            def take_g(n, ps, m):
                si, s, f = sg.take()
                a = act(s[:, :], ps[:, :], ACT.Silu, [m] + f, free=True)
                sg.done(si, tt(oT[:, n, :], oT[:, n, :], s[:, :], M, [a]))
                return a

            linear("gout2", 8, 2, 8, hk, take_g)
            if dump("oT", oT[:, :, :]):
                return endit()
            ya = qk
            linear("gatea", 8, 2, 8, hk, lambda n, ps, m: act(ya[:, n, :], ps[:, :], ACT.Sigmoid, [m], free=True))
        am.close()
        with ExitStack() as a2:
            Q.barrier()
            oh = sb("oh", [128, 4, 512], R32, a2)
            ol = sb("ol", [128, 4, 512], R32, a2)
            o2h = sb("o2h", [128, 4, 512], R32, a2)
            o2l = sb("o2l", [128, 4, 512], R32, a2)
            for k in range(8):
                r = split((oh if k < 4 else o2h)[:, k % 4, :], (ol if k < 4 else o2l)[:, k % 4, :], oT[:, k, :],
                          eng=VE, f=k > 0)
            linear("upgla", 8, 2, 8, lambda k: ((oh if k < 4 else o2h)[:, k % 4, :], (ol if k < 4 else o2l)[:, k % 4, :]),
                   lambda n, ps, m: tt(ya[:, n, :], ya[:, n, :], ps[:, :], M, [m] + Q.last(SC)), [r])
            ysp = Q.dma(SY, "ysp", yd_, ya[:, :, :], Q.last(VE))
            Q.barrier([ysp])

    with ExitStack() as ar:
        yT = sb("yT", [128, 16, 512], F32, ar)
        with ExitStack() as a2:
            dtt = sb("dtt", [128, 5, 32], F32, a2)
            av = sb("av", [128, 5, 32], F32, a2)
            ac = sb("ac", [128, 5, 32], F32, a2)
            dtx = sb("dtx", [128, 5, 32], F32, a2)
            te = sb("te", [128, 9, 32], F32, a2)
            al2 = sb("al2", [128, 4, 64], F32, a2)
            eal = sb("eal", [128, 8, 32], F32, a2)
            eac = sb("eac", [128, 4, 32], F32, a2)
            i, (h_, l_), t = slot("dt2", 0)
            wdh, wdl = (x[:, 0:256].rearrange("p (k n) -> p k n", k=8) for x in (h_, l_))
            z0 = Q.add(VE, lambda e: e.memset(dtt[:, 4, :], 0.0))
            z0 = Q.add(VE, lambda e: e.memset(av[:, 4, :], 0.0))
            bi, ps, fr = B.take()
            for j in range(4):
                m = mm3(ps[:, 32 * j:32 * j + 32], [(hkt(k, j), (wdh[:, k, :], wdl[:, k, :])) for k in range(8)],
                        t + fr, start=j == 0, check=False)
            lst = []
            for k in range(8):
                for a_ in mk(k):
                    for w_ in (wdh, wdl):
                        lst.append((a_.bitcast(F32), w_[:, k, :].bitcast(F32)))
            m = mm(ps[0:16, 128:160], lst, start=False, check=False)
            release(i, m)
            v = tt(dtt[:, 0:4, :], ps[:, 0:128].rearrange("p (a b) -> p a b", a=4), rep(cc["dtb2"], 4), A_, [m])
            v = tt(dtt[0:16, 4, :], ps[0:16, 128:160], cc["dtb2"][0:16, :], A_)
            B.done(bi, v)
            act(dtx[:, :, :], dtt[:, :, :], ACT.Abs, [v])
            act(dtx[:, :, :], dtx[:, :, :], ACT.Exp, scale=-1.0)
            a = act(dtx[:, :, :], dtx[:, :, :], ACT.Ln, bias=1.0)
            a = act(eac[:, 0, :], cc["alog2"], ACT.Exp)
            stt(dtt[:, :, :], dtt[:, :, :], 0.0, dtx[:, :, :], ALU.max, A_, [a])
            ts(eac[:, 1, :], eac[:, 0, :], -1.0, M)
            tt(av[:, 0:4, :], dtt[:, 0:4, :], rep(eac[:, 1, :], 4), M)
            tt(av[0:16, 4, :], dtt[0:16, 4, :], eac[0:16, 1, :], M)
            ts(al2[:, :, 0:32], av[:, 0:4, :], C["col01"][:, 0:1], M, free=False)
            v = ts(al2[:, :, 32:64], av[:, 0:4, :], C["col01"][:, 1:2], M)
            bi, ps, fr = B.take()
            avf = av[:, :, :].rearrange("p a b -> p (a b)")
            m = mm(ps[:, 0:160], [(C["cum64"], avf)], [v] + fr, check=False)
            m = mm(ps[:, 160:320], [(C["same64"], avf)], check=False, start=False)
            v = copy(ac[:, :, :].rearrange("p a b -> p (a b)"), ps[:, 0:160], [m])
            v = tt(dtx[:, :, :].rearrange("p a b -> p (a b)"), ps[:, 160:320],
                   ac[:, :, :].rearrange("p a b -> p (a b)"), S_)
            B.done(bi, v)
            act(dtx[:, :, :], dtx[:, :, :], ACT.Exp, [v])
            a = act(eac[:, :, :], ac[:, 0:4, :], ACT.Exp)
            tt(dtx[:, :, :], dtx[:, :, :], dtt[:, :, :], M, [a])
            t8 = te[:, 0:8, :].rearrange("p (m c) h -> p m c h", c=2)
            ts(t8[:, :, 0, :], dtx[:, 0:4, :], C["col01"][:, 0:1], M)
            ts(t8[:, :, 1, :], dtx[:, 0:4, :], C["col01"][:, 1:2], M)
            v = copy(te[:, 8, :], dtx[:, 4, :])
            bi, ps, fr = B.take()
            m = mm(ps[:, 0:256], [(C["ones"], al2[:, :, :].rearrange("p a b -> p (a b)"))], fr)
            a = act(eal[:, :, :].rearrange("p a b -> p (a b)"), ps[:, 0:256], ACT.Exp, [m])
            B.done(bi, a)

            raw = Slots([sb(f"raw{j}", [128, 532], F32, a2) for j in range(2)])
            for r in raw.bufs:
                rz = Q.add(VE, lambda e, r=r: e.memset(r[:, 0:3], 0.0))
            cvo = Slots([sb(f"cvo{j}", [128, 528], F32, a2) for j in range(2)])
            xsg = sb("xsg", [128, 5, 512], F32, a2)
            BT_ = sb("BTg", [128, 528], F32, a2)
            CT_ = sb("CTg", [128, 528], F32, a2)
            CTm = sb("CTm", [128, 2, 512], F32, a2)
            Bt = sb("Bt", [128, 5, 128], F32, a2)
            cb = sb("cb", [128, 4, 128], F32, a2)
            yz = sb("yz", [128, 4, 512], F32, a2)
            zg = yz
            SS = Slots([sb(f"SS{j}", [128, 512], F32, a2) for j in range(2)])
            xd = sb("xd", [128, 512], F32, a2)
            xe = Slots([sb(f"xe{j}", [128, 512], F32, a2) for j in range(2)])
            sg = sb("sgm", [128, 8, 128], F32, a2)
            zt = sb("zt", [128, 512], F32, a2)
            yt = sb("yt", [128, 512], F32, a2)
            y2 = zt
            ms = sb("ms", [128, 4], F32, a2)

            def b8(ap, n=64):
                return bc(ap, n)

            cz = Q.add(VE, lambda e: e.memset(CTm[:, :, :], 0.0))
            for g in range(4):
                hs = slice(8 * g, 8 * g + 8)

                def conv_out(tile_no, dst):
                    st8 = {}

                    def take(n, ps, m, meta):
                        if meta:
                            ri, r, f = raw.take()
                            st8["r"] = (ri, r)
                            return copy(r[:, 3:19], ps[:, 0:16], [m, rz] + f, eng=SC, free=True)
                        ri, r = st8["r"]
                        a = copy(r[:, 19:531], ps[:, :], [m], eng=SC, free=True)
                        tn = tile_no(n)
                        w = cc["conv2"][:, 5 * tn:5 * tn + 5]
                        o_, dn = dst(n)
                        ts(o_[:, 0:528], r[:, 3:531], w[:, 3:4], M, w[:, 4:5], A_, w=[a] + dn)
                        for d in (1, 2, 3):
                            v = stt(o_[:, 0:528], r[:, 3 - d:531 - d], w[:, 3 - d:4 - d], o_[:, 0:528], M, A_)
                        raw.done(ri, v)
                        act(o_[:, 0:528], o_[:, 0:528], ACT.Silu, [v], free=True)
                        return a
                    return take

                cur = {}

                def xs_dst(n):
                    ci, c, f = cvo.take()
                    cur["c"] = (ci, c)
                    return c, f

                base = conv_out(lambda n: 4 * g + n, xs_dst)

                def xs_take(n, ps, m, meta):
                    r = base(n, ps, m, meta)
                    if meta:
                        return r
                    ci, c = cur["c"]
                    sil = Q.last(SC)
                    bi, pt, fr = B.take()
                    for j in range(4):
                        mt_ = tr(pt[:, 128 * j:128 * j + 128], c[:, 16 + 128 * j:144 + 128 * j],
                                 (sil + fr) if j == 0 else ())
                    v = copy(xsg[:, 0:4, 128 * n:128 * n + 128], pt[:, :].rearrange("p (a b) -> p a b", a=4),
                             [mt_] + gprev)
                    B.done(bi, v)
                    bi, pt, fr = B.take()
                    mt_ = tr(pt[0:16, 0:128], c[:, 0:16], fr)
                    v = copy(xsg[0:16, 4, 128 * n:128 * n + 128], pt[0:16, 0:128], [mt_])
                    B.done(bi, v)
                    cvo.done(ci, mt_)
                    return r

                gprev = Q.last(PE, VE, GP)
                linear("xs2", 4, 2, 8, hk, xs_take, first=0, s0=2 * g)
                linear("bc2", 2, 2, 8, hk, conv_out(lambda n: (16 if n == 0 else 20) + g,
                                                    lambda n: (BT_ if n == 0 else CT_, gprev)), first=0, s0=g)
                sil = Q.last(SC)
                for q_ in range(2):
                    half = lambda ap: ap.rearrange("p (m c t) -> p m c t", m=4, c=2)[:, :, q_, :]
                    vct = copy(half(CTm[:, q_, :]), half(CT_[:, 16:528]), sil + gprev + [cz])
                bi, ps, fr = B.take()
                for j in range(4):
                    m = tr(ps[:, 128 * j:128 * j + 128], BT_[:, 16 + 128 * j:144 + 128 * j], (sil + fr) if j == 0 else ())
                v = copy(Bt[:, 0:4, :], ps[:, :].rearrange("p (a b) -> p a b", a=4), [m])
                B.done(bi, v)
                bi, ps, fr = B.take()
                m = tr(ps[0:16, 0:128], BT_[:, 0:16], fr)
                v = copy(Bt[0:16, 4, :], ps[0:16, 0:128], [m])
                B.done(bi, v)
                bi, ps, fr = B.take()
                for j in range(4):
                    c = slice(16 + 128 * j, 144 + 128 * j)
                    m = mm(ps[:, 128 * j:128 * j + 128], [(BT_[:, c], CT_[:, c])], fr, start=j == 0, check=False)
                v = tt(cb[:, :, :], ps[:, :].rearrange("p (a b) -> p a b", a=4), rep(C["same64"], 4), M, [m])
                B.done(bi, v)
                x3 = lambda ap: ap.rearrange("p (h d) -> p h d", h=8)
                xi, x_, f = xe.take()
                v = tt(x3(x_[0:16, :]), x3(xsg[0:16, 4, :]), b8(te[0:16, 8, hs]), M, f)
                bi, ps, fr = B.take()
                m = mm(ps[:, :], [(Bt[0:16, 4, :], x_[0:16, :])], [v] + fr)
                xe.done(xi, m)
                s0i, s0, f = SS.take()
                vS = copy(s0[:, :], ps[:, :], [m] + f)
                B.done(bi, vS)
                for c in range(2):
                    iz, (h_, l_), tz = slot("z2", 2 * g + c)
                    vh, vl = (x[:, :].rearrange("p (k n) -> p k n", k=8) for x in (h_, l_))
                    for j in range(4):
                        zb, pz, fr = B.take()
                        mz = mm3(pz[:, 0:256], [(hkt(k, j), (vh[:, k, :], vl[:, k, :])) for k in range(8)], tz + fr)
                        B.done(zb, act(zg[:, j, 256 * c:256 * c + 256], pz[:, 0:256], ACT.Silu, [mz] + gprev, free=True))
                    release(iz, mz)
                zready = Q.last(SC)
                for j in range(4):
                    va = []
                    for q4 in range(2):
                        bi, ps, fr = B.take()
                        for h in range(4):
                            hx = 8 * g + 4 * q4 + h
                            m = mm(ps[:, 128 * h:128 * h + 128],
                                   [(av[:, j, hx:hx + 1].to_broadcast([128, 128]), C["cum64"])], fr,
                                   start=h == 0, check=False)
                        v = tt(sg[:, 4 * q4:4 * q4 + 4, :], ps[:, :].rearrange("p (a b) -> p a b", a=4),
                               bc(ac[:, j, 8 * g + 4 * q4:8 * g + 4 * q4 + 4], 128), S_,
                               [m] + (Q.last(PE) if q4 == 0 else []))
                        B.done(bi, v)
                    act(sg[:, :, :], sg[:, :, :], ACT.Abs, [v])
                    a = act(sg[:, :, :], sg[:, :, :], ACT.Exp, scale=-1.0)
                    v = tt(sg[:, :, :], sg[:, :, :], rep(cb[:, j, :], 8), M, [a])
                    v = tt(x3(xd[:, :]), x3(xsg[:, j, :]), b8(dtt[:, j, hs]), M)
                    yb, py, fr = B.take()
                    for h in range(8):
                        m = mm(py[:, 64 * h:64 * h + 64], [(sg[:, h, :], xd[:, 64 * h:64 * h + 64])], [v] + fr,
                               start=h == 0, check=False)
                    my = m
                    ib, pi_, fr2 = B.take()
                    for cpar in range(2):
                        c = 2 * j + cpar
                        m = mm(pi_[:, :], [(CTm[:, cpar, 128 * j:128 * j + 128], s0[:, :])], [vS, vct] + fr2,
                               start=cpar == 0, stop=cpar == 1)
                        SS.done(s0i, m)
                        if c < 7:
                            xi, x_, f = xe.take()
                            v = tt(x3(x_[:, :]), x3(xsg[:, j, :]), b8(te[:, c, hs]), M, f)
                            bi, ps, fr = B.take()
                            m2 = mm(ps[:, :], [(Bt[:, j, :], x_[:, :])], [v] + fr)
                            xe.done(xi, m2)
                            s1i, s1, f = SS.take()
                            tt(x3(s1[:, :]), x3(s0[:, :]), b8(eal[:, c, hs]), M, f)
                            vS = tt(s1[:, :], s1[:, :], ps[:, :], A_, [m2])
                            B.done(bi, vS)
                            SS.done(s0i, vS)
                            s0i, s0 = s1i, s1
                    v = tt(x3(yt[:, :]), x3(pi_[:, :]), b8(eac[:, j, hs]), M, [m])
                    B.done(ib, v)
                    v = tt(yt[:, :], yt[:, :], py[:, :], A_, [my])
                    B.done(yb, v)
                    tt(x3(y2[:, :]), x3(xsg[:, j, :]), b8(cc["dsk"][:, hs]), M)
                    v = tt(yt[:, :], yt[:, :], y2[:, :], A_)
                    v = tt(yz[:, j, :], yt[:, :], zg[:, j, :], M, zready)
                    a = act(zt[:, :], yz[:, j, :], ACT.Square, [v], accum_out=ms[:, 0:1])
                    ts(ms[:, 1:2], ms[:, 0:1], 1 / 512, M, EPS, A_, w=[a])
                    v = recip(ms[:, 2:3], ms[:, 1:2])
                    a = act(ms[:, 3:4], ms[:, 2:3], ACT.Sqrt, [v])
                    v = ts(yz[:, j, :], yz[:, j, :], ms[:, 3:4], M, w=[a])
                for n_ in range(4):
                    bi, ps, fr = B.take()
                    for j in range(4):
                        m = tr(ps[:, 128 * j:128 * j + 128], yz[:, j, 128 * n_:128 * n_ + 128],
                               ([v] + fr) if j == 0 else ())
                    B.done(bi, act(yT[:, 4 * g + n_, :], ps[:, :], ACT.Copy, [m], free=True,
                                   scale=cc["ssdn"][:, 4 * g + n_:4 * g + n_ + 1]))
            Q.barrier()
        if dump("yn", yT[:, :, :]):
            return endit()
        acc = sb("acc", [128, 8, 512], F32, ar)
        yh = sb("yh", [128, 8, 512], R32, ar)
        yl = sb("yl", [128, 8, 512], R32, ar)
        for half in range(2):
            pe_ = Q.last(PE)
            for k in range(8):
                r = split(yh[:, k, :], yl[:, k, :], yT[:, 8 * half + k, :], pe_, f=True)
            linear("upssd", 8, 2, 8, lambda k: (yh[:, k, :], yl[:, k, :]),
                   (lambda n, ps, m: copy(acc[:, n, :], ps[:, :], [m])) if half == 0 else
                   (lambda n, ps, m: tt(acc[:, n, :], acc[:, n, :], ps[:, :], A_, [m])), [r], s0=4 * half)
        asp = Q.dma(SY, "asp", xa_, acc[:, :, :], Q.last(VE))
        Q.barrier([asp])
    with ExitStack() as ar:
        acc, ka = load("acc2", ar, xa_, Q.last(PE, SC, VE, GP) + [asp])
        ya, ky = load("ya2", ar, yd_, Q.last(PE, SC, VE, GP) + [ysp])
        xT, kx = load("x2", ar, xd_, Q.last(PE, SC, VE, GP) + [xsp])
        gsl = Slots([sb(f"gs{j}", [128, 512], F32, ar) for j in range(2)])
        mh = sb("mh", [128, 8, 512], R32, ar)
        ml = sb("ml", [128, 8, 512], R32, ar)

        def take_b(n, ps, m):
            gi, g_, f = gsl.take()
            a = act(g_[:, :], ps[:, :], ACT.Sigmoid, [m] + f, free=True)
            v = tt(g_[:, :], g_[:, :], acc[:, n, :], M, [a, ka])
            v = tt(g_[:, :], g_[:, :], ya[:, n, :], A_, [ky])
            gsl.done(gi, split(mh[:, n, :], ml[:, n, :], g_[:, :], [v], f=True))
            return a

        linear("gateb", 8, 2, 8, hk, take_b)
        Q.hold[VE] += [kx]
        linear("wout2", 8, 2, 8, lambda k: (mh[:, k, :], ml[:, k, :]),
               lambda n, ps, m: tt(xT[:, n, :], xT[:, n, :], ps[:, :], A_, [m], free=True), Q.last(VE))
        if dump("x3", xT[:, :, :]):
            return endit()
        Q.barrier()
        hready = norm_to(xT, None, cc["lnffn"], ar)
        xsp = Q.dma(SY, "xsp", xd_, xT[:, :, :], Q.last(VE))
        Q.barrier([xsp])

    sd_ = nc.dram_tensor("score_spill", (4, 128, 2048), F32).ap()
    gd_ = nc.dram_tensor("gelu_spill", (64, 128, 2, 512), F32).ap()
    wd_ = nc.dram_tensor("weight_spill", (64, 128, 2, 512), F32).ap()
    with ExitStack() as ar:
        qT = sb("pqT", [128, 16, 512], F32, ar)
        ssg = Slots([sb(f"ssg{j}", [128, 2048], F32, ar) for j in range(2)])
        linear("wq", 16, 2, 8, hk, lambda n, ps, m: copy(qT[:, n, :], ps[:, :], [m], free=True))
        i, buf, t = slot("subk", 0)
        sk = buf[:, 0:2048].rearrange("p (a n) -> p a n", a=16)
        for j in range(4):
            gi, g_, f = ssg.take()
            for q4 in range(4):
                bi, ps, fr = B.take()
                for a_ in range(4):
                    n_ = 4 * q4 + a_
                    m = mm(ps[:, 128 * a_:128 * a_ + 128], [(qT[:, n_, 128 * j:128 * j + 128], sk[:, n_, :])],
                           t + Q.last(VE) + fr, start=a_ == 0, check=False)
                c_ = copy(g_[:, 512 * q4:512 * q4 + 512], ps[:, :], [m] + f, eng=SC, free=True)
                B.done(bi, c_)
            ssp = Q.dma(SY, f"ssp{j}", sd_[j], g_[:, :], [c_])
            ssg.done(gi, ssp)
            if j == 0:
                sdone = []
            sdone.append(ssp)
        release(i, m)
        Q.barrier(sdone)

    with ExitStack() as ar:
        stage = sb("stage", [128, 128, 128], F32, ar)
        s_ = sb("s_", [128, 16, 128], F32, ar)
        sr = sb("sr", [128, 256], F32, ar)
        top = sb("top", [128, 16, 16], F32, ar)
        tix = sb("tix", [128, 16, 16], U32, ar)
        tif = top
        cand = sb("cand", [128, 8, 256], F32, ar)
        best = sb("best", [128, 8, 16], F32, ar)
        pix = sb("pix", [128, 8, 16], U32, ar)
        pa = sb("pa", [128, 8, 16], U32, ar)
        paf = sb("paf", [128, 2, 128], F32, ar)
        eq = s_[:, :, :].rearrange("p (h x) k -> p h (x k)", h=8)
        sel = sb("sel", [128, 3, 128], F32, ar)
        ijw = sb("ijw", [128, 3, 128], F32, ar)
        red8 = sb("red8", [128, 2, 8], F32, ar)
        AB = Slots([sb(f"AB{j}", [128, 2, 2, 128], F32, ar) for j in range(2)])
        gst = Slots([sb(f"gst{j}", [128, 512], F32, ar) for j in range(2)])

        def top16(vals, idx, src, scratch, w=()):
            Q.add(VE, lambda e: e.max(vals[:, 0:8], src), w)
            Q.add(VE, lambda e: e.max_index(idx[:, 0:8], vals[:, 0:8], src))
            Q.add(VE, lambda e: e.match_replace(scratch, vals[:, 0:8], src, -3e38))
            Q.add(VE, lambda e: e.max(vals[:, 8:16], scratch))
            Q.add(VE, lambda e: e.max_index(idx[:, 8:16], vals[:, 8:16], scratch))

        def choose():
            wout = None
            for j in range(4):
                ls = Q.dma(SY, "sload", s_[:, :, :], sd_[j].rearrange("p (a b) -> p a b", a=16), Q.last(VE))
                for n_ in range(16):
                    top16(top[:, n_, :], tix[:, n_, :], s_[:, n_, :], sr[:, 0:128], [ls])
                    if n_ % 2:
                        yield
                for h in range(8):
                    tt(cand[:, h, :].rearrange("p (a b) -> p a b", a=16), bc(top[:, 2 * h, :], 16),
                       rep(top[:, 2 * h + 1, :], 16), A_, free=h > 0)
                copy(tif[:, :, :], tix[:, :, :])
                yield
                for h in range(8):
                    top16(best[:, h, :], pix[:, h, :], cand[:, h, :], sr[:, :])
                    yield
                ts(pa[:, :, :], pix[:, :, :], 4, ALU.logical_shift_right)
                copy(paf[:, 0, :], pa[:, :, :].rearrange("p a b -> p (a b)"))
                ts(pa[:, :, :], pix[:, :, :], 15, ALU.bitwise_and)
                copy(paf[:, 1, :], pa[:, :, :].rearrange("p a b -> p (a b)"))
                yield
                for c in range(2):
                    for h in range(8):
                        e3 = eq[:, h, :].rearrange("p (k a) -> p k a", k=16)
                        tt(e3, bc(paf[:, c, 16 * h:16 * h + 16], 16), rep(C["iota"][:, 0:16], 16), ALU.is_equal,
                           free=h > 0)
                    yield
                    for h in range(8):
                        e3 = eq[:, h, :].rearrange("p (k a) -> p k a", k=16)
                        tt(e3, e3, rep(tif[:, 2 * h + c, :], 16), M, free=h > 0)
                    yield
                    red(sel[:, c, :], eq[:, :, :].rearrange("p h (k a) -> p (h k) a", a=16), A_,
                        w=Q.last(PE) if c == 0 else ())
                    yield
                w3 = sel[:, 2, :].rearrange("p (h k) -> p h k", h=8)
                v = tt(w3, best[:, :, :], best[:, :, 0:1].to_broadcast([128, 8, 16]), S_)
                a = act(w3, w3, ACT.Exp, [v])
                red(red8[:, 0, :], w3, A_, w=[a])
                recip(red8[:, 1, :], red8[:, 0, :])
                v = tt(w3, w3, bc(red8[:, 1, :], 16), M)
                yield
                yield
                bi, ps, fr = B.take()
                for c in range(3):
                    m = tr(ps[:, 128 * c:128 * c + 128], sel[:, c, :], ([v] + fr) if c == 0 else ())
                v = copy(ijw[:, :, :], ps[:, 0:384].rearrange("p (a b) -> p a b", a=3), [m])
                B.done(bi, v)
                late = None
                for t0 in range(0, 128, 4):
                    new = []
                    for x in range(2):
                        ai, ab, f = AB.take()
                        for y in range(2):
                            tok = t0 + 2 * x + y
                            ts(ab[:, y, 0, :], C["iota"], ijw[:, 0, tok:tok + 1], ALU.is_equal,
                               ijw[:, 2, tok:tok + 1], M, w=[v] + f, free=True)
                            vb_ = ts(ab[:, y, 1, :], C["iota"], ijw[:, 1, tok:tok + 1], ALU.is_equal, free=True)
                        new.append((ai, ab, vb_))
                        if x == 0:
                            bi, ps, fr = B.take()
                        for y in range(2):
                            q_ = 2 * x + y
                            m = mm(ps[:, 128 * q_:128 * q_ + 128], [(ab[:, y, 0, :], ab[:, y, 1, :])], [vb_] + fr,
                                   start=q_ == 0, check=False)
                        AB.done(ai, m)
                    a = act(stage[:, :, t0:t0 + 4].rearrange("p j t -> p t j"),
                            ps[:, :].rearrange("p (t j) -> p t j", t=4), ACT.Copy,
                            [m] + ([wout] if wout else []), free=True)
                    B.done(bi, a)
                    yield
                for q4 in range(4):
                    for x in range(2):
                        wout = Q.dma(SY, "wst", wd_[16 * q4:16 * q4 + 16, :, x, 128 * j:128 * j + 128].rearrange(
                            "jp i t -> i jp t"), stage[:, 32 * q4 + x:32 * q4 + 32:2, :], [a])
            wlast.append(wout)

        wlast = []
        side = choose()
        for s in range(64):
            i, (h_, l_), t = slot("u", s)
            vh, vl = (x[:, :].rearrange("p (x k n) -> p x k n", x=2, k=8) for x in (h_, l_))
            for x in range(2):
                bi, ps, fr = B.take()
                mm3(ps[:, :], [((vh[:, x, k, :], vl[:, x, k, :]), hk(k)) for k in range(4)], t + fr, stop=False)
                next(side, None)
                m = mm3(ps[:, :], [((vh[:, x, k, :], vl[:, x, k, :]), hk(k)) for k in range(4, 8)], start=False)
                if x == 1:
                    release(i, m)
                gi, g_, f = gst.take()
                a = act(g_[:, :], ps[:, :], ACT.Gelu_apprx_tanh, [m] + f, free=True)
                B.done(bi, a)
                gt_ = Q.dma(SY, f"gst{gi}", gd_[s][:, x, :], g_[:, :], [a])
                gst.done(gi, gt_)
                if 2 * s + x >= 126:
                    wlast.append(gt_)
                next(side, None)
        for _ in side:
            pass
        Q.barrier(wlast)

    with ExitStack() as ar:
        xT, kx = load("x3", ar, xd_, Q.last(PE, SC, VE, GP) + wlast + [xsp])
        gw = Slots([(sb(f"gv{j}", [128, 2, 512], F32, ar), sb(f"wv{j}", [128, 2, 512], F32, ar)) for j in range(3)])
        Pm = Slots([(sb(f"ph{j}", [128, 2, 512], R32, ar), sb(f"pl{j}", [128, 2, 512], R32, ar)) for j in range(2)])
        sums = []
        for d in range(8):
            sums.append(B.take())
        started = Q.last(PE, SC, VE, GP) + wlast
        gq = []

        def fetch(s):
            wi, (g_, w_), f = gw.take()
            ta = Q.dma(SY, f"gv{wi}", g_[:, :, :], gd_[s], (f or started))
            ta = Q.dma(SY, f"gv{wi}", w_[:, :, :], wd_[s])
            gq.append((wi, g_, w_, ta))

        def multiply():
            wi, g_, w_, ta = gq.pop(0)
            pi, (ph, pl), f = Pm.take()
            v = tt(g_[:, :, :], g_[:, :, :], w_[:, :, :], M, [ta] + f, free=True)
            a = act(ph[:, :, :], g_[:, :, :], ACT.Copy, [v], free=True)
            v = tt(pl[:, :, :], g_[:, :, :], ph[:, :, :].bitcast(F32), S_, [a], free=True)
            gw.done(wi, v)
            return pi, ph, pl, v

        for s in range(3):
            fetch(s)
        nxt = multiply()
        for s in range(64):
            pi, ph, pl, pv = nxt
            i, (h_, l_), t = slot("v", s)
            if s < 63:
                nxt = multiply()
            if s + 3 < 64:
                fetch(s + 3)
            for d in range(8):
                bi, ps, fr = sums[d]
                m = mm3(ps[:, :], [((h_[:, 1024 * x + 128 * d:1024 * x + 128 * d + 128],
                                     l_[:, 1024 * x + 128 * d:1024 * x + 128 * d + 128]),
                                    (ph[:, x, :], pl[:, x, :])) for x in range(2)],
                        t + [pv] + (fr if s == 0 else []), start=s == 0, stop=s == 63)
            release(i, m)
            Pm.done(pi, m)
        for d in range(8):
            bi, ps, _ = sums[d]
            B.done(bi, tt(xT[:, d, :], xT[:, d, :], ps[:, :], A_, [m, kx], free=True))
        Q.barrier()
        fin = sb("fin", [128, 8, 512], F32, ar)
        norm_to(xT, None, cc["lnfin"], ar, out=fin)
        Q.dma(SY, "out", D["out"], fin[:, :, :], Q.last(VE))
        Q.q[SY].append((None, [("out", 16)], None))
    finish()




def _layout(I):
    import numpy as np
    f = {k: np.asarray(v) for k, v in I.items()}
    g = {k: (v[0] if v.shape[0] == 1 else v) for k, v in f.items()}

    def fm(W, per):
        K, N = W.shape
        a = W.reshape(K // 128, 128, N // 128 // per, per, 128)
        return np.ascontiguousarray(a.transpose(2, 1, 3, 0, 4)).reshape(N // 128 // per, 128, -1)

    def tmj(W, n):
        K, N = W.shape
        a = W.reshape(K // 128, 128, N // n, n)
        return np.ascontiguousarray(a.transpose(2, 1, 0, 3)).reshape(N // n, 128, -1)

    def col(v):
        return np.ascontiguousarray(v.reshape(-1, 128).T)

    def row(v):
        return np.ascontiguousarray(np.broadcast_to(v.reshape(1, -1), (128, v.size)))

    o = {}
    w = g["w_in"]
    o["ada"] = tmj(g["ada_w"], 256)
    o["win1"] = fm(np.concatenate([w[:, 0:2048], w[:, 2056:2568], w[:, 2568:2696], w[:, 2696:2824],
                                   w[:, 2824:2952], w[:, 3080:3208]], axis=1), 2)
    o["win1t"] = tmj(np.concatenate([w[:, 2952:3080], w[:, 3208:3336]], axis=1), 256)
    o["win1g"] = tmj(np.concatenate([w[:, 2048:2056], w[:, 3336:3348]], axis=1), 20)
    o["cmpw1"] = np.stack([g[n].reshape(32, 128, 128).transpose(1, 0, 2).reshape(128, 4096)
                           for n in ("cmp_k_w1", "cmp_v_w1")])
    o["cmpw1"] = o["cmpw1"].reshape(2, 128, 2, 2048).transpose(0, 2, 1, 3).reshape(4, 128, 2048)
    o["cmpw2"] = np.concatenate([g["cmp_k_w2"], g["cmp_v_w2"]], axis=1)[None]
    o["wout1"] = fm(g["w_out"], 2)
    up = g["ffn_w_up"].reshape(1024, 2, 22, 128).transpose(0, 2, 1, 3).reshape(1024, 5632)
    o["wup"] = fm(up, 2)
    o["wdn"] = fm(g["ffn_w_down"], 1).reshape(8, 128, 2, 1408).transpose(2, 0, 1, 3).reshape(16, 128, 1408)
    w = g["w_in_2"]
    o["qk2"] = fm(w[:, 0:1024], 2)
    o["v2"] = tmj(w[:, 1024:2048], 256)
    o["gout2"] = fm(w[:, 2048:3072], 2)
    o["glow"] = fm(np.concatenate([w[:, 3072:3088]] * 8, axis=1), 1)
    z, xbc = w[:, 3088:5136], w[:, 5136:8208]
    o["z2"] = tmj(z, 256)
    o["xs2"] = fm(xbc[:, 0:2048], 2)
    bcw = np.stack([xbc[:, 2048:2560].reshape(1024, 4, 128), xbc[:, 2560:3072].reshape(1024, 4, 128)], axis=2)
    o["bc2"] = fm(bcw.reshape(1024, 1024), 2)
    o["dt2"] = tmj(w[:, 8208:8240], 32)
    o["gatea"] = fm(w[:, 8240:9264], 2)
    o["gateb"] = fm(w[:, 9264:10288], 2)
    o["upgla"] = fm(g["w_up_gla_2"], 2)
    o["upssd"] = np.concatenate([fm(g["w_up_ssd_2"][0:1024], 2), fm(g["w_up_ssd_2"][1024:2048], 2)])
    o["wout2"] = fm(g["w_out_2"], 2)
    o["wq"] = fm(g["peer_w_q_2"], 2)
    o["subk"] = np.ascontiguousarray(g["peer_sub_keys_2"].reshape(16, 128, 128).transpose(2, 0, 1)).reshape(1, 128, 2048)
    u = g["peer_u_2"].reshape(128, 128, 8, 128).transpose(1, 3, 2, 0)
    v = g["peer_v_2"].reshape(128, 128, 1024).transpose(1, 0, 2)
    for n, a in (("u", u), ("v", v)):
        a = a.reshape(64, 2, 128, 1024).transpose(0, 2, 1, 3)
        o[n] = np.ascontiguousarray(a).reshape(64, 128, 2048)
    o["gate2w"] = g["gla_w_gate2_2"]
    o["xT"] = np.ascontiguousarray(g["x"].reshape(512, 8, 128).transpose(2, 1, 0))
    o["metaT"] = np.ascontiguousarray(f["meta_tokens_2"].reshape(16, 8, 128).transpose(2, 1, 0))
    parts = [("c", col(g["c"])), ("adab", col(g["ada_b"])), ("norm1", col(g["norm1_w"])),
             ("norm2", col(g["norm2_w"])),
             ("conv1", g["gdn_conv_w"].reshape(4, 12, 128).transpose(2, 1, 0).reshape(128, 48)),
             ("qn", col(g["nsa_q_norm_w"])), ("kslc", col(g["nsa_k_norm_slc"])),
             ("kwin", col(g["nsa_k_norm_win"])), ("kcmpn", col(g["nsa_k_norm_cmp"])),
             ("kpos", g["cmp_k_pos"].T), ("vpos", g["cmp_v_pos"].T),
             ("alog", row(g["gdn_A_log"])), ("dtb1", row(g["gdn_dt_bias"])), ("gdnn", col(g["gdn_out_norm_w"])),
             ("fconv", np.concatenate([g["ffn_conv_w"], g["ffn_conv_b"][None]], 0).reshape(4, 2, 22, 128)
              .transpose(3, 2, 1, 0).reshape(128, 176)),
             ("lnmix", col(g["ln_mix_w_2"])), ("lnffn", col(g["ln_ffn_w_2"])), ("lnfin", col(f["ln_final_w_2"])),
             ("bgate", col(g["gla_b_gate_2"])), ("glan", col(g["gla_norm_w_2"])), ("ssdn", col(g["ssd_norm_w_2"])),
             ("dtb2", row(g["ssd_dt_bias_2"])), ("alog2", row(g["ssd_a_log_2"])), ("dsk", row(g["ssd_d_2"])),
             ("conv2", np.concatenate([g["ssd_conv_w_2"], g["ssd_conv_b_2"][None]], 0).reshape(5, 24, 128)
              .transpose(2, 1, 0).reshape(128, 120))]
    COLS.clear()
    off = 0
    for name, a in parts:
        COLS[name] = (off, a.shape[1])
        off += a.shape[1]
    o["cols"] = np.ascontiguousarray(np.concatenate([a for _, a in parts], axis=1))
    o["consts"] = const_array()
    o["masks"] = mask_array()
    return {k: np.ascontiguousarray(v) for k, v in o.items()}


COLS = {}


def kernel(**inputs):
    import numpy as _np
    import concourse.bacc as _bacc
    from concourse import mybir as _mybir
    from concourse.bass_utils import run_bass_kernel_spmd as _run

    arrays = _layout(inputs)
    nc = _bacc.Bacc("TRN2", target_bir_lowering=False, num_devices=1)
    D = {}
    for name, a in arrays.items():
        D[name] = nc.dram_tensor("in_" + name, a.shape, _mybir.dt.from_np(a.dtype), kind="ExternalInput").ap()
    D["out"] = nc.dram_tensor("out_0", (128, 8, 512), _mybir.dt.float32, kind="ExternalOutput").ap()
    if DBG is not None:
        D["dbg"] = nc.dram_tensor("dbg", (128, 8192), _mybir.dt.float32, kind="ExternalOutput").ap()
    build(nc, D, None)
    r = _run(nc, [{"in_" + k: v for k, v in arrays.items()}], core_ids=[0])
    got = r.results[0]["out_0"]
    return _np.ascontiguousarray(got.transpose(2, 1, 0)).reshape(1, 512, 1024)
```

```python
import concourse.bass as bass
from concourse import mybir
from contextlib import ExitStack

F32 = mybir.dt.float32
R32 = mybir.dt.float32r
U32 = mybir.dt.uint32
ALU = mybir.AluOpType
ACT = mybir.ActivationFunctionType
AX = mybir.AxisListType
PE, SC, VE, GP, SY = "tensor", "scalar", "vector", "gpsimd", "sync"
NEG = -1e30
EPS = 1e-6
DBG = None


class Queues:

    def __init__(self, nc, ctx):
        self.nc, self.ctx = nc, ctx
        self.q = {e: [] for e in (PE, SC, VE, GP, SY)}
        self.hold = {e: [] for e in self.q}
        self.dma_sems = {}
        self.counts = {}

    def add(self, eng, fn, w=(), free=False):
        q = self.q[eng]
        waits = [t for t in w if t is not None] + self.hold[eng]
        self.hold[eng] = []
        if not free and eng in (SC, VE, GP):
            for n in range(len(q) - 1, -1, -1):
                if q[n][2] is None:
                    waits.append((eng, n))
                    break
        q.append((fn, waits, None))
        return (eng, len(q) - 1)

    def dma(self, eng, sem, out, in_, w=()):
        if sem not in self.dma_sems:
            self.dma_sems[sem] = self.ctx.enter_context(self.nc.semaphore("d_" + sem))
            self.counts[sem] = 0
        self.counts[sem] += 16
        waits = [t for t in w if t is not None] + self.hold[eng]
        self.hold[eng] = []
        self.q[eng].append((lambda e: e.dma_start(out, in_), waits, sem))
        return (sem, self.counts[sem])

    def last(self, *engs):
        out = []
        for e in engs:
            for n in range(len(self.q[e]) - 1, -1, -1):
                if self.q[e][n][2] is None:
                    out.append((e, n))
                    break
        return out

    def barrier(self, extra=()):
        marks = {e: self.last(e) for e in (PE, SC, VE, GP)}
        for e in marks:
            self.hold[e] += [t for x in marks if x != e or e != PE for t in marks[x]] + list(extra)
        return [t for x in marks.values() for t in x]

    def emit(self, block):
        used = set()
        for q in self.q.values():
            for _, waits, _ in q:
                used |= {t for t in waits if t[0] in self.q}
        sems = {e: self.ctx.enter_context(self.nc.semaphore("s_" + e)) for e in self.q}
        value, total = {}, {}
        for e, q in self.q.items():
            n = 0
            for i in range(len(q)):
                if (e, i) in used:
                    n += 1
                    value[(e, i)] = n
        for e, q in self.q.items():
            def body(eng, e=e, q=q):
                seen = {}
                for i, (fn, waits, dsem) in enumerate(q):
                    need = {}
                    for t in waits:
                        v = value[t] if t[0] in self.q else t[1]
                        need[t[0]] = max(need.get(t[0], 0), v)
                    for s, v in need.items():
                        if seen.get(s, 0) < v:
                            eng.wait_ge(sems[s] if s in self.q else self.dma_sems[s], v)
                            seen[s] = v
                    if fn is None:
                        continue
                    ins = fn(eng)
                    if dsem is not None:
                        ins.then_inc(self.dma_sems[dsem], 16)
                    elif (e, i) in value:
                        ins.then_inc(sems[e], 1)
            {PE: block.tensor, SC: block.scalar, VE: block.vector, GP: block.gpsimd, SY: block.sync}[e](body)


class Slots:

    def __init__(self, bufs):
        self.bufs = bufs
        self.free = list(range(len(bufs)))
        self.readers = [[] for _ in bufs]

    def take(self):
        i = self.free.pop(0)
        r, self.readers[i] = self.readers[i], []
        return i, self.bufs[i], r

    def done(self, i, *toks):
        if i not in self.free:
            self.free.append(i)
        self.readers[i] += list(toks)


CONST = {}


def const_array():
    import numpy as np
    CONST.clear()
    p = np.arange(128)[:, None]
    i = np.arange(128)[None, :]
    ch = (p // 64) == (i // 64)
    parts = [("ident", p == i), ("ones", np.ones((128, 128))), ("upper", p <= i), ("strict", p < i),
             ("cum64", ch & (p <= i)), ("same64", ch)]
    for l in range(7):
        s = 1 << l
        parts.append((f"lvl{l}", (p // (2 * s) == i // (2 * s)) & (i % (2 * s) >= s) & (p % (2 * s) < s)))
    parts.append(("causal", np.where(i > p, NEG, 0.0)))
    t = np.arange(512)[None, :]
    parts.append(("notfirst", np.broadcast_to(t % 64 != 0, (128, 512))))
    parts.append(("col01", np.concatenate([p // 64 == 0, p // 64 == 1], 1)))
    n = np.arange(31)[None, None, :]
    q = np.arange(4)[None, :, None] * 128 + p[:, :, None]
    ok = (n * 16 + 31 <= q)
    parts.append(("cmpadd", np.where(ok, 0.0, NEG).reshape(128, 124)))
    parts.append(("cmpmul", ok.reshape(128, 124)))
    parts.append(("iota", np.broadcast_to(i, (128, 128))))
    off = 0
    for name, a in parts:
        CONST[name] = (off, a.shape[1])
        off += a.shape[1]
    return np.concatenate([a.astype(np.float32) for _, a in parts], axis=1)


def mask_array():
    import numpy as np
    s = np.arange(128)[:, None]
    t = np.arange(512)[None, :]
    same = (s // 64) == ((t % 128) // 64)
    a = np.concatenate([same & (s <= t % 128), same & (s > t % 128)], axis=1)
    return a.astype(np.uint32)


def build(nc, D, shapes):
    with ExitStack() as ctx:
        _build(nc, D, ctx)


def _build(nc, D, ctx):
    Q = Queues(nc, ctx)

    def sb(name, shape, dt=F32, c=ctx):
        return c.enter_context(nc.sbuf_tensor(name, shape, dt))

    ncst = D["consts"].shape[1]
    cst = sb("cst", [128, ncst])
    C = {k: cst[:, o:o + n] for k, (o, n) in CONST.items()}
    colw = D["cols"].shape[1]
    cols = sb("cols", [128, colw])
    cc = {k: cols[:, o:o + n] for k, (o, n) in COLS.items()}
    hh = sb("hh", [128, 8, 512], R32)
    hl = sb("hl", [128, 8, 512], R32)
    mT = sb("mT", [128, 8, 16])
    hmh = sb("hmh", [128, 8, 16], R32)
    hml = sb("hml", [128, 8, 16], R32)
    modc = sb("modc", [128, 48])
    scl = sb("scl", [128, 16])
    ring = [sb(f"ring{i}", [128, 2048]) for i in range(4)]
    wh = [sb(f"wh{i}", [128, 2048], R32) for i in range(2)]
    wl = [sb(f"wl{i}", [128, 2048], R32) for i in range(2)]
    bank = [ctx.enter_context(nc.psum_tensor(f"bank{i}", [128, 512], F32)) for i in range(8)]
    B = Slots(bank)
    R = Slots(ring)
    WS = Slots(list(zip(wh, wl)))
    ident = C["ident"]

    def mm(out, pairs, w=(), start=True, stop=True, check=True):
        n = len(pairs)
        for i, (a, b) in enumerate(pairs):
            t = Q.add(PE, lambda e, a=a, b=b, s=start and i == 0, z=stop and i == n - 1: e.matmul(
                out, a, b, start=s, stop=z, skip_group_check=not check), w if i == 0 else ())
        return t

    def mm3(out, pairs, w=(), start=True, stop=True, check=True):
        lst = []
        for (ah, al), (bh, bl) in pairs:
            lst += [(ah, bh), (ah, bl), (al, bh)]
        return mm(out, lst, w, start, stop, check)

    def tr(out, in_, w=()):
        k = in_.shape[0]
        return Q.add(PE, lambda e: e.transpose(out, in_, ident[0:k, 0:k]), w)

    def act(out, in_, fn, w=(), free=False, **kw):
        return Q.add(SC, lambda e: e.activation(out, in_, fn, **kw), w, free)

    def tt(out, a, b, op, w=(), free=False, eng=VE):
        return Q.add(eng, lambda e: e.tensor_tensor(out, a, b, op), w, free)

    def ts(out, a, s1, op0, s2=None, op1=None, w=(), free=False, eng=VE):
        if op1 is None:
            return Q.add(eng, lambda e: e.tensor_scalar(out, a, s1, None, op0), w, free)
        return Q.add(eng, lambda e: e.tensor_scalar(out, a, s1, s2, op0, op1), w, free)

    def stt(out, a, s, b, op0, op1, w=(), free=False):
        return Q.add(VE, lambda e: e.scalar_tensor_tensor(out=out, in0=a, scalar=s, in1=b, op0=op0, op1=op1),
                     w, free)

    def recip(out, a, w=(), free=False):
        return Q.add(VE, lambda e: e.reciprocal(out, a), w, free)

    def copy(out, a, w=(), free=False, eng=VE):
        if eng == SC:
            return act(out, a, ACT.Copy, w, free)
        return Q.add(eng, lambda e: e.tensor_copy(out, a), w, free)

    def red(out, a, op, w=(), free=False):
        return Q.add(VE, lambda e: e.tensor_reduce(out, a, AX.X, op), w, free)

    def bc(ap, n):
        a = ap.unsqueeze(2)
        return a.to_broadcast([a.shape[0], a.shape[1], n])

    def rep(ap, n):
        a = ap.unsqueeze(1)
        return a.to_broadcast([a.shape[0], n, a.shape[2]])

    M, A_, S_ = ALU.mult, ALU.add, ALU.subtract

    def split(hi, lo, src, w=(), eng=VE, f=False):
        a = act(hi, src, ACT.Copy, w, free=f)
        return tt(lo, src, hi.bitcast(F32), S_, [a], free=True, eng=eng)

    plan = []

    def want(name, lo_, hi_, n, parts=True):
        for s in range(lo_, hi_):
            plan.append((name, s, n, parts))

    want("ada", 0, 8, 2048, False)
    want("win1", 0, 12, 2048)
    want("win1t", 0, 1, 2048)
    want("win1g", 0, 1, 160)
    want("cmpw1", 0, 4, 2048, False)
    want("cmpw2", 0, 1, 256, False)
    want("ada", 8, 24, 2048, False)
    want("wout1", 0, 4, 2048)
    for g in range(2):
        want("wup", 11 * g, 11 * g + 11, 2048)
        want("wdn", 8 * g, 8 * g + 8, 1408)
    want("qk2", 0, 4, 2048)
    want("glow", 0, 1, 1024)
    want("v2", 0, 4, 2048)
    want("gout2", 0, 4, 2048)
    want("gatea", 0, 4, 2048)
    want("upgla", 0, 4, 2048)
    want("dt2", 0, 1, 256)
    for g in range(4):
        want("xs2", 2 * g, 2 * g + 2, 2048)
        want("bc2", g, g + 1, 2048)
        want("z2", 2 * g, 2 * g + 2, 2048)
    want("upssd", 0, 8, 2048)
    want("gateb", 0, 4, 2048)
    want("wout2", 0, 4, 2048)
    want("wq", 0, 8, 2048)
    want("subk", 0, 1, 2048, False)
    want("u", 0, 64, 2048)
    want("v", 0, 64, 2048)
    order = [(a, b) for a, b, _, _ in plan]
    stream, ready = [], []

    def weights():
        name, idx, n, parts = plan.pop(0)
        i, buf, free = R.take()
        t = Q.dma(SY, f"ring{i}", buf[:, 0:n], D[name][idx][:, 0:n], free)
        stream.append((i, buf, t, n, parts))

    def freed(i, tok):
        R.done(i, tok)
        if plan:
            weights()

    def prepare():
        if not stream:
            return
        i, buf, t, n, parts = stream.pop(0)
        if not parts:
            ready.append((("raw", i), buf, [t]))
            return
        wi, (h_, l_), free = WS.take()
        a = act(h_[:, 0:n], buf[:, 0:n], ACT.Copy, [t] + free, free=True)
        g = Q.add(GP, lambda e: e.tensor_tensor(l_[:, 0:n], buf[:, 0:n], h_[:, 0:n].bitcast(F32), S_),
                  [a] + free, True)
        ready.append((("parts", wi), (h_, l_), [a, g]))
        freed(i, g)

    def slot(name, idx):
        assert order.pop(0) == (name, idx), (name, idx)
        if not ready:
            prepare()
        r = ready.pop(0)
        if len(WS.free) and not ready and stream and (r[0][0] == "parts" or not stream[0][4]):
            prepare()
        elif len(WS.free) and not ready:
            prepare()
        return r

    def release(key, tok):
        if key[0] == "raw":
            freed(key[1], tok)
        else:
            WS.done(key[1], tok)

    k0 = Q.dma(SC, "c0", cst[:, :], D["consts"])
    k0 = Q.dma(SC, "c0", cols[:, :], D["cols"])
    k0 = Q.dma(SC, "c0", mT[:, :, :], D["metaT"])
    xd_ = nc.dram_tensor("x_spill", (128, 8, 512), F32).ap()
    xa_ = nc.dram_tensor("a_spill", (128, 8, 512), F32).ap()
    gs_ = nc.dram_tensor("gate_spill", (128, 4, 512), F32).ap()
    yd_ = nc.dram_tensor("y_spill", (128, 8, 512), F32).ap()

    def load(name, c, src, w=()):
        t_ = sb(name, [128, 8, 512], F32, c)
        return t_, Q.dma(SY, name, t_[:, :, :], src, w)
    for _ in range(4):
        weights()
    for e in (PE, VE, GP):
        Q.hold[e] += [k0]
    Q.hold[SC] += [k0]

    dumped = []

    def dump(name, ap):
        if DBG == name:
            toks = Q.last(PE, SC, VE, GP)
            d = D["dbg"]
            shp = list(ap.shape)
            n = 1
            for v in shp[1:]:
                n *= v
            dst = d[0:shp[0], 0:n]
            if len(shp) == 3:
                dst = dst.rearrange("p (a b) -> p a b", b=shp[2])
            Q.dma(SY, "dbg", dst, ap, toks)
            dumped.append(1)
            return True
        return False

    def norm_stats(src, T, N, out, tmp, w=()):
        k = len(src)
        i, ps, fr = B.take()
        for j, s in enumerate(src):
            a = act(tmp[j % 2][:, 0:T], s, ACT.Square, (list(w) if j == 0 else []) +
                    ([pes[-2]] if j >= 2 else []), free=j > 0)
            if j == 0:
                pes = []
            pes.append(mm(ps[:, 0:T], [(C["ones"], tmp[j % 2][:, 0:T])], [a] + (fr if j == 0 else []),
                          start=j == 0, stop=j == k - 1))
        ts(out, ps[:, 0:T], 1.0 / N, M, EPS, A_, w=[pes[-1]])
        v = recip(out, out)
        B.done(i, v)
        return act(out, out, ACT.Sqrt, [v])

    def linear(name, ntiles, per, kt, rhs, consume, w=(), first=None, s0=0):
        for _ in steps(name, ntiles, per, kt, rhs, consume, w, first, s0):
            pass

    def steps(name, ntiles, per, kt, rhs, consume, w=(), first=None, s0=0, fine=False):
        n = 0
        for s in range(ntiles // per):
            i, (h_, l_), t = slot(name, s0 + s)
            vh, vl = (x[:, 0:per * kt * 128].rearrange("p (a k n) -> p a k n", a=per, k=kt) for x in (h_, l_))
            for a in range(per):
                tile_ = lambda k: (vh[:, a, k, :], vl[:, a, k, :])
                if first is not None and n >= first:
                    bi, ps, fr = B.take()
                    m = mm3(ps[:, 0:16], [(tile_(k), mk(k)) for k in range(kt)], t + fr)
                    B.done(bi, consume(n, ps, m, True))
                bi, ps, fr = B.take()
                if callable(w):
                    for k in range(kt):
                        m = mm3(ps[:, :], [(tile_(k), rhs(k))], t + fr + (w(k) if n == 0 else []),
                                start=k == 0, stop=k == kt - 1)
                elif fine:
                    mm3(ps[:, :], [(tile_(k), rhs(k)) for k in range(kt // 2)], t + fr + list(w), stop=False)
                    yield
                    m = mm3(ps[:, :], [(tile_(k), rhs(k)) for k in range(kt // 2, kt)], start=False)
                else:
                    m = mm3(ps[:, :], [(tile_(k), rhs(k)) for k in range(kt)], t + fr + list(w))
                if a == per - 1:
                    release(i, m)
                B.done(bi, consume(n, ps, m) if first is None else consume(n, ps, m, False))
                n += 1
                yield

    hk = lambda k: (hh[:, k, :], hl[:, k, :])
    mk = lambda k: (hmh[:, k, :], hml[:, k, :])
    hkt = lambda k, j: (hh[:, k, 128 * j:128 * j + 128], hl[:, k, 128 * j:128 * j + 128])

    def norm_to(src, wcol, ar, shift=None, out=None, w=()):
        uniq.append(1)
        tmp = [sb(f"nt{j}_{len(uniq)}", [128, 512], F32, ar) for j in range(2)]
        tq = Slots([sb(f"nq{j}_{len(uniq)}", [128, 512], F32, ar) for j in range(3)])
        rstd = sb(f"nr{len(uniq)}", [128, 512], F32, ar)
        n = norm_stats([src[:, k, :] for k in range(8)], 512, 1024, rstd[:, :], tmp, w)
        rk = []
        for k in range(8):
            if out is not None:
                stt(out[:, k, :], src[:, k, :], wcol[:, k:k + 1], rstd[:, :], M, M, [n], free=True)
                continue
            qi, q, f = tq.take()
            v = stt(q[:, :], src[:, k, :], wcol[:, k:k + 1], rstd[:, :], M, M, [n] + f, free=True)
            if shift is not None:
                v = ts(q[:, :], q[:, :], shift[:, k:k + 1], A_)
            rk.append(split(hh[:, k, :], hl[:, k, :], q[:, :], [v], f=True))
            tq.done(qi, rk[-1])
        return lambda k: [rk[k]]

    def norm_meta(wcol, ar):
        tmp = [sb(f"nmt{j}", [128, 16], F32, ar) for j in range(2)]
        rst2 = sb("nm", [128, 16], F32, ar)
        q16 = sb("nm16", [128, 8, 16], F32, ar)
        n = norm_stats([mT[:, k, :] for k in range(8)], 16, 1024, rst2[:, :], tmp)
        yield
        for k in range(8):
            v = stt(q16[:, k, :], mT[:, k, :], wcol[:, k:k + 1], rst2[:, :], M, M, [n], free=k > 0)
        split(hmh[:, :, :], hml[:, :, :], q16[:, :, :], [v])

    uniq = []

    def together(*gens):
        for _ in weave(*gens):
            pass

    def weave(*gens):
        gens = [[g, n, 0.0] for g, n in gens]
        while gens:
            for x in list(gens):
                x[2] += x[1]
                while x[2] >= 1:
                    x[2] -= 1
                    if next(x[0], 0) == 0:
                        gens.remove(x)
                        break
                    yield

    finish = lambda: Q.emit(ctx.enter_context(nc.Block()))

    def endit():
        Q.q[SY].append((None, [("dbg", Q.counts["dbg"])], None))
        finish()

    scv = sb("scv", [128, 8])

    def modulation(s0, s1, row):
        bi, pm, fr = B.take()
        cprev = []
        for s in range(s0, s1):
            i, buf, t = slot("ada", s)
            v = buf[:, :].rearrange("p (k n) -> p k n", k=8)
            pi, ps, f2 = B.take()
            m = mm(ps[0:1, 0:256], [(scv[:, k:k + 1], v[:, k, :]) for k in range(8)], t + [a0] + f2)
            release(i, m)
            cp = copy(row[0:1, s % 2, :], ps[0:1, 0:256], [m] + cprev[-2:-1], eng=VE)
            B.done(pi, cp)
            yield
            for j in range(2):
                m = Q.add(PE, lambda e, c=2 * (s - s0) + j, s=s, j=j: e.matmul(
                    pm[:, c:c + 1], row[0:1, s % 2, 128 * j:128 * j + 128],
                    C["ones"][0:1, 0:1], start=c == 0, stop=True, skip_group_check=True), [cp] + fr)
            cprev.append(m)
        B.done(bi, tt(modc[:, 2 * s0:2 * s1], pm[:, 0:2 * (s1 - s0)], cc["adab"][:, 2 * s0:2 * s1], A_, [m]))

    with ExitStack() as ar:
        xT, k1 = load("x0", ar, D["xT"])
        row = sb("modrow", [1, 2, 256], F32, ar)
        a0 = act(scv[:, :], cc["c"], ACT.Silu)
        for _ in modulation(0, 8, row):
            pass
        v = stt(scl[:, 0:8], modc[:, 8:16], 1.0, cc["norm1"], A_, M)
        Q.hold[SC] += [v, k1]
        hready = norm_to(xT, scl[:, 0:8], ar, modc[:, 0:8])

    with ExitStack() as ar:
        qkv = sb("qkv", [128, 12, 512], F32, ar)
        nsq = sb("nsq", [128, 4, 512], F32, ar)
        kk2 = sb("kk2", [128, 2, 512], F32, ar)
        tm = sb("tm", [128, 4, 276], F32, ar)
        kcmp = sb("kcmp", [128, 32], F32, ar)
        vcmp = sb("vcmp", [32, 128], F32, ar)
        mix = sb("mix", [128, 4, 512], F32, ar)
        sm = {k: sb("g_" + k, [128, 4, 4], F32, ar) for k in
                  ("g", "beta", "u", "v", "gc", "gt", "egc", "kds", "gl", "bg")}
        gA = tm[:, :, 256:260]
        gB = tm[:, :, 260:264]
        nA = sb("nA", [128, 4], F32, ar)
        with ExitStack() as a2:
            gz = sb("gz", [128, 4, 512], F32, a2)
            cv = Slots([sb(f"cv{j}", [128, 512], F32, a2) for j in range(2)])
            rs = Slots([sb(f"rs{j}", [128, 512], F32, a2) for j in range(4)])
            kvc = mix[:, 0:2, :]

            def units(lst, rdy, T=512):
                st_ = []
                for src, scale, fac in lst:
                    ri, r, f = rs.take()
                    st_.append((ri, r[:, 0:T], act(r[:, 0:T], src, ACT.Square, rdy + f, free=True)))
                mms = []
                for ri, r, a in st_:
                    bi, ps, fr = B.take()
                    mms.append((bi, ps, mm(ps[:, 0:T], [(C["ones"], r)], [a] + fr)))
                vs = []
                for (ri, r, _), (bi, ps, m), (src, scale, fac) in zip(st_, mms, lst):
                    v = ts(r, ps[:, 0:T], scale, M, EPS, A_, w=[m], free=True)
                    B.done(bi, v)
                for ri, r, _ in st_:
                    vs.append(recip(r, r))
                as_ = [act(r, r, ACT.Sqrt, [v], free=True) for (ri, r, _), v in zip(st_, vs)]
                for (ri, r, _), a, (src, scale, fac) in zip(st_, as_, lst):
                    v = stt(src, src, fac, r, M, M, [a], free=True)
                    rs.done(ri, v)
                return v

            def take1(n, ps, m):
                if n < 12:
                    ci, c, f = cv.take()
                    w = cc["conv1"][:, 4 * n:4 * n + 4]
                    ts(c[:, :], ps[:, :], w[:, 3:4], M, w=[m] + f)
                    for d in (1, 2, 3):
                        v = stt(c[:, d:512], ps[:, 0:512 - d], w[:, 3 - d:4 - d], c[:, d:512], M, A_)
                    a = act(qkv[:, n, :], c[:, :], ACT.Silu, [v])
                    cv.done(ci, a)
                    return v
                if n < 16:
                    return act(gz[:, n - 12, :], ps[:, :], ACT.Silu, [m])
                if n < 20:
                    return copy(nsq[:, n - 16, :], ps[:, :], [m], eng=SC)
                if n < 22:
                    return copy(kvc[:, n - 20, :], ps[:, :], [m])
                return copy(kk2[:, n - 22, :], ps[:, :], [m], eng=SC)

            def take_all(n, ps, m):
                v = take1(n, ps, m)
                if n in (5, 9):
                    units([(qkv[:, x, :], 1.0, 128 ** -0.5 if n == 5 else 1.0)
                           for x in range(n - 5, n - 1)], Q.last(SC))
                if n == 21:
                    units([(nsq[:, x, :], 1 / 128, cc["qn"]) for x in range(4)], Q.last(SC))
                return v

            linear("win1", 24, 2, 8, hk, take_all, hready)
            gsp = Q.dma(SY, "gsp", gs_, gz[:, :, :], Q.last(SC))
            units([(kk2[:, 0, :], 1 / 128, cc["kslc"]), (kk2[:, 1, :], 1 / 128, cc["kwin"])], Q.last(SC))
            for name, off, n_ in (("win1t", 0, 256), ("win1g", 256, 20)):
                i, (h_, l_), t = slot(name, 0)
                vh, vl = (x[:, 0:8 * n_].rearrange("p (k n) -> p k n", k=8) for x in (h_, l_))
                for j in range(4):
                    bi, ps, fr = B.take()
                    m = mm3(ps[:, 0:n_], [(hkt(k, j), (vh[:, k, :], vl[:, k, :])) for k in range(8)], t + fr)
                    B.done(bi, copy(tm[:, j, off:off + n_], ps[:, 0:n_], [m]))
                release(i, m)
            blk = mix[:, 2:4, :].rearrange("p a b -> p (a b)")[:, 0:992].rearrange("p (a n) -> p a n", a=32)
            hid = sb("hid", [128, 32], F32, a2)
            hidk = sb("hidk", [128, 32], F32, a2)
            def compress():
                for c in range(2):
                    src = kvc[:, c, 0:512].rearrange("p (n s) -> p s n", s=16)
                    pos = cc["kpos" if c == 0 else "vpos"]
                    tt(blk[:, 0:16, :], src[:, :, 0:31], bc(pos[:, 0:16], 31), A_, Q.last(PE))
                    v = tt(blk[:, 16:32, :], src[:, :, 1:32], bc(pos[:, 16:32], 31), A_)
                    bi, ps, fr = B.take()
                    for half in range(2):
                        i, buf, t = slot("cmpw1", 2 * c + half)
                        w1 = buf[:, :].rearrange("p (a n) -> p a n", a=16)
                        m = mm(ps[:, 0:31], [(w1[:, a, :], blk[:, 16 * half + a, :]) for a in range(16)], t + [v] + fr,
                               start=half == 0, stop=half == 1)
                        release(i, m)
                        yield
                    a = act((hidk, hid)[c][:, 0:31], ps[:, 0:31], ACT.Silu, [m])
                    if c == 0:
                        akey = a
                    B.done(bi, a)
                    yield
                i2, w2, t2 = slot("cmpw2", 0)
                bi, ps, fr = B.take()
                m = mm(ps[:, 0:31], [(w2[:, 0:128], hidk[:, 0:31])], t2 + [akey] + fr)
                v = copy(kcmp[:, 0:31], ps[:, 0:31], [m])
                B.done(bi, v)
                yield
                units([(kcmp[:, 0:31], 1 / 128, cc["kcmpn"])], [v], T=31)
                yield
                bi, ps, fr = B.take()
                m = mm(ps[0:31, 0:128], [(hid[:, 0:31], w2[:, 128:256])], [a] + fr)
                release(i2, m)
                B.done(bi, copy(vcmp[0:31, :], ps[0:31, 0:128], [m]))

            def decays():
                act(nA[:, :], cc["alog"], ACT.Exp)
                yield
                ts(nA[:, :], nA[:, :], -1.0, M, w=Q.last(SC))
                v = tt(sm["u"][:, :, :], gA, rep(cc["dtb1"], 4), A_)
                act(sm["v"][:, :, :], sm["u"][:, :, :], ACT.Abs, [v])
                yield
                act(sm["v"][:, :, :], sm["v"][:, :, :], ACT.Exp, scale=-1.0)
                yield
                a = act(sm["v"][:, :, :], sm["v"][:, :, :], ACT.Ln, bias=1.0)
                yield
                stt(sm["u"][:, :, :], sm["u"][:, :, :], 0.0, sm["v"][:, :, :], ALU.max, A_, [a])
                g = tt(sm["g"][:, :, :], sm["u"][:, :, :], rep(nA[:, :], 4), M)
                a = act(sm["beta"][:, :, :], gB, ACT.Sigmoid)
                yield
                bi, ps, fr = B.take()
                m = mm(ps[:, 0:16], [(C["upper"], sm["g"][:, :, :].rearrange("p a b -> p (a b)"))], [g, a] + fr)
                v = copy(sm["gc"][:, :, :].rearrange("p a b -> p (a b)"), ps[:, 0:16], [m])
                B.done(bi, v)
                bi, ps, fr = B.take()
                m = mm(ps[:, 0:16], [(C["ones"], sm["g"][:, :, :].rearrange("p a b -> p (a b)"))], fr)
                v = copy(sm["gt"][:, :, :].rearrange("p a b -> p (a b)"), ps[:, 0:16], [m])
                B.done(bi, v)
                v = tt(sm["kds"][:, :, :], sm["gt"][:, :, :], sm["gc"][:, :, :], S_)
                act(sm["kds"][:, :, :], sm["kds"][:, :, :], ACT.Exp, [v])
                yield
                act(sm["gl"][:, :, :], sm["gt"][:, :, :], ACT.Exp)
                yield
                a = act(sm["egc"][:, :, :], sm["gc"][:, :, :], ACT.Exp)
                yield
                tt(sm["bg"][:, :, :], sm["beta"][:, :, :], sm["egc"][:, :, :], M, [a])

            together((compress(), 1), (decays(), 1))
            if dump("qkv", qkv[:, :, :]) or dump("kcmp", kcmp[:, 0:31]) or dump("vcmp", vcmp[0:31, :]) \
                    or dump("nsq", nsq[:, :, :]) or dump("kk2", kk2[:, :, :]) or dump("tm", tm[:, :, :]):
                return endit()
            Q.barrier([gsp])

        with ExitStack() as a2:
            def big(name):
                return sb(name, [128, 4, 128], F32, a2)
            lanes = [[big(f"{n_}{j}") for n_ in ("kbe", "kd", "egb", "btb", "dtm", "AT", "XT", "BT")]
                     for j in range(2)]
            St = big("St")
            scanned = [None]

            def four(fn, w=()):
                bi, ps, fr = B.take()
                for h in range(4):
                    lst = fn(h)
                    for n_, (l, r) in enumerate(lst):
                        m = Q.add(PE, lambda e, l=l, r=r, h=h, s=(h == 0 and n_ == 0): e.matmul(
                            ps[:, 128 * h:128 * h + 128], l, r, start=s, stop=True, skip_group_check=True),
                            (list(w) + fr) if h == 0 and n_ == 0 else ())
                return bi, ps[:, :].rearrange("p (a b) -> p a b", a=4), m

            def gdn(lane):
                kbe, kd, egb, btb, dtm, AT, XT, BT = lanes[lane]
                aT = mix[:, 0:4, 128 * (lane + 2):128 * (lane + 3)]
                Y, wT, u, vn = dtm, btb, egb, kbe
                for mt in (lane, lane + 2):
                    c0 = 128 * mt
                    X = qkv[:, 4:8, c0:c0 + 128]
                    kT = lambda h: qkv[:, 4 + h, c0:c0 + 128]
                    qT = lambda h: qkv[:, h, c0:c0 + 128]
                    for what in (4, 8):
                        yield
                        bi, ps, fr = B.take()
                        for h in range(4):
                            m = tr(ps[:, 128 * h:128 * h + 128], qkv[:, what + h, c0:c0 + 128],
                                   fr if h == 0 else ())
                        p3 = ps[:, :].rearrange("p (a b) -> p a b", a=4)
                        if what == 4:
                            tt(kbe[:, :, :], p3, bc(sm["bg"][:, mt, :], 128), M, [m])
                            v = tt(kd[:, :, :], p3, bc(sm["kds"][:, mt, :], 128), M, free=True)
                        else:
                            vb = qkv[:, 8:12, c0:c0 + 128]
                            v = tt(vb, p3, bc(sm["beta"][:, mt, :], 128), M, [m])
                        B.done(bi, v)
                    yield
                    bi, p3, m = four(lambda h: [(sm["g"][:, mt, h:h + 1].to_broadcast([128, 128]), C["upper"])])
                    ae = act(egb[:, :, :], p3, ACT.Exp, [m, v], free=True)
                    v = tt(dtm[:, :, :], p3, bc(sm["gc"][:, mt, :], 128), S_, [ae])
                    B.done(bi, v)
                    v = ts(dtm[:, :, :], dtm[:, :, :], 0.0, ALU.min)
                    a = act(dtm[:, :, :], dtm[:, :, :], ACT.Exp, [v])
                    tt(dtm[:, :, :], dtm[:, :, :], rep(C["upper"], 4), M, [a])
                    yield
                    bi, p3, m = four(lambda h: [(sm["beta"][:, mt, h:h + 1].to_broadcast([128, 128]), ident)])
                    v = tt(btb[:, :, :], p3, rep(C["strict"], 4), M, [m])
                    B.done(bi, v)
                    v = tt(btb[:, :, :], btb[:, :, :], dtm[:, :, :], M)
                    yield
                    bi, p3, m = four(lambda h: [(kT(h), kT(h))])
                    v = tt(AT[:, :, :], p3, btb[:, :, :], M, [m])
                    B.done(bi, v)
                    yield
                    bi, p3, m = four(lambda h: [(kT(h), qT(h))])
                    v = tt(aT, p3, dtm[:, :, :], M, [m])
                    B.done(bi, v)
                    qd = qkv[:, 0:4, c0:c0 + 128]
                    tt(qd, qkv[:, 0:4, c0:c0 + 128], egb[:, :, :], M)
                    tt(BT[:, :, :], AT[:, :, :], rep(C["lvl0"], 4), M)
                    v = tt(XT[:, :, :], rep(ident, 4), BT[:, :, :], S_)
                    yield
                    bi, ps, fr = B.take()
                    for h in range(4):
                        m = tr(ps[:, 128 * h:128 * h + 128], XT[:, h, :], ([v] + fr) if h == 0 else ())
                    v = copy(X, ps[:, :].rearrange("p (a b) -> p a b", a=4), [m])
                    B.done(bi, v)
                    for l in range(1, 7):
                        v = tt(BT[:, :, :], AT[:, :, :], rep(C[f"lvl{l}"], 4), M)
                        yield
                        bi, p3, m = four(lambda h: [(BT[:, h, :], X[:, h, :])], [v])
                        v = copy(Y[:, :, :], p3, [m])
                        B.done(bi, v)
                        yield
                        bi, p3, m = four(lambda h: [(Y[:, h, :], XT[:, h, :])], [v])
                        if l < 6:
                            b2, p4, m2 = four(lambda h: [(XT[:, h, :], Y[:, h, :])])
                        else:
                            m2 = m
                        v = tt(XT[:, :, :], XT[:, :, :], p3, S_, [m2])
                        B.done(bi, v)
                        if l < 6:
                            v = tt(X, X, p4, S_, [m2])
                            B.done(b2, v)
                    yield
                    bi, p3, m = four(lambda h: [(kbe[:, h, :], XT[:, h, :])], [v])
                    v = copy(wT[:, :, :], p3, [m])
                    B.done(bi, v)
                    yield
                    bi, p3, m = four(lambda h: [(XT[:, h, :], vb[:, h, :])])
                    v = copy(u[:, :, :], p3, [m])
                    B.done(bi, v)
                    while len(scanned) <= mt:
                        yield
                    if mt > 0:
                        yield
                        bi, p3, m = four(lambda h: [(wT[:, h, :], St[:, h, :])], [v, scanned[mt]])
                        v = tt(vn[:, :, :], u[:, :, :], p3, S_, [m])
                        B.done(bi, v)
                        V_ = vn
                    else:
                        V_ = u
                    yield
                    bi, p3, m = four(lambda h: ([(St[:, h, :], qd[:, h, :])] if mt > 0 else []) +
                                     [(V_[:, h, :], aT[:, h, :])], [v])
                    v = copy(mix[:, 0:4, c0:c0 + 128], p3, [m])
                    B.done(bi, v)
                    if mt < 3:
                        yield
                        bi, p3, m = four(lambda h: [(kd[:, h, :], V_[:, h, :])])
                        if mt == 0:
                            v = copy(St[:, :, :], p3, [m])
                        else:
                            tt(St[:, :, :], St[:, :, :], bc(sm["gl"][:, mt, :], 128), M, [m])
                            v = tt(St[:, :, :], St[:, :, :], p3, A_)
                        B.done(bi, v)
                        scanned.append(v)

            def gdn_out():
                sq = Slots([x[:, :, :].rearrange("p a b -> p (a b)") for x in (lanes[0][0], lanes[0][1])])
                rs = Slots([x[:, :, :].rearrange("p a b -> p (a b)") for x in (lanes[0][2], lanes[0][3])])
                w_ = Q.last(PE)
                gzs = [x[:, :, :].rearrange("p a b -> p (a b)") for x in lanes[1][0:4]]
                for h in range(4):
                    kg = Q.dma(SY, "gzl", gzs[h], gs_[:, h, :], Q.last(PE, VE, SC))
                for h in range(4):
                    si, s, f = sq.take()
                    a = act(s[:, :], mix[:, h, :], ACT.Square, f + w_ + Q.last(VE))
                    bi, ps, fr = B.take()
                    m = mm(ps[:, :], [(C["ones"], s[:, :])], [a] + fr)
                    sq.done(si, m)
                    yield
                    ri, r, f = rs.take()
                    v = ts(r[:, :], ps[:, :], 1 / 128, M, EPS, A_, w=[m] + f)
                    B.done(bi, v)
                    v = recip(r[:, :], r[:, :])
                    a = act(r[:, :], r[:, :], ACT.Sqrt, [v])
                    yield
                    stt(mix[:, h, :], mix[:, h, :], cc["gdnn"], r[:, :], M, M, [a])
                    v = tt(mix[:, h, :], mix[:, h, :], gzs[h], M, [kg])
                    rs.done(ri, split(hh[:, h, :], hl[:, h, :], mix[:, h, :], [v]))

            Pb = Slots([sb(f"P{j}", [128, 512], F32, a2) for j in range(2)])
            PC = Slots([sb("PC", [32, 128], F32, a2)])
            PT = Slots([sb(f"PT{j}", [128, 512], F32, a2) for j in range(2)])
            st = sb("st", [128, 48, 4], F32, a2)
            gates = sb("gates", [128, 4, 12], F32, a2)
            act(gates[:, :, :], tm[:, :, 264:276], ACT.Sigmoid)
            gtok = Q.last(SC)[0]
            SCL = 128 ** -0.5
            def attention():
                nst = 0
                for mt in range(4):
                    L = 128 * (mt + 1)
                    for h in range(4):
                        qT = nsq[:, h, 128 * mt:128 * mt + 128]
                        pvs = []
                        for br in range(3):
                            n_ = 31 if br == 0 else L
                            rhs = kcmp[:, 0:31] if br == 0 else kk2[:, br - 1, 0:L]
                            bi, ps, fr = B.take()
                            m = mm(ps[:, 0:n_], [(qT, rhs)], fr)
                            s4 = st[:, nst, :]
                            nst += 1
                            if br == 0:
                                add = C["cmpadd"][:, 31 * mt:31 * mt + 31]
                                tt(ps[:, 0:31], ps[:, 0:31], add, A_, [m], free=True)
                            else:
                                tt(ps[:, L - 128:L], ps[:, L - 128:L], C["causal"], A_, [m], free=True)
                            red(s4[:, 0:1], ps[:, 0:n_], ALU.max)
                            v = ts(s4[:, 1:2], s4[:, 0:1], -1e25, ALU.max, -SCL, M)
                            pi, P, f = Pb.take()
                            yield
                            a = act(P[:, 0:n_], ps[:, 0:n_], ACT.Exp, [v] + f, free=True, bias=s4[:, 1:2],
                                    scale=SCL, accum_out=s4[:, 2:3])
                            B.done(bi, a)
                            v = ts(s4[:, 3:4], s4[:, 2:3], 1e-30, ALU.max, w=[a, gtok])
                            recip(s4[:, 3:4], s4[:, 3:4])
                            tt(s4[:, 3:4], s4[:, 3:4], gates[:, mt, 3 * h + br:3 * h + br + 1], M)
                            if br == 0:
                                v = stt(P[:, 0:31], P[:, 0:31], s4[:, 3:4], C["cmpmul"][:, 31 * mt:31 * mt + 31], M, M)
                            else:
                                v = ts(P[:, 0:n_], P[:, 0:n_], s4[:, 3:4], M)
                            yield
                            bi, ps, fr = B.take()
                            ring_ = PC if br == 0 else PT
                            ti, T_, tf = ring_.take()
                            if br == 0:
                                m = tr(ps[0:31, 0:128], P[:, 0:31], [v] + fr)
                                v = copy(T_[0:31, 0:128], ps[0:31, 0:128], [m] + tf, eng=SC, free=True)
                                pvs.append((vcmp[0:31, :], T_[0:31, 0:128], v, ti, ring_))
                            else:
                                for j in range(mt + 1):
                                    m = tr(ps[:, 128 * j:128 * j + 128], P[:, 128 * j:128 * j + 128],
                                           ([v] + fr) if j == 0 else ())
                                v = copy(T_[:, 0:L], ps[:, 0:L], [m] + tf, eng=SC, free=True)
                                for j in range(mt + 1):
                                    pvs.append((tm[:, j, 128 * (br - 1):128 * br], T_[:, 128 * j:128 * j + 128], v, ti, ring_))
                            Pb.done(pi, m)
                            yield
                            B.done(bi, v)
                        bi, ps, fr = B.take()
                        for n_, (l, r, v, ti, ring_) in enumerate(pvs):
                            m = mm(ps[:, 0:128], [(l, r)], [v] + (fr if n_ == 0 else []), start=n_ == 0,
                                   stop=n_ == len(pvs) - 1)
                            ring_.done(ti, m)
                        c_ = slice(128 * mt, 128 * mt + 128)
                        a = copy(hh[:, 4 + h, c_], ps[:, 0:128], [m], eng=SC, free=True)
                        B.done(bi, tt(hl[:, 4 + h, c_], ps[:, 0:128], hh[:, 4 + h, c_].bitcast(F32), S_, [a], free=True))
                        yield

            def both():
                alive = [gdn(0), gdn(1)]
                while alive:
                    for x in list(alive):
                        if next(x, 0) == 0:
                            alive.remove(x)
                        yield
                yield from gdn_out()

            row = sb("modrow2", [1, 2, 256], F32, a2)
            together((both(), 1.2), (attention(), 2), (modulation(8, 24, row), 0.3), (norm_meta(cc["lnmix"], a2), 0.05))
            v = stt(scl[:, 8:16], modc[:, 32:40], 1.0, cc["norm2"], A_, M)
            if dump("mixed", hh[:, :, :].bitcast(F32)):
                return endit()
            Q.barrier()

    free0 = Q.last(PE, SC, VE, GP)
    with ExitStack() as ar:
        xT, k1 = load("x1", ar, D["xT"], free0)
        Q.hold[VE] += [k1]

        def res1(gate):
            def f(n, ps, m):
                return stt(xT[:, n, :], ps[:, :], modc[:, gate + n:gate + n + 1], xT[:, n, :], M, A_, [m], free=True)
            return f

        linear("wout1", 8, 2, 8, hk, res1(16))
        if dump("x1", xT[:, :, :]):
            return endit()
        hready = norm_to(xT, scl[:, 8:16], ar, modc[:, 24:32], w=Q.last(VE))
        ffh = sb("ffh", [128, 11, 512], R32, ar)
        ffl = sb("ffl", [128, 11, 512], R32, ar)
        cv = Slots([sb(f"fcv{j}", [128, 512], F32, ar) for j in range(6)])

        def ffn(half, war):
            def f_(n, ps, m):
                ci, c, f = cv.take()
                w = cc["fconv"][:, 4 * (n + 22 * half):4 * (n + 22 * half) + 4]
                ts(c[:, :], ps[:, :], w[:, 2:3], M, w[:, 3:4], A_, w=[m] + f)
                stt(c[:, 1:512], ps[:, 0:511], w[:, 1:2], c[:, 1:512], M, A_)
                v = stt(c[:, 2:512], ps[:, 0:510], w[:, 0:1], c[:, 2:512], M, A_)
                if n % 2 == 0:
                    a = act(c[:, :], c[:, :], ACT.Silu, [v], free=True)
                    ffa[0] = (ci, c, a)
                else:
                    ai, ca, a = ffa[0]
                    v2 = tt(c[:, :], ca[:, :], c[:, :], M, [a])
                    cv.done(ai, v2)
                    cv.done(ci, split(ffh[:, n // 2, :], ffl[:, n // 2, :], c[:, :], [v2] + war, eng=GP, f=True))
                return v
            return f_

        ffa = {}
        for half in range(2):
            linear("wup", 22, 2, 8, hk, ffn(half, Q.last(PE) if half else []), [] if half else hready, s0=11 * half)
            linear("wdn", 8, 1, 11, lambda k: (ffh[:, k, :], ffl[:, k, :]), res1(40), Q.last(GP), s0=8 * half)
        if dump("x2", xT[:, :, :]):
            return endit()
        hready = norm_to(xT, cc["lnmix"], ar, w=Q.last(VE))
        xsp = Q.dma(SY, "xsp", xd_, xT[:, :, :], Q.last(VE))
    with ExitStack() as ar:
        oT = sb("oT", [128, 8, 512], F32, ar)
        qk = sb("qk", [128, 8, 512], F32, ar)
        am = ar.enter_context(ExitStack())
        gg_ = nc.dram_tensor("gla_gates", (128, 16, 512), F32).ap()
        km = sb("km", [128, 4, 16], F32, am)
        glo = sb("glo", [16, 528], F32, am)
        vt = sb("vt", [128, 4, 1024], F32, am)
        vm = sb("vm", [16, 1024], F32, am)
        G = sb("G", [128, 4, 512], F32, am)
        lt = oT[:, 0:4, :].rearrange("p a b -> p (a b)")
        g2w = oT[0:16, 5, :]
        k2 = Q.dma(SY, "g2w", g2w, D["gate2w"], Q.last(PE, SC, VE, GP) + [xsp])
        Gm = sb("Gm", [128, 4, 16], F32, am)
        msk = sb("msk", [128, 1024], U32, am)
        kmsk = Q.dma(SY, "msk", msk[:, :], D["masks"], Q.last(PE, SC, VE, GP))

        def take_qk(n, ps, m, meta):
            if meta:
                return copy(km[:, n - 4, :], ps[:, 0:16], [m]) if n >= 4 else None
            if n < 4:
                return act(qk[:, n, :], ps[:, :], ACT.Copy, [m], free=True, scale=128 ** -0.5)
            return copy(qk[:, n, :], ps[:, :], [m], free=True)

        linear("qk2", 8, 2, 8, hk, take_qk, hready, first=4)
        for e in (VE, SC):
            Q.hold[e] += [xsp]
        i, (h_, l_), t = slot("glow", 0)
        vh, vl = (x[:, 0:1024].rearrange("p (k n) -> p k n", k=8) for x in (h_, l_))
        bi, ps, fr = B.take()
        m = mm3(ps[:, :], [((vh[:, k, :], vl[:, k, :]), hk(k)) for k in range(8)], t + fr)
        B.done(bi, copy(glo[:, 0:512], ps[0:16, :], [m]))
        bi, ps, fr = B.take()
        m = mm3(ps[:, 0:16], [((vh[:, k, :], vl[:, k, :]), mk(k)) for k in range(8)], fr)
        glt = copy(glo[:, 512:528], ps[0:16, 0:16], [m])
        B.done(bi, glt)
        release(i, m)
        for h in range(4):
            bi, ps, fr = B.take()
            m = mm(ps[:, :], [(g2w[:, 128 * h:128 * h + 128], glo[:, 0:512])], [glt, k2] + fr)
            v = ts(G[:, h, :], ps[:, :], cc["bgate"][:, h:h + 1], A_, w=[m])
            B.done(bi, v)
            bi, ps, fr = B.take()
            m = mm(ps[:, 0:16], [(g2w[:, 128 * h:128 * h + 128], glo[:, 512:528])], fr)
            gz_ = ts(Gm[:, h, :], ps[:, 0:16], cc["bgate"][:, h:h + 1], A_, w=[m])
            B.done(bi, gz_)
        vmf = lt[:, 0:128].rearrange("p (a n) -> p a n", a=8)
        for s in range(4):
            i, (h_, l_), t = slot("v2", s)
            vh, vl = (x[:, :].rearrange("p (k n) -> p k n", k=8) for x in (h_, l_))
            for j in range(4):
                bi, ps, fr = B.take()
                m = mm3(ps[:, 0:256], [(hkt(k, j), (vh[:, k, :], vl[:, k, :])) for k in range(8)], t + fr)
                B.done(bi, copy(vt[:, j, 256 * s:256 * s + 256], ps[:, 0:256], [m], eng=SC, free=True))
            for c in range(2):
                bi, ps, fr = B.take()
                cs = slice(128 * c, 128 * c + 128)
                m = mm3(ps[:, 0:16], [((vh[:, k, cs], vl[:, k, cs]), mk(k)) for k in range(8)], fr)
                v = copy(vmf[:, 2 * s + c, :], ps[:, 0:16], [m])
                B.done(bi, v)
            release(i, m)
        for c in range(2):
            bi, ps, fr = B.take()
            for x in range(4):
                m = tr(ps[0:16, 128 * x:128 * x + 128], vmf[:, 4 * c + x, :], [v] + fr)
            B.done(bi, copy(vm[:, 512 * c:512 * c + 512], ps[0:16, :], [m]))
        Q.barrier()
        with ExitStack() as a2:
            names = ("eG", "eN", "qe", "qn", "ke", "kn")
            Es = {n_: [sb(f"gl_{n_}{j}", [128, 512], F32, a2) for j in range(1)]
                  for n_ in names}
            kdt = sb("kdt", [128, 2, 512], F32, a2)
            att = Es["eG"][0]
            kdm = sb("kdm", [128, 16], F32, a2)
            kdmt = sb("kdmt", [16, 128], F32, a2)
            S = sb("Sg", [128, 8, 256], F32, a2)
            gl = sb("glg", [128, 8], F32, a2)
            gst2 = Slots([sb(f"ggs{j}", [128, 512], F32, a2) for j in range(2)])

            def scan():
                done_pe = None
                for z_, n_, first in ((G[:, :, :].rearrange("p a b -> p (a b)"), 2048, True),
                                      (Gm[:, :, :].rearrange("p a b -> p (a b)"), 64, False)):
                    l_ = lt[:, 0:n_]
                    act(l_, z_, ACT.Abs, [gz_] + Q.last(VE))
                    act(l_, l_, ACT.Exp, scale=-1.0)
                    a = act(l_, l_, ACT.Ln, bias=1.0)
                    v = stt(z_, z_, 0.0, l_, ALU.min, S_, [a])
                    v = ts(z_, z_, 1 / 16, M)
                    yield
                for h in range(4):
                    Q.add(VE, lambda e, h=h: e.tensor_tensor_scan(lt[:, 512 * h:512 * h + 512], C["notfirst"],
                                                                  G[:, h, :], 0.0, M, A_), free=h > 0)
                for h in range(4):
                    v = Q.add(VE, lambda e, h=h: e.tensor_tensor_scan(Gm[:, h, :], C["ones"][:, 0:16],
                                                                      Gm[:, h, :], 0.0, M, A_), free=h > 0)
                copy(G[:, :, :].rearrange("p a b -> p (a b)"), lt[:, :])
                yield
                for h in range(4):
                    Gh = G[:, h, :]
                    qh, kh = qk[:, h, :], qk[:, 4 + h, :]
                    E = {n_: Es[n_][0] for n_ in names}
                    prev = [done_pe] + Q.last(VE)
                    act(E["eG"][:, :], Gh, ACT.Exp, prev)
                    a = act(E["eN"][:, :], Gh, ACT.Exp, scale=-1.0, free=True)
                    tt(E["qe"][:, :], qh, E["eG"][:, :], M, [a] + prev)
                    tt(E["qn"][:, :], qh, E["eN"][:, :], M, free=True)
                    tt(E["ke"][:, :], kh, E["eG"][:, :], M, free=True)
                    v1 = tt(E["kn"][:, :], kh, E["eN"][:, :], M, free=True)
                    g3 = Gh.rearrange("p (c t) -> p c t", c=8)
                    e3 = E["eG"][:, :].rearrange("p (c t) -> p c t", c=8)
                    yield
                    copy(gl[:, :].unsqueeze(2), e3[:, :, 63:64])
                    v = tt(E["eN"][:, :].rearrange("p (c t) -> p c t", c=8), g3[:, :, 63:64].to_broadcast([128, 8, 64]),
                           g3, S_)
                    a = act(E["eN"][:, :], E["eN"][:, :], ACT.Exp, [v])
                    v = tt(E["eN"][:, :], E["eN"][:, :], kh, M, [a])
                    yield
                    vmt = ts(kdm[:, :], Gm[:, h, :], Gm[:, h, 15:16], S_, -1.0, M)
                    a = act(kdm[:, :], kdm[:, :], ACT.Exp, [vmt])
                    vmt = tt(kdm[:, :], kdm[:, :], km[:, h, :], M, [a])
                    yield
                    bi, ps, fr = B.take()
                    m = tr(ps[0:16, 0:128], kdm[:, :], [vmt] + fr)
                    c_ = copy(kdmt[:, :], ps[0:16, 0:128], [m])
                    B.done(bi, c_)
                    yield
                    bi, ps, fr = B.take()
                    m = mm(ps[:, 0:256], [(kdmt[:, :], vm[:, 256 * h:256 * h + 256])], [c_] + fr)
                    B.done(bi, copy(S[:, 0, :], ps[:, 0:256], [m]))
                    bi, ps, fr = B.take()
                    for j in range(4):
                        m = tr(ps[:, 128 * j:128 * j + 128], E["eN"][:, 128 * j:128 * j + 128],
                               ([v] + fr) if j == 0 else ())
                    ts(kdt[:, 0, :], ps[:, :], C["col01"][:, 0:1], M, w=[m])
                    v = ts(kdt[:, 1, :], ps[:, :], C["col01"][:, 1:2], M, free=True)
                    B.done(bi, v)
                    yield
                    b1, p1, f1 = B.take()
                    b2, p2, f2 = B.take()
                    for j in range(4):
                        c = slice(128 * j, 128 * j + 128)
                        mm(p1[:, c], [(E["kn"][:, c], E["qe"][:, c])], [v1] + f1, start=j == 0, check=False)
                        m = mm(p2[:, c], [(E["ke"][:, c], E["qn"][:, c])], f2, start=j == 0, check=False)
                    Q.add(VE, lambda e: e.memset(att[:, :], 0.0))
                    Q.add(VE, lambda e, p1=p1: e.copy_predicated(att[:, :], msk[:, 0:512], p1[:, :]), [m, kmsk])
                    va = Q.add(VE, lambda e, p2=p2: e.copy_predicated(att[:, :], msk[:, 512:1024], p2[:, :]))
                    B.done(b1, va)
                    B.done(b2, va)
                    yield
                    for c2 in range(4):
                        bi, ps, fr = B.take()
                        for c in range(2 * c2, min(2 * c2 + 2, 7)):
                            m = mm(ps[:, 256 * (c % 2):256 * (c % 2) + 256],
                                   [(kdt[:, c % 2, 128 * c2:128 * c2 + 128], vt[:, c2, 256 * h:256 * h + 256])],
                                   [v] + fr, start=c % 2 == 0, check=False)
                        for c in range(2 * c2, min(2 * c2 + 2, 7)):
                            vs = stt(S[:, c + 1, :], S[:, c, :], gl[:, c:c + 1], ps[:, 256 * (c % 2):256 * (c % 2) + 256],
                                     M, A_, [m])
                        B.done(bi, vs)
                        yield
                    for dv in range(2):
                        bi, ps, fr = B.take()
                        for j in range(4):
                            m = mm(ps[:, 128 * j:128 * j + 128],
                                   [(vt[:, j, 256 * h + 128 * dv:256 * h + 128 * dv + 128],
                                     att[:, 128 * j:128 * j + 128])], [va] + fr, start=j == 0, stop=False, check=False)
                        for c in range(8):
                            m = mm(ps[:, 64 * c:64 * c + 64], [(S[:, c, 128 * dv:128 * dv + 128],
                                                                E["qe"][:, 64 * c:64 * c + 64])], [vs],
                                   start=False, check=False)
                        B.done(bi, copy(oT[:, 2 * h + dv, :], ps[:, :], [m], eng=SC, free=True))
                        done_pe = m
                        yield
                    bi, ps, fr = B.take()
                    for dv, x in ((0, "qn"), (1, "ke")):
                        a = act(E[x][:, :], oT[:, 2 * h + dv, :], ACT.Square)
                        m = mm(ps[:, :], [(C["ones"], E[x][:, :])], [a] + fr, start=dv == 0, stop=dv == 1)
                    yield
                    r_ = E["kn"]
                    ts(r_[:, :], ps[:, :], 1 / 256, M, EPS, A_, w=[m])
                    v = recip(r_[:, :], r_[:, :])
                    B.done(bi, v)
                    a = act(r_[:, :], r_[:, :], ACT.Sqrt, [v])
                    yield
                    for dv in range(2):
                        o_ = oT[:, 2 * h + dv, :]
                        stt(o_, o_, cc["glan"][:, dv:dv + 1], r_[:, :], M, M, [a], free=dv > 0)
                    done_pe = m

            gspill = []

            def gate_rows(n0, fn):
                def f_(n, ps, m):
                    si, s, f = gst2.take()
                    a = act(s[:, :], ps[:, :], fn, [m] + f, free=True)
                    gspill.append(Q.dma(SY, f"ggs{si}", gg_[:, n0 + n, :], s[:, :], [a]))
                    gst2.done(si, gspill[-1])
                    return a
                return f_

            def gate_steps():
                yield from steps("gout2", 8, 2, 8, hk, gate_rows(0, ACT.Silu), fine=True)
                yield from steps("gatea", 8, 2, 8, hk, gate_rows(8, ACT.Sigmoid), fine=True)

            together((scan(), 1), (gate_steps(), 0.6))
        am.close()
        with ExitStack() as a2:
            Q.barrier()
            oh = sb("oh", [128, 8, 512], R32, a2)
            ol = sb("ol", [128, 8, 512], R32, a2)
            og = sb("og", [128, 8, 512], F32, a2)
            ya = qk
            ld = Q.last(PE, VE, SC) + gspill[-2:]
            kog = [Q.dma(SY, f"og{x}", og[:, 4 * x:4 * x + 4, :], gg_[:, 4 * x:4 * x + 4, :], ld) for x in range(2)]
            kya = Q.dma(SY, "yag", ya[:, :, :], gg_[:, 8:16, :], ld)
            rk = []
            for k in range(8):
                v = tt(oT[:, k, :], oT[:, k, :], og[:, k, :], M, [kog[k // 4]], free=True)
                rk.append(split(oh[:, k, :], ol[:, k, :], oT[:, k, :], [v], eng=VE, f=True))
            linear("upgla", 8, 2, 8, lambda k: (oh[:, k, :], ol[:, k, :]),
                   lambda n, ps, m: tt(ya[:, n, :], ya[:, n, :], ps[:, :], M, [m, kya]), lambda k: [rk[k]])
            ysp = Q.dma(SY, "ysp", yd_, ya[:, :, :], Q.last(VE))
            Q.barrier([ysp])

    with ExitStack() as ar:
        ys_ = nc.dram_tensor("ssd_spill", (128, 16, 512), F32).ap()
        ydone = []
        with ExitStack() as a2:
            dtt = sb("dtt", [128, 5, 32], F32, a2)
            av = sb("av", [128, 5, 32], F32, a2)
            ac = sb("ac", [128, 5, 32], F32, a2)
            dtx = sb("dtx", [128, 5, 32], F32, a2)
            te = sb("te", [128, 9, 32], F32, a2)
            al2 = sb("al2", [128, 4, 64], F32, a2)
            eal = sb("eal", [128, 8, 32], F32, a2)
            eac = sb("eac", [128, 4, 32], F32, a2)
            i, (h_, l_), t = slot("dt2", 0)
            wdh, wdl = (x[:, 0:256].rearrange("p (k n) -> p k n", k=8) for x in (h_, l_))
            z0 = Q.add(VE, lambda e: e.memset(dtt[:, 4, :], 0.0))
            z0 = Q.add(VE, lambda e: e.memset(av[:, 4, :], 0.0))
            bi, ps, fr = B.take()
            for j in range(4):
                m = mm3(ps[:, 32 * j:32 * j + 32], [(hkt(k, j), (wdh[:, k, :], wdl[:, k, :])) for k in range(8)],
                        t + fr, start=j == 0, check=False)
            lst = []
            for k in range(8):
                for a_ in mk(k):
                    for w_ in (wdh, wdl):
                        lst.append((a_.bitcast(F32), w_[:, k, :].bitcast(F32)))
            m = mm(ps[0:16, 128:160], lst, start=False, check=False)
            release(i, m)
            v = tt(dtt[:, 0:4, :], ps[:, 0:128].rearrange("p (a b) -> p a b", a=4), rep(cc["dtb2"], 4), A_, [m])
            v = tt(dtt[0:16, 4, :], ps[0:16, 128:160], cc["dtb2"][0:16, :], A_)
            B.done(bi, v)
            vd = v

            def decays():
                act(dtx[:, :, :], dtt[:, :, :], ACT.Abs, [vd])
                act(dtx[:, :, :], dtx[:, :, :], ACT.Exp, scale=-1.0)
                a = act(dtx[:, :, :], dtx[:, :, :], ACT.Ln, bias=1.0)
                a = act(eac[:, 0, :], cc["alog2"], ACT.Exp)
                yield
                stt(dtt[:, :, :], dtt[:, :, :], 0.0, dtx[:, :, :], ALU.max, A_, [a])
                ts(eac[:, 1, :], eac[:, 0, :], -1.0, M)
                tt(av[:, 0:4, :], dtt[:, 0:4, :], rep(eac[:, 1, :], 4), M)
                tt(av[0:16, 4, :], dtt[0:16, 4, :], eac[0:16, 1, :], M)
                ts(al2[:, :, 0:32], av[:, 0:4, :], C["col01"][:, 0:1], M, free=False)
                v = ts(al2[:, :, 32:64], av[:, 0:4, :], C["col01"][:, 1:2], M)
                yield
                bi, ps, fr = B.take()
                avf = av[:, :, :].rearrange("p a b -> p (a b)")
                m = mm(ps[:, 0:160], [(C["cum64"], avf)], [v] + fr, check=False)
                m = mm(ps[:, 160:320], [(C["same64"], avf)], check=False, start=False)
                v = copy(ac[:, :, :].rearrange("p a b -> p (a b)"), ps[:, 0:160], [m])
                v = tt(dtx[:, :, :].rearrange("p a b -> p (a b)"), ps[:, 160:320],
                       ac[:, :, :].rearrange("p a b -> p (a b)"), S_)
                B.done(bi, v)
                act(dtx[:, :, :], dtx[:, :, :], ACT.Exp, [v])
                a = act(eac[:, :, :], ac[:, 0:4, :], ACT.Exp)
                yield
                tt(dtx[:, :, :], dtx[:, :, :], dtt[:, :, :], M, [a])
                t8 = te[:, 0:8, :].rearrange("p (m c) h -> p m c h", c=2)
                ts(t8[:, :, 0, :], dtx[:, 0:4, :], C["col01"][:, 0:1], M)
                ts(t8[:, :, 1, :], dtx[:, 0:4, :], C["col01"][:, 1:2], M)
                v = copy(te[:, 8, :], dtx[:, 4, :])
                yield
                bi, ps, fr = B.take()
                m = mm(ps[:, 0:256], [(C["ones"], al2[:, :, :].rearrange("p a b -> p (a b)"))], fr)
                a = act(eal[:, :, :].rearrange("p a b -> p (a b)"), ps[:, 0:256], ACT.Exp, [m])
                B.done(bi, a)

            raw = Slots([sb(f"raw{j}", [128, 532], F32, a2) for j in range(2)])
            for r in raw.bufs:
                rz = Q.add(VE, lambda e, r=r: e.memset(r[:, 0:3], 0.0))
            cvo = Slots([sb(f"cvo{j}", [128, 528], F32, a2) for j in range(2)])
            sets = [{n_: sb(f"{n_}{j}", shp, F32, a2) for n_, shp in
                     (("xsg", [128, 5, 512]),
                      ("CTm", [128, 2, 512]), ("Bt", [128, 5, 128]), ("cb", [128, 4, 128]),
                      ("yz", [128, 4, 512]))} for j in range(2)]
            BT_ = sb("BTg", [128, 528], F32, a2)
            CT_ = sb("CTg", [128, 528], F32, a2)
            SS = Slots([sb(f"SS{j}", [128, 512], F32, a2) for j in range(2)])
            xd = sb("xd", [128, 512], F32, a2)
            xe = Slots([sb(f"xe{j}", [128, 512], F32, a2) for j in range(2)])
            sg = sb("sgm", [128, 8, 128], F32, a2)
            zt = sb("zt", [128, 512], F32, a2)
            yt = sb("yt", [128, 512], F32, a2)
            yst = Slots([sb(f"yst{j}", [128, 512], F32, a2) for j in range(2)])
            y2 = zt
            ms = sb("ms", [128, 4], F32, a2)

            def b8(ap, n=64):
                return bc(ap, n)

            for t_ in sets:
                cz = Q.add(VE, lambda e, t_=t_: e.memset(t_["CTm"][:, :, :], 0.0))
            done_ = {}

            def project(g):
                xsg, CTm, Bt, cb, zg = (sets[g % 2][n_] for n_ in ("xsg", "CTm", "Bt", "cb", "yz"))

                def conv_out(tile_no, dst):
                    st8 = {}

                    def take(n, ps, m, meta):
                        if meta:
                            ri, r, f = raw.take()
                            st8["r"] = (ri, r)
                            return copy(r[:, 3:19], ps[:, 0:16], [m, rz] + f, eng=SC, free=True)
                        ri, r = st8["r"]
                        a = copy(r[:, 19:531], ps[:, :], [m], eng=SC, free=True)
                        tn = tile_no(n)
                        w = cc["conv2"][:, 5 * tn:5 * tn + 5]
                        o_, dn = dst(n)
                        ts(o_[:, 0:528], r[:, 3:531], w[:, 3:4], M, w[:, 4:5], A_, w=[a] + dn)
                        for d in (1, 2, 3):
                            v = stt(o_[:, 0:528], r[:, 3 - d:531 - d], w[:, 3 - d:4 - d], o_[:, 0:528], M, A_)
                        raw.done(ri, v)
                        act(o_[:, 0:528], o_[:, 0:528], ACT.Silu, [v], free=True)
                        return a
                    return take

                cur = {}
                later = []

                def flush():
                    while later:
                        later.pop(0)()

                def xs_dst(n):
                    ci, c, f = cvo.take()
                    cur["c"] = (ci, c)
                    return c, f

                base = conv_out(lambda n: 4 * g + n, xs_dst)

                def xs_take(n, ps, m, meta):
                    r = base(n, ps, m, meta)
                    if meta:
                        return r
                    flush()
                    ci, c = cur["c"]
                    sil = Q.last(SC)

                    def turn():
                        bi, pt, fr = B.take()
                        for j in range(4):
                            mt_ = tr(pt[:, 128 * j:128 * j + 128], c[:, 16 + 128 * j:144 + 128 * j],
                                     (sil + fr) if j == 0 else ())
                        v = copy(xsg[:, 0:4, 128 * n:128 * n + 128], pt[:, :].rearrange("p (a b) -> p a b", a=4),
                                 [mt_] + gprev)
                        B.done(bi, v)
                        bi, pt, fr = B.take()
                        mt_ = tr(pt[0:16, 0:128], c[:, 0:16], fr)
                        v = copy(xsg[0:16, 4, 128 * n:128 * n + 128], pt[0:16, 0:128], [mt_])
                        B.done(bi, v)
                        cvo.done(ci, mt_)

                    later.append(turn)
                    return r

                gprev = Q.last(PE, VE, GP, SC)
                yield from steps("xs2", 4, 2, 8, hk, xs_take, first=0, s0=2 * g, fine=True)
                bc_base = conv_out(lambda n: (16 if n == 0 else 20) + g, lambda n: (BT_ if n == 0 else CT_, gprev))

                def bc_take(n, ps, m, meta):
                    r = bc_base(n, ps, m, meta)
                    if not meta:
                        flush()
                    return r

                yield from steps("bc2", 2, 2, 8, hk, bc_take, first=0, s0=g, fine=True)
                sil = Q.last(SC)

                def turn_bc():
                    for q_ in range(2):
                        half = lambda ap: ap.rearrange("p (m c t) -> p m c t", m=4, c=2)[:, :, q_, :]
                        vct = copy(half(CTm[:, q_, :]), half(CT_[:, 16:528]), sil + gprev + [cz])
                    bi, ps, fr = B.take()
                    for j in range(4):
                        m = tr(ps[:, 128 * j:128 * j + 128], BT_[:, 16 + 128 * j:144 + 128 * j], (sil + fr) if j == 0 else ())
                    v = copy(Bt[:, 0:4, :], ps[:, :].rearrange("p (a b) -> p a b", a=4), [m])
                    B.done(bi, v)
                    bi, ps, fr = B.take()
                    m = tr(ps[0:16, 0:128], BT_[:, 0:16], fr)
                    v = copy(Bt[0:16, 4, :], ps[0:16, 0:128], [m])
                    B.done(bi, v)
                    bi, ps, fr = B.take()
                    for j in range(4):
                        c = slice(16 + 128 * j, 144 + 128 * j)
                        m = mm(ps[:, 128 * j:128 * j + 128], [(BT_[:, c], CT_[:, c])], fr, start=j == 0, check=False)
                    v = tt(cb[:, :, :], ps[:, :].rearrange("p (a b) -> p a b", a=4), rep(C["same64"], 4), M, [m])
                    B.done(bi, v)
                    done_[g] = vct

                later.append(turn_bc)
                for c in range(2):
                    iz, (h_, l_), tz = slot("z2", 2 * g + c)
                    vh, vl = (x[:, :].rearrange("p (k n) -> p k n", k=8) for x in (h_, l_))
                    for j in range(4):
                        zb, pz, fr = B.take()
                        mm3(pz[:, 0:256], [(hkt(k, j), (vh[:, k, :], vl[:, k, :])) for k in range(4)], tz + fr, stop=False)
                        yield
                        mz = mm3(pz[:, 0:256], [(hkt(k, j), (vh[:, k, :], vl[:, k, :])) for k in range(4, 8)], start=False)
                        B.done(zb, act(zg[:, j, 256 * c:256 * c + 256], pz[:, 0:256], ACT.Silu, [mz] + gprev, free=True))
                        flush()
                        if j == 3:
                            release(iz, mz)
                        yield
                done_[g] = (done_[g], Q.last(SC, VE))

            x3 = lambda ap: ap.rearrange("p (h d) -> p h d", h=8)

            def scan(g):
                hs = slice(8 * g, 8 * g + 8)
                xsg, CTm, Bt, cb, yz = (sets[g % 2][n_] for n_ in ("xsg", "CTm", "Bt", "cb", "yz"))
                zg = yz
                vct, zready = done_[g]
                xi, x_, f = xe.take()
                v = tt(x3(x_[0:16, :]), x3(xsg[0:16, 4, :]), b8(te[0:16, 8, hs]), M, f)
                bi, ps, fr = B.take()
                m = mm(ps[:, :], [(Bt[0:16, 4, :], x_[0:16, :])], [v] + fr)
                xe.done(xi, m)
                s0i, s0, f = SS.take()
                vS = copy(s0[:, :], ps[:, :], [m] + f)
                B.done(bi, vS)
                pys = {}
                vn_ = None

                def intra(j):
                    for q4 in range(2):
                        bi, ps, fr = B.take()
                        for h in range(4):
                            hx = 8 * g + 4 * q4 + h
                            m = mm(ps[:, 128 * h:128 * h + 128],
                                   [(av[:, j, hx:hx + 1].to_broadcast([128, 128]), C["cum64"])], fr,
                                   start=h == 0, check=False)
                        v = tt(sg[:, 4 * q4:4 * q4 + 4, :], ps[:, :].rearrange("p (a b) -> p a b", a=4),
                               bc(ac[:, j, 8 * g + 4 * q4:8 * g + 4 * q4 + 4], 128), S_,
                               [m])
                        B.done(bi, v)
                        yield
                    act(sg[:, :, :], sg[:, :, :], ACT.Abs, [v])
                    a = act(sg[:, :, :], sg[:, :, :], ACT.Exp, scale=-1.0)
                    v = tt(sg[:, :, :], sg[:, :, :], rep(cb[:, j, :], 8), M, [a])
                    v = tt(x3(xd[:, :]), x3(xsg[:, j, :]), b8(dtt[:, j, hs]), M)
                    yield
                    yb, py, fr = B.take()
                    for h in range(8):
                        m = mm(py[:, 64 * h:64 * h + 64], [(sg[:, h, :], xd[:, 64 * h:64 * h + 64])], [v] + fr,
                               start=h == 0, check=False)
                    pys[j] = (yb, py, m)

                def inter(j):
                    nonlocal vS, s0i, s0, vn_
                    yb, py, my = pys.pop(j)
                    ib, pi_, fr2 = B.take()
                    for cpar in range(2):
                        yield
                        c = 2 * j + cpar
                        m = mm(pi_[:, :], [(CTm[:, cpar, 128 * j:128 * j + 128], s0[:, :])], [vS, vct] + fr2,
                               start=cpar == 0, stop=cpar == 1)
                        SS.done(s0i, m)
                        if c < 7:
                            xi, x_, f = xe.take()
                            v = tt(x3(x_[:, :]), x3(xsg[:, j, :]), b8(te[:, c, hs]), M, f)
                            bi, ps, fr = B.take()
                            m2 = mm(ps[:, :], [(Bt[:, j, :], x_[:, :])], [v] + fr)
                            xe.done(xi, m2)
                            s1i, s1, f = SS.take()
                            tt(x3(s1[:, :]), x3(s0[:, :]), b8(eal[:, c, hs]), M, f)
                            vS = tt(s1[:, :], s1[:, :], ps[:, :], A_, [m2])
                            B.done(bi, vS)
                            SS.done(s0i, vS)
                            s0i, s0 = s1i, s1
                    yield
                    v = tt(x3(yt[:, :]), x3(pi_[:, :]), b8(eac[:, j, hs]), M, [m])
                    B.done(ib, v)
                    v = tt(yt[:, :], yt[:, :], py[:, :], A_, [my])
                    B.done(yb, v)
                    tt(x3(y2[:, :]), x3(xsg[:, j, :]), b8(cc["dsk"][:, hs]), M)
                    v = tt(yt[:, :], yt[:, :], y2[:, :], A_)
                    v = tt(yz[:, j, :], yt[:, :], zg[:, j, :], M, zready)
                    yield
                    a = act(zt[:, :], yz[:, j, :], ACT.Square, [v], accum_out=ms[:, 0:1])
                    ts(ms[:, 1:2], ms[:, 0:1], 1 / 512, M, EPS, A_, w=[a])
                    v = recip(ms[:, 2:3], ms[:, 1:2])
                    a = act(ms[:, 3:4], ms[:, 2:3], ACT.Sqrt, [v])
                    v = ts(yz[:, j, :], yz[:, j, :], ms[:, 3:4], M, w=[a])
                    vn_ = v
                    yield

                yield from intra(0)
                for j in range(4):
                    yield from weave((inter(j), 1), *([(intra(j + 1), 1)] if j < 3 else []))
                for n_ in range(4):
                    bi, ps, fr = B.take()
                    for j in range(4):
                        m = tr(ps[:, 128 * j:128 * j + 128], yz[:, j, 128 * n_:128 * n_ + 128],
                               ([vn_] + fr) if j == 0 else ())
                    yi, y_, f = yst.take()
                    a = act(y_[:, :], ps[:, :], ACT.Copy, [m] + f, free=True, scale=cc["ssdn"][:, 4 * g + n_:4 * g + n_ + 1])
                    B.done(bi, a)
                    ydone.append(Q.dma(SY, f"yst{yi}", ys_[:, 4 * g + n_, :], y_[:, :], [a]))
                    yst.done(yi, ydone[-1])
                    yield

            together((project(0), 1), (decays(), 1))
            for g in range(4):
                together((scan(g), 1), *([(project(g + 1), 0.7)] if g < 3 else []))
            Q.barrier()
        yT = sb("yT", [128, 16, 512], F32, ar)
        free1 = Q.last(PE, SC, VE, GP) + ydone
        ky2 = [Q.dma(SY, f"yT{half}", yT[:, 8 * half:8 * half + 8, :], ys_[:, 8 * half:8 * half + 8, :], free1)
               for half in range(2)]
        acc = sb("acc", [128, 8, 512], F32, ar)
        yh = sb("yh", [128, 8, 512], R32, ar)
        yl = sb("yl", [128, 8, 512], R32, ar)
        for half in range(2):
            pe_ = Q.last(PE)
            for k in range(8):
                r = split(yh[:, k, :], yl[:, k, :], yT[:, 8 * half + k, :], pe_ + [ky2[half]], f=True)
            linear("upssd", 8, 2, 8, lambda k: (yh[:, k, :], yl[:, k, :]),
                   (lambda n, ps, m: copy(acc[:, n, :], ps[:, :], [m])) if half == 0 else
                   (lambda n, ps, m: tt(acc[:, n, :], acc[:, n, :], ps[:, :], A_, [m])), [r], s0=4 * half)
        asp = Q.dma(SY, "asp", xa_, acc[:, :, :], Q.last(VE))
        Q.barrier([asp])
    with ExitStack() as ar:
        acc, ka = load("acc2", ar, xa_, Q.last(PE, SC, VE, GP) + [asp])
        ya, ky = load("ya2", ar, yd_, Q.last(PE, SC, VE, GP) + [ysp])
        xT, kx = load("x2", ar, xd_, Q.last(PE, SC, VE, GP) + [xsp])
        gsl = Slots([sb(f"gs{j}", [128, 512], F32, ar) for j in range(2)])
        mh = sb("mh", [128, 8, 512], R32, ar)
        ml = sb("ml", [128, 8, 512], R32, ar)

        def take_b(n, ps, m):
            gi, g_, f = gsl.take()
            a = act(g_[:, :], ps[:, :], ACT.Sigmoid, [m] + f, free=True)
            v = tt(g_[:, :], g_[:, :], acc[:, n, :], M, [a, ka])
            v = tt(g_[:, :], g_[:, :], ya[:, n, :], A_, [ky])
            gsl.done(gi, split(mh[:, n, :], ml[:, n, :], g_[:, :], [v], f=True))
            return a

        linear("gateb", 8, 2, 8, hk, take_b)
        Q.hold[VE] += [kx]
        linear("wout2", 8, 2, 8, lambda k: (mh[:, k, :], ml[:, k, :]),
               lambda n, ps, m: tt(xT[:, n, :], xT[:, n, :], ps[:, :], A_, [m], free=True), Q.last(VE))
        if dump("x3", xT[:, :, :]):
            return endit()
        hready = norm_to(xT, cc["lnffn"], ar, w=Q.last(VE))
        xsp = Q.dma(SY, "xsp", xd_, xT[:, :, :], Q.last(VE))

    sd_ = nc.dram_tensor("score_spill", (4, 128, 2048), F32).ap()
    gd_ = nc.dram_tensor("gelu_spill", (64, 128, 2, 512), F32).ap()
    wd_ = nc.dram_tensor("weight_spill", (64, 128, 2, 512), F32).ap()
    with ExitStack() as ar:
        qT = sb("pqT", [128, 16, 512], F32, ar)
        ssg = Slots([sb(f"ssg{j}", [128, 2048], F32, ar) for j in range(2)])
        linear("wq", 16, 2, 8, hk, lambda n, ps, m: copy(qT[:, n, :], ps[:, :], [m], free=True), hready)
        i, buf, t = slot("subk", 0)
        sk = buf[:, 0:2048].rearrange("p (a n) -> p a n", a=16)
        for j in range(4):
            gi, g_, f = ssg.take()
            for q4 in range(4):
                bi, ps, fr = B.take()
                for a_ in range(4):
                    n_ = 4 * q4 + a_
                    m = mm(ps[:, 128 * a_:128 * a_ + 128], [(qT[:, n_, 128 * j:128 * j + 128], sk[:, n_, :])],
                           t + Q.last(VE) + fr, start=a_ == 0, check=False)
                c_ = copy(g_[:, 512 * q4:512 * q4 + 512], ps[:, :], [m, xsp] + f, eng=SC, free=True)
                B.done(bi, c_)
            ssp = Q.dma(SY, f"ssp{j}", sd_[j], g_[:, :], [c_])
            ssg.done(gi, ssp)
            if j == 0:
                sdone = []
            sdone.append(ssp)
        release(i, m)
        Q.barrier(sdone)

    with ExitStack() as ar:
        s_ = sb("s_", [128, 16, 128], F32, ar)
        sr = sb("sr", [128, 256], F32, ar)
        top = sb("top", [128, 16, 16], F32, ar)
        tix = sb("tix", [128, 16, 16], U32, ar)
        tif = top
        cand = sb("cand", [128, 8, 256], F32, ar)
        best = sb("best", [128, 8, 16], F32, ar)
        pix = sb("pix", [128, 8, 16], U32, ar)
        pa = sb("pa", [128, 8, 16], U32, ar)
        paf = sb("paf", [128, 2, 128], F32, ar)
        eq = s_[:, :, :].rearrange("p (h x) k -> p h (x k)", h=8)
        sel = sb("sel", [128, 3, 128], F32, ar)
        ijw = sb("ijw", [128, 3, 128], F32, ar)
        red8 = sb("red8", [128, 2, 8], F32, ar)
        AB = Slots([sb(f"AB{j}", [128, 2, 2, 128], F32, ar) for j in range(2)])
        gst = Slots([sb(f"gst{j}", [128, 512], F32, ar) for j in range(2)])
        stage = sb("stage", [128, 128, 128], F32, ar)

        def top16(vals, idx, src, scratch, w=()):
            Q.add(VE, lambda e: e.max(vals[:, 0:8], src), w)
            Q.add(VE, lambda e: e.max_index(idx[:, 0:8], vals[:, 0:8], src))
            Q.add(VE, lambda e: e.match_replace(scratch, vals[:, 0:8], src, -3e38))
            Q.add(VE, lambda e: e.max(vals[:, 8:16], scratch))
            Q.add(VE, lambda e: e.max_index(idx[:, 8:16], vals[:, 8:16], scratch))

        def choose():
            wout, sfree, outs = None, Q.last(VE), []
            for j in range(4):
                ls = Q.dma(SY, "sload", s_[:, :, :], sd_[j].rearrange("p (a b) -> p a b", a=16), sfree)
                for n_ in range(16):
                    top16(top[:, n_, :], tix[:, n_, :], s_[:, n_, :], sr[:, 0:128], [ls])
                    if n_ % 2:
                        if outs:
                            wout = outs.pop(0)()
                        yield
                for h in range(8):
                    tt(cand[:, h, :].rearrange("p (a b) -> p a b", a=16), bc(top[:, 2 * h, :], 16),
                       rep(top[:, 2 * h + 1, :], 16), A_, free=h > 0)
                copy(tif[:, :, :], tix[:, :, :])
                yield
                for h in range(8):
                    top16(best[:, h, :], pix[:, h, :], cand[:, h, :], sr[:, :])
                    yield
                ts(pa[:, :, :], pix[:, :, :], 4, ALU.logical_shift_right)
                copy(paf[:, 0, :], pa[:, :, :].rearrange("p a b -> p (a b)"))
                ts(pa[:, :, :], pix[:, :, :], 15, ALU.bitwise_and)
                copy(paf[:, 1, :], pa[:, :, :].rearrange("p a b -> p (a b)"))
                yield
                for c in range(2):
                    for h in range(8):
                        e3 = eq[:, h, :].rearrange("p (k a) -> p k a", k=16)
                        tt(e3, bc(paf[:, c, 16 * h:16 * h + 16], 16), rep(C["iota"][:, 0:16], 16), ALU.is_equal,
                           free=h > 0)
                    yield
                    for h in range(8):
                        e3 = eq[:, h, :].rearrange("p (k a) -> p k a", k=16)
                        tt(e3, e3, rep(tif[:, 2 * h + c, :], 16), M, free=h > 0)
                    yield
                    sfree = [red(sel[:, c, :], eq[:, :, :].rearrange("p h (k a) -> p (h k) a", a=16), A_,
                        w=Q.last(PE) if c == 0 else ())]
                    yield
                w3 = sel[:, 2, :].rearrange("p (h k) -> p h k", h=8)
                v = tt(w3, best[:, :, :], best[:, :, 0:1].to_broadcast([128, 8, 16]), S_)
                a = act(w3, w3, ACT.Exp, [v])
                red(red8[:, 0, :], w3, A_, w=[a])
                recip(red8[:, 1, :], red8[:, 0, :])
                v = tt(w3, w3, bc(red8[:, 1, :], 16), M)
                yield
                yield
                bi, ps, fr = B.take()
                for c in range(3):
                    m = tr(ps[:, 128 * c:128 * c + 128], sel[:, c, :], ([v] + fr) if c == 0 else ())
                v = copy(ijw[:, :, :], ps[:, 0:384].rearrange("p (a b) -> p a b", a=3), [m])
                B.done(bi, v)
                late = None
                for t0 in range(0, 128, 4):
                    new = []
                    for x in range(2):
                        ai, ab, f = AB.take()
                        for y in range(2):
                            tok = t0 + 2 * x + y
                            ts(ab[:, y, 0, :], C["iota"], ijw[:, 0, tok:tok + 1], ALU.is_equal,
                               ijw[:, 2, tok:tok + 1], M, w=[v] + f, free=True)
                            vb_ = ts(ab[:, y, 1, :], C["iota"], ijw[:, 1, tok:tok + 1], ALU.is_equal, free=True)
                        new.append((ai, ab, vb_))
                        if x == 0:
                            bi, ps, fr = B.take()
                        for y in range(2):
                            q_ = 2 * x + y
                            m = mm(ps[:, 128 * q_:128 * q_ + 128], [(ab[:, y, 0, :], ab[:, y, 1, :])], [vb_] + fr,
                                   start=q_ == 0, check=False)
                        AB.done(ai, m)
                    a = act(stage[:, :, t0:t0 + 4].rearrange("p j t -> p t j"),
                            ps[:, :].rearrange("p (t j) -> p t j", t=4), ACT.Copy,
                            [m] + ([wout] if wout else []), free=True)
                    B.done(bi, a)
                    yield
                for q4 in range(4):
                    for x in range(2):
                        outs.append(lambda q4=q4, x=x, j=j, a=a: Q.dma(
                            SY, "wst", wd_[16 * q4:16 * q4 + 16, :, x, 128 * j:128 * j + 128].rearrange(
                                "jp i t -> i jp t"), stage[:, 32 * q4 + x:32 * q4 + 32:2, :], [a]))
            wlast.extend([o() for o in outs])

        wlast, glast = [], []
        side = choose()
        for s in range(64):
            i, (h_, l_), t = slot("u", s)
            vh, vl = (x[:, :].rearrange("p (x k n) -> p x k n", x=2, k=8) for x in (h_, l_))
            for x in range(2):
                bi, ps, fr = B.take()
                mm3(ps[:, :], [((vh[:, x, k, :], vl[:, x, k, :]), hk(k)) for k in range(4)], t + fr, stop=False)
                next(side, None)
                m = mm3(ps[:, :], [((vh[:, x, k, :], vl[:, x, k, :]), hk(k)) for k in range(4, 8)], start=False)
                if x == 1:
                    release(i, m)
                gi, g_, f = gst.take()
                a = act(g_[:, :], ps[:, :], ACT.Gelu_apprx_tanh, [m] + f, free=True)
                B.done(bi, a)
                gt_ = Q.dma(SY, f"gst{gi}", gd_[s][:, x, :], g_[:, :], [a])
                gst.done(gi, gt_)
                if 2 * s + x >= 126:
                    glast.append(gt_)
                next(side, None)
        for _ in side:
            pass
        Q.barrier()

    with ExitStack() as ar:
        def vbufs(j):
            return sb(f"gv{j}", [128, 2, 512], F32, ar), sb(f"wv{j}", [128, 2, 512], F32, ar)

        gws = [vbufs(0), vbufs(1)]
        Pm = Slots([(sb(f"ph{j}", [128, 2, 512], R32, ar), sb(f"pl{j}", [128, 2, 512], R32, ar)) for j in range(2)])
        gw = Slots(gws + [vbufs(2)])
        sums = []
        for d in range(8):
            sums.append(B.take())
        started = Q.last(PE, SC, VE, GP) + glast
        gq = []

        def fetch(s):
            wi, (g_, w_), f = gw.take()
            ready_ = wlast if s == 2 else wlast[0:2 * (s // 16 + 1)]
            ta = Q.dma(SY, f"gv{wi}", g_[:, :, :], gd_[s], (f or started) + ready_)
            ta = Q.dma(SY, f"gv{wi}", w_[:, :, :], wd_[s])
            gq.append((wi, g_, w_, ta))

        def multiply():
            wi, g_, w_, ta = gq.pop(0)
            pi, (ph, pl), f = Pm.take()
            v = tt(g_[:, :, :], g_[:, :, :], w_[:, :, :], M, [ta] + f, free=True)
            a = act(ph[:, :, :], g_[:, :, :], ACT.Copy, [v], free=True)
            v = tt(pl[:, :, :], g_[:, :, :], ph[:, :, :].bitcast(F32), S_, [a], free=True)
            gw.done(wi, v)
            return pi, ph, pl, v

        for s in range(3):
            fetch(s)
        xT, kx = load("x3", ar, xd_, started + wlast + [xsp])
        nxt = multiply()
        for s in range(64):
            pi, ph, pl, pv = nxt
            i, (h_, l_), t = slot("v", s)
            if s < 63:
                nxt = multiply()
            if s + 3 < 64:
                fetch(s + 3)
            for d in range(8):
                bi, ps, fr = sums[d]
                m = mm3(ps[:, :], [((h_[:, 1024 * x + 128 * d:1024 * x + 128 * d + 128],
                                     l_[:, 1024 * x + 128 * d:1024 * x + 128 * d + 128]),
                                    (ph[:, x, :], pl[:, x, :])) for x in range(2)],
                        t + [pv] + (fr if s == 0 else []), start=s == 0, stop=s == 63)
            release(i, m)
            Pm.done(pi, m)
        for d in range(8):
            bi, ps, _ = sums[d]
            B.done(bi, tt(xT[:, d, :], xT[:, d, :], ps[:, :], A_, [m, kx], free=True))
        Q.barrier()
        fin = sb("fin", [128, 8, 512], F32, ar)
        norm_to(xT, cc["lnfin"], ar, out=fin)
        Q.dma(SY, "out", D["out"], fin[:, :, :], Q.last(VE))
        Q.q[SY].append((None, [("out", 16)], None))
    finish()




def _layout(I):
    import numpy as np
    f = {k: np.asarray(v) for k, v in I.items()}
    g = {k: (v[0] if v.shape[0] == 1 else v) for k, v in f.items()}

    def fm(W, per):
        K, N = W.shape
        a = W.reshape(K // 128, 128, N // 128 // per, per, 128)
        return np.ascontiguousarray(a.transpose(2, 1, 3, 0, 4)).reshape(N // 128 // per, 128, -1)

    def tmj(W, n):
        K, N = W.shape
        a = W.reshape(K // 128, 128, N // n, n)
        return np.ascontiguousarray(a.transpose(2, 1, 0, 3)).reshape(N // n, 128, -1)

    def col(v):
        return np.ascontiguousarray(v.reshape(-1, 128).T)

    def row(v):
        return np.ascontiguousarray(np.broadcast_to(v.reshape(1, -1), (128, v.size)))

    o = {}
    w = g["w_in"]
    o["ada"] = tmj(g["ada_w"], 256)
    o["win1"] = fm(np.concatenate([w[:, 0:2048], w[:, 2056:2568], w[:, 2568:2696], w[:, 2696:2824],
                                   w[:, 2824:2952], w[:, 3080:3208]], axis=1), 2)
    o["win1t"] = tmj(np.concatenate([w[:, 2952:3080], w[:, 3208:3336]], axis=1), 256)
    o["win1g"] = tmj(np.concatenate([w[:, 2048:2056], w[:, 3336:3348]], axis=1), 20)
    o["cmpw1"] = np.stack([g[n].reshape(32, 128, 128).transpose(1, 0, 2).reshape(128, 4096)
                           for n in ("cmp_k_w1", "cmp_v_w1")])
    o["cmpw1"] = o["cmpw1"].reshape(2, 128, 2, 2048).transpose(0, 2, 1, 3).reshape(4, 128, 2048)
    o["cmpw2"] = np.concatenate([g["cmp_k_w2"], g["cmp_v_w2"]], axis=1)[None]
    o["wout1"] = fm(g["w_out"], 2)
    up = g["ffn_w_up"].reshape(1024, 2, 22, 128).transpose(0, 2, 1, 3).reshape(1024, 5632)
    o["wup"] = fm(up, 2)
    o["wdn"] = fm(g["ffn_w_down"], 1).reshape(8, 128, 2, 1408).transpose(2, 0, 1, 3).reshape(16, 128, 1408)
    w = g["w_in_2"]
    o["qk2"] = fm(w[:, 0:1024], 2)
    o["v2"] = tmj(w[:, 1024:2048], 256)
    o["gout2"] = fm(w[:, 2048:3072], 2)
    o["glow"] = fm(np.concatenate([w[:, 3072:3088]] * 8, axis=1), 1)
    z, xbc = w[:, 3088:5136], w[:, 5136:8208]
    o["z2"] = tmj(z, 256)
    o["xs2"] = fm(xbc[:, 0:2048], 2)
    bcw = np.stack([xbc[:, 2048:2560].reshape(1024, 4, 128), xbc[:, 2560:3072].reshape(1024, 4, 128)], axis=2)
    o["bc2"] = fm(bcw.reshape(1024, 1024), 2)
    o["dt2"] = tmj(w[:, 8208:8240], 32)
    o["gatea"] = fm(w[:, 8240:9264], 2)
    o["gateb"] = fm(w[:, 9264:10288], 2)
    o["upgla"] = fm(g["w_up_gla_2"], 2)
    o["upssd"] = np.concatenate([fm(g["w_up_ssd_2"][0:1024], 2), fm(g["w_up_ssd_2"][1024:2048], 2)])
    o["wout2"] = fm(g["w_out_2"], 2)
    o["wq"] = fm(g["peer_w_q_2"], 2)
    o["subk"] = np.ascontiguousarray(g["peer_sub_keys_2"].reshape(16, 128, 128).transpose(2, 0, 1)).reshape(1, 128, 2048)
    u = g["peer_u_2"].reshape(128, 128, 8, 128).transpose(1, 3, 2, 0)
    v = g["peer_v_2"].reshape(128, 128, 1024).transpose(1, 0, 2)
    for n, a in (("u", u), ("v", v)):
        a = a.reshape(64, 2, 128, 1024).transpose(0, 2, 1, 3)
        o[n] = np.ascontiguousarray(a).reshape(64, 128, 2048)
    o["gate2w"] = g["gla_w_gate2_2"]
    o["xT"] = np.ascontiguousarray(g["x"].reshape(512, 8, 128).transpose(2, 1, 0))
    o["metaT"] = np.ascontiguousarray(f["meta_tokens_2"].reshape(16, 8, 128).transpose(2, 1, 0))
    parts = [("c", col(g["c"])), ("adab", col(g["ada_b"])), ("norm1", col(g["norm1_w"])),
             ("norm2", col(g["norm2_w"])),
             ("conv1", g["gdn_conv_w"].reshape(4, 12, 128).transpose(2, 1, 0).reshape(128, 48)),
             ("qn", col(g["nsa_q_norm_w"])), ("kslc", col(g["nsa_k_norm_slc"])),
             ("kwin", col(g["nsa_k_norm_win"])), ("kcmpn", col(g["nsa_k_norm_cmp"])),
             ("kpos", g["cmp_k_pos"].T), ("vpos", g["cmp_v_pos"].T),
             ("alog", row(g["gdn_A_log"])), ("dtb1", row(g["gdn_dt_bias"])), ("gdnn", col(g["gdn_out_norm_w"])),
             ("fconv", np.concatenate([g["ffn_conv_w"], g["ffn_conv_b"][None]], 0).reshape(4, 2, 22, 128)
              .transpose(3, 2, 1, 0).reshape(128, 176)),
             ("lnmix", col(g["ln_mix_w_2"])), ("lnffn", col(g["ln_ffn_w_2"])), ("lnfin", col(f["ln_final_w_2"])),
             ("bgate", col(g["gla_b_gate_2"])), ("glan", col(g["gla_norm_w_2"])), ("ssdn", col(g["ssd_norm_w_2"])),
             ("dtb2", row(g["ssd_dt_bias_2"])), ("alog2", row(g["ssd_a_log_2"])), ("dsk", row(g["ssd_d_2"])),
             ("conv2", np.concatenate([g["ssd_conv_w_2"], g["ssd_conv_b_2"][None]], 0).reshape(5, 24, 128)
              .transpose(2, 1, 0).reshape(128, 120))]
    COLS.clear()
    off = 0
    for name, a in parts:
        COLS[name] = (off, a.shape[1])
        off += a.shape[1]
    o["cols"] = np.ascontiguousarray(np.concatenate([a for _, a in parts], axis=1))
    o["consts"] = const_array()
    o["masks"] = mask_array()
    return {k: np.ascontiguousarray(v) for k, v in o.items()}


COLS = {}


def kernel(**inputs):
    import numpy as _np
    import concourse.bacc as _bacc
    from concourse import mybir as _mybir
    from concourse.bass_utils import run_bass_kernel_spmd as _run

    arrays = _layout(inputs)
    nc = _bacc.Bacc("TRN2", target_bir_lowering=False, num_devices=1)
    D = {}
    for name, a in arrays.items():
        D[name] = nc.dram_tensor("in_" + name, a.shape, _mybir.dt.from_np(a.dtype), kind="ExternalInput").ap()
    D["out"] = nc.dram_tensor("out_0", (128, 8, 512), _mybir.dt.float32, kind="ExternalOutput").ap()
    if DBG is not None:
        D["dbg"] = nc.dram_tensor("dbg", (128, 8192), _mybir.dt.float32, kind="ExternalOutput").ap()
    build(nc, D, None)
    r = _run(nc, [{"in_" + k: v for k, v in arrays.items()}], core_ids=[0])
    got = r.results[0]["out_0"]
    return _np.ascontiguousarray(got.transpose(2, 1, 0)).reshape(1, 512, 1024)
```
